# Optimizing a Trainium2 kernel written in Bass

```python
import math
import jax, jax.numpy as jnp
from jax import lax
import numpy as np

D_MODEL = 1024
BATCH = 1
SEQ = 512
DEPTH = 1
DEC_BATCH = 8
DEC_SEQ = 4
PAST_LEN = 4096
PAGE_SIZE = 128

N_BRANCH = 4
BRANCH_W = D_MODEL // N_BRANCH
GDN_H = 4
GDN_DK = 64
GDN_DV = BRANCH_W // GDN_H
HG_H = 4
HG_DK = 64
HG_DV = BRANCH_W // HG_H
SSD_H = 8
SSD_P = BRANCH_W // SSD_H
SSD_N = 64
SSD_G = 2
ML_H = 4
ML_DK = 64
ML_DV = BRANCH_W // ML_H
CONV_K = 4
CHUNK = 64
D_FF = -(-8 * D_MODEL // (3 * 256)) * 256
EPS = 1e-6
NEG = -1e30
GDN_CONV_W = 2 * GDN_H * GDN_DK + GDN_H * GDN_DV
SSD_CONV_W = SSD_H * SSD_P + 2 * SSD_G * SSD_N
IN_SPLITS = (GDN_CONV_W, GDN_H * GDN_DV, GDN_H, GDN_H,
             HG_H * HG_DK, HG_H * HG_DK, HG_H * HG_DV, HG_H * HG_DV,
             SSD_H * SSD_P, SSD_CONV_W, SSD_H,
             ML_H * ML_DK, ML_H * ML_DK, ML_H * ML_DV, ML_H * ML_DV, ML_H, ML_H,
             N_BRANCH * D_MODEL)

kernel_name = 'hybrid_gdn_hgrn2_ssd_mlstm_step'

def _rms(x, w):
    xf = x.astype(jnp.float32)
    return xf * lax.rsqrt(jnp.mean(xf * xf, axis=-1, keepdims=True) + EPS) * w.astype(jnp.float32)

def _l2n(x):
    return x * lax.rsqrt(jnp.sum(x * x, axis=-1, keepdims=True) + EPS)

def _masked_exp(d, mask):
    return jnp.where(mask, jnp.exp(jnp.where(mask, d, 0.0)), 0.0)

def _chunk_len(T):
    return CHUNK if T % CHUNK == 0 else T

def _chunk_heads(a, L):
    B, T, H = a.shape[:3]
    a = a.reshape((B, T // L, L, H) + a.shape[3:])
    return jnp.moveaxis(jnp.moveaxis(a, 1, 0), 3, 2)

def _unchunk_heads(o):
    o = jnp.moveaxis(jnp.moveaxis(o, 2, 3), 0, 1)
    return o.reshape((o.shape[0], -1) + o.shape[3:])

def _causal_conv(u, buf, w, b):
    T = u.shape[1]
    up = jnp.concatenate([buf.astype(u.dtype), u], axis=1)
    y = b
    for i in range(CONV_K):
        y = y + up[:, i:i + T] * w[i]
    return jax.nn.silu(y), up[:, T:]

def _gated_delta(q, k, v, beta, logd, S0):
    L = _chunk_len(q.shape[1])
    incl = jnp.tril(jnp.ones((L, L), bool))
    strict = jnp.tril(jnp.ones((L, L), bool), -1)
    eye = jnp.eye(L, dtype=jnp.float32)
    dv = v.shape[-1]
    xs = tuple(_chunk_heads(a, L) for a in (q, k, v, beta, logd))

    def step(S, inp):
        qc, kc, vc, bc, lc = inp
        g = jnp.cumsum(lc, axis=-1)
        dec = _masked_exp(g[..., :, None] - g[..., None, :], incl)
        kk = jnp.einsum('bhld,bhmd->bhlm', kc, kc)
        lhs = eye + jnp.where(strict, kk * dec * bc[..., :, None], 0.0)
        rhs = jnp.concatenate([vc * bc[..., None], kc * (bc * jnp.exp(g))[..., None]], axis=-1)
        sol = lax.linalg.triangular_solve(lhs, rhs, left_side=True, lower=True, unit_diagonal=True)
        u = sol[..., :dv] - jnp.einsum('bhlk,bhkv->bhlv', sol[..., dv:], S)
        qk = jnp.einsum('bhld,bhmd->bhlm', qc, kc) * dec
        o = (jnp.einsum('bhlk,bhkv->bhlv', qc * jnp.exp(g)[..., None], S)
             + jnp.einsum('bhlm,bhmv->bhlv', qk, u))
        gl = g[..., -1:]
        S = S * jnp.exp(gl)[..., None] + jnp.einsum('bhlk,bhlv->bhkv', kc * jnp.exp(gl - g)[..., None], u)
        return S, o

    S, o = lax.scan(step, S0, xs)
    return _unchunk_heads(o), S

def _hgrn2(q, k, v, logf, S0):
    L = _chunk_len(q.shape[1])
    incl = jnp.tril(jnp.ones((L, L), bool))[..., None]
    xs = tuple(_chunk_heads(a, L) for a in (q, k, v, logf))

    def step(S, inp):
        qc, kc, vc, fc = inp
        g = jnp.cumsum(fc, axis=2)
        dec = _masked_exp(g[:, :, :, None, :] - g[:, :, None, :, :], incl)
        a = jnp.einsum('bhlc,bhmc,bhlmc->bhlm', qc, kc, dec)
        o = (jnp.einsum('bhlc,bhcv->bhlv', qc * jnp.exp(g), S)
             + jnp.einsum('bhlm,bhmv->bhlv', a, vc))
        gl = g[:, :, -1:, :]
        S = S * jnp.exp(gl[:, :, 0, :, None]) + jnp.einsum('bhlc,bhlv->bhcv', kc * jnp.exp(gl - g), vc)
        return S, o

    S, o = lax.scan(step, S0, xs)
    return _unchunk_heads(o), S

def _ssd_scan(c, b, v, da, S0):
    L = _chunk_len(c.shape[1])
    incl = jnp.tril(jnp.ones((L, L), bool))
    xs = tuple(_chunk_heads(a, L) for a in (c, b, v, da))

    def step(S, inp):
        cc, bc, vc, dc = inp
        g = jnp.cumsum(dc, axis=-1)
        dec = _masked_exp(g[..., :, None] - g[..., None, :], incl)
        a = jnp.einsum('bhln,bhmn->bhlm', cc, bc) * dec
        o = (jnp.einsum('bhln,bhnp->bhlp', cc * jnp.exp(g)[..., None], S)
             + jnp.einsum('bhlm,bhmp->bhlp', a, vc))
        gl = g[..., -1:]
        S = S * jnp.exp(gl)[..., None] + jnp.einsum('bhln,bhlp->bhnp', bc * jnp.exp(gl - g)[..., None], vc)
        return S, o

    S, o = lax.scan(step, S0, xs)
    return _unchunk_heads(o), S

def _mlstm(q, k, v, ig, lf, C0, n0, m0):
    L = _chunk_len(q.shape[1])
    incl = jnp.tril(jnp.ones((L, L), bool))
    xs = tuple(_chunk_heads(a, L) for a in (q, k, v, ig, lf))

    def step(carry, inp):
        C, n, m = carry
        qc, kc, vc, ic, fc = inp
        b = jnp.cumsum(fc, axis=-1)
        logw = jnp.where(incl, b[..., :, None] - b[..., None, :] + ic[..., None, :], NEG)
        log0 = b + m[..., None]
        mt = jnp.maximum(log0, jnp.max(logw, axis=-1))
        w = jnp.where(incl, jnp.exp(logw - mt[..., None]), 0.0)
        w0 = jnp.exp(log0 - mt)
        qk = jnp.einsum('bhld,bhmd->bhlm', qc, kc) * w
        num = w0[..., None] * jnp.einsum('bhld,bhdv->bhlv', qc, C) + jnp.einsum('bhlm,bhmv->bhlv', qk, vc)
        den = w0 * jnp.einsum('bhld,bhd->bhl', qc, n) + jnp.sum(qk, axis=-1)
        h = num / jnp.maximum(jnp.abs(den), jnp.exp(-mt))[..., None]
        mL = mt[..., -1]
        wL0 = jnp.exp(b[..., -1] + m - mL)
        wL = jnp.exp(b[..., -1:] - b + ic - mL[..., None])
        C = wL0[..., None, None] * C + jnp.einsum('bhl,bhld,bhlv->bhdv', wL, kc, vc)
        n = wL0[..., None] * n + jnp.einsum('bhl,bhld->bhd', wL, kc)
        return (C, n, mL), h

    (C, n, m), h = lax.scan(step, (C0, n0, m0), xs)
    return _unchunk_heads(h), C, n, m

def _mixer(h, st, p):
    Bsz, T, _ = h.shape
    proj = (h @ p['w_in']).astype(jnp.float32)
    (g_qkv, g_z, g_b, g_a, h_q, h_f, h_i, h_g, s_z, s_xbc, s_dt,
     m_q, m_k, m_v, m_o, m_i, m_f, gate) = jnp.split(proj, np.cumsum(IN_SPLITS)[:-1].tolist(), axis=-1)
    S_gdn, buf_gdn, S_hg, S_ssd, buf_ssd, C_ml, n_ml, m_ml = st

    qkv, buf_gdn = _causal_conv(g_qkv, buf_gdn, p['gdn_conv_w'], p['gdn_conv_b'])
    q, k, v = jnp.split(qkv, [GDN_H * GDN_DK, 2 * GDN_H * GDN_DK], axis=-1)
    q = _l2n(q.reshape(Bsz, T, GDN_H, GDN_DK)) * GDN_DK ** -0.5
    k = _l2n(k.reshape(Bsz, T, GDN_H, GDN_DK))
    v = v.reshape(Bsz, T, GDN_H, GDN_DV)
    beta = jax.nn.sigmoid(g_b)
    logd = -jnp.exp(p['gdn_a_log']) * jax.nn.softplus(g_a + p['gdn_dt_bias'])
    o, S_gdn = _gated_delta(q, k, v, beta, logd, S_gdn)
    out_a = (_rms(o, p['gdn_norm_w']) * jax.nn.silu(g_z.reshape(Bsz, T, GDN_H, GDN_DV))).reshape(Bsz, T, -1)

    lb = p['hg_lb'].reshape(HG_H, HG_DK)
    fz = h_f.reshape(Bsz, T, HG_H, HG_DK)
    lb_pos = lb > 0
    log_lb = jnp.log(jnp.where(lb_pos, lb, 1.0))
    ls = jax.nn.log_sigmoid(fz)
    logf = jnp.where(lb_pos, jnp.logaddexp(log_lb, jnp.log1p(-lb) + ls), ls)
    kg = (1.0 - lb) * jax.nn.sigmoid(-fz)
    o, S_hg = _hgrn2(jax.nn.silu(h_q.reshape(Bsz, T, HG_H, HG_DK)), kg,
                     h_i.reshape(Bsz, T, HG_H, HG_DV), logf, S_hg)
    out_b = (_rms(o, p['hg_norm_w']) * jax.nn.silu(h_g.reshape(Bsz, T, HG_H, HG_DV))).reshape(Bsz, T, -1)

    xbc, buf_ssd = _causal_conv(s_xbc, buf_ssd, p['ssd_conv_w'], p['ssd_conv_b'])
    xs_, Bs, Cs = jnp.split(xbc, [SSD_H * SSD_P, SSD_H * SSD_P + SSD_G * SSD_N], axis=-1)
    dt = jax.nn.softplus(s_dt + p['ssd_dt_bias'])
    xh = xs_.reshape(Bsz, T, SSD_H, SSD_P)
    Bh = jnp.repeat(Bs.reshape(Bsz, T, SSD_G, SSD_N), SSD_H // SSD_G, axis=2)
    Ch = jnp.repeat(Cs.reshape(Bsz, T, SSD_G, SSD_N), SSD_H // SSD_G, axis=2)
    y, S_ssd = _ssd_scan(Ch, Bh, xh * dt[..., None], dt * -jnp.exp(p['ssd_a_log']), S_ssd)
    y = (y + p['ssd_d'][:, None] * xh).reshape(Bsz, T, -1) * jax.nn.silu(s_z)
    out_c = _rms(y.reshape(Bsz, T, SSD_G, -1), p['ssd_norm_w'].reshape(SSD_G, -1)).reshape(Bsz, T, -1)

    qm = m_q.reshape(Bsz, T, ML_H, ML_DK) * ML_DK ** -0.5
    km = m_k.reshape(Bsz, T, ML_H, ML_DK)
    vm = m_v.reshape(Bsz, T, ML_H, ML_DV)
    ig = m_i + p['ml_b_i']
    lf = jax.nn.log_sigmoid(m_f + p['ml_b_f'])
    hh, C_ml, n_ml, m_ml = _mlstm(qm, km, vm, ig, lf, C_ml, n_ml, m_ml)
    out_d = (_rms(hh, p['ml_norm_w']) * jax.nn.sigmoid(m_o.reshape(Bsz, T, ML_H, ML_DV))).reshape(Bsz, T, -1)

    branches = jnp.stack([out_a, out_b, out_c, out_d], axis=2)
    up = jnp.einsum('btnw,nwd->btnd', branches, p['w_branch'].astype(jnp.float32))
    gates = jax.nn.sigmoid(gate.reshape(Bsz, T, N_BRANCH, D_MODEL))
    merged = jnp.einsum('btnd,btnd->btd', gates, up)
    y = merged.astype(h.dtype) @ p['w_out']
    return y, (S_gdn, buf_gdn, S_hg, S_ssd, buf_ssd, C_ml, n_ml, m_ml)

def _swiglu(h, w_in, w_out):
    a, b = jnp.split(h @ w_in, 2, axis=-1)
    return (jax.nn.silu(a) * b) @ w_out

def _trunk(x, c, states, P, final_norm_w):
    new = [[] for _ in states]
    cs = jax.nn.silu(c)
    for l in range(DEPTH):
        p = {name: arr[l] for name, arr in P.items()}
        mod = cs @ p['ada_w'] + p['ada_b']
        sh1, sc1, gt1, sh2, sc2, gt2 = (m[:, None, :] for m in jnp.split(mod, 6, axis=-1))
        hmix = (_rms(x, p['norm1_w']) * (1 + sc1) + sh1).astype(x.dtype)
        y, st = _mixer(hmix, tuple(s[l].astype(jnp.float32) for s in states), p)
        x = x + gt1 * y
        hffn = (_rms(x, p['norm2_w']) * (1 + sc2) + sh2).astype(x.dtype)
        x = x + gt2 * _swiglu(hffn, p['ffn_w_in'], p['ffn_w_out'])
        for lst, s in zip(new, st):
            lst.append(s)
    return _rms(x, final_norm_w).astype(x.dtype), tuple(jnp.stack(s) for s in new)

def setup_inputs(seed: int = 0) -> dict:
    key = jax.random.key(seed)
    keys = iter(jax.random.split(key, 64))

    def nrm(shape, scale):
        return scale * jax.random.normal(next(keys), shape, jnp.float32)

    def dt_bias(shape):
        dt = jnp.exp(jax.random.uniform(next(keys), shape, jnp.float32, math.log(1e-3), math.log(1e-1)))
        return dt + jnp.log(-jnp.expm1(-dt))

    def a_log(shape):
        return jnp.log(jax.random.uniform(next(keys), shape, jnp.float32, 1.0, 16.0))

    n_in = sum(IN_SPLITS)
    return {
        'x_prompt': nrm((BATCH, SEQ, D_MODEL), 1.0),
        'x_sample': nrm((DEC_BATCH, DEC_SEQ, D_MODEL), 1.0),
        'c_prompt': nrm((BATCH, D_MODEL), 1.0),
        'c_sample': nrm((DEC_BATCH, D_MODEL), 1.0),
        'state_gdn': nrm((DEPTH, DEC_BATCH, GDN_H, GDN_DK, GDN_DV), 0.1),
        'state_gdn_conv': nrm((DEPTH, DEC_BATCH, CONV_K - 1, GDN_CONV_W), 1.0),
        'state_hgrn': nrm((DEPTH, DEC_BATCH, HG_H, HG_DK, HG_DV), 0.5),
        'state_ssd': nrm((DEPTH, DEC_BATCH, SSD_H, SSD_N, SSD_P), 0.1),
        'state_ssd_conv': nrm((DEPTH, DEC_BATCH, CONV_K - 1, SSD_CONV_W), 1.0),
        'state_mlstm_c': nrm((DEPTH, DEC_BATCH, ML_H, ML_DK, ML_DV), 0.1),
        'state_mlstm_n': nrm((DEPTH, DEC_BATCH, ML_H, ML_DK), 0.1),
        'state_mlstm_m': nrm((DEPTH, DEC_BATCH, ML_H), 1.0),
        'ada_w': nrm((DEPTH, D_MODEL, 6 * D_MODEL), 0.5 * D_MODEL ** -0.5),
        'ada_b': nrm((DEPTH, 6 * D_MODEL), 0.02),
        'norm1_w': 1.0 + nrm((DEPTH, D_MODEL), 0.1),
        'norm2_w': 1.0 + nrm((DEPTH, D_MODEL), 0.1),
        'w_in': nrm((DEPTH, D_MODEL, n_in), D_MODEL ** -0.5),
        'gdn_conv_w': nrm((DEPTH, CONV_K, GDN_CONV_W), CONV_K ** -0.5),
        'gdn_conv_b': nrm((DEPTH, GDN_CONV_W), 0.02),
        'gdn_a_log': a_log((DEPTH, GDN_H)),
        'gdn_dt_bias': dt_bias((DEPTH, GDN_H)),
        'gdn_norm_w': 1.0 + nrm((DEPTH, GDN_DV), 0.1),
        'hg_lb_logits': nrm((DEPTH, HG_H * HG_DK), 1.0),
        'hg_norm_w': 1.0 + nrm((DEPTH, HG_DV), 0.1),
        'ssd_conv_w': nrm((DEPTH, CONV_K, SSD_CONV_W), CONV_K ** -0.5),
        'ssd_conv_b': nrm((DEPTH, SSD_CONV_W), 0.02),
        'ssd_a_log': a_log((DEPTH, SSD_H)),
        'ssd_dt_bias': dt_bias((DEPTH, SSD_H)),
        'ssd_d': 1.0 + nrm((DEPTH, SSD_H), 0.1),
        'ssd_norm_w': 1.0 + nrm((DEPTH, SSD_H * SSD_P), 0.1),
        'ml_b_i': nrm((DEPTH, ML_H), 0.1),
        'ml_b_f': 3.0 + nrm((DEPTH, ML_H), 0.5),
        'ml_norm_w': 1.0 + nrm((DEPTH, ML_DV), 0.1),
        'w_branch': nrm((DEPTH, N_BRANCH, BRANCH_W, D_MODEL), BRANCH_W ** -0.5),
        'w_out': nrm((DEPTH, D_MODEL, D_MODEL), D_MODEL ** -0.5),
        'ffn_w_in': nrm((DEPTH, D_MODEL, 2 * D_FF), D_MODEL ** -0.5),
        'ffn_w_out': nrm((DEPTH, D_FF, D_MODEL), D_FF ** -0.5),
        'final_norm_w': 1.0 + nrm((D_MODEL,), 0.1),
    }

def reference(x_prompt, x_sample, c_prompt, c_sample, state_gdn, state_gdn_conv, state_hgrn,
              state_ssd, state_ssd_conv, state_mlstm_c, state_mlstm_n, state_mlstm_m,
              ada_w, ada_b, norm1_w, norm2_w, w_in, gdn_conv_w, gdn_conv_b, gdn_a_log,
              gdn_dt_bias, gdn_norm_w, hg_lb_logits, hg_norm_w, ssd_conv_w, ssd_conv_b,
              ssd_a_log, ssd_dt_bias, ssd_d, ssd_norm_w, ml_b_i, ml_b_f, ml_norm_w,
              w_branch, w_out, ffn_w_in, ffn_w_out, final_norm_w):
    sm = jax.nn.softmax(hg_lb_logits.astype(jnp.float32), axis=0)
    hg_lb = jnp.cumsum(sm, axis=0) - sm[0]
    P = dict(ada_w=ada_w, ada_b=ada_b, norm1_w=norm1_w, norm2_w=norm2_w, w_in=w_in,
             gdn_conv_w=gdn_conv_w, gdn_conv_b=gdn_conv_b, gdn_a_log=gdn_a_log,
             gdn_dt_bias=gdn_dt_bias, gdn_norm_w=gdn_norm_w, hg_lb=hg_lb, hg_norm_w=hg_norm_w,
             ssd_conv_w=ssd_conv_w, ssd_conv_b=ssd_conv_b, ssd_a_log=ssd_a_log,
             ssd_dt_bias=ssd_dt_bias, ssd_d=ssd_d, ssd_norm_w=ssd_norm_w, ml_b_i=ml_b_i,
             ml_b_f=ml_b_f, ml_norm_w=ml_norm_w, w_branch=w_branch, w_out=w_out,
             ffn_w_in=ffn_w_in, ffn_w_out=ffn_w_out)
    sample_states = (state_gdn, state_gdn_conv, state_hgrn, state_ssd, state_ssd_conv,
                     state_mlstm_c, state_mlstm_n, state_mlstm_m)
    prompt_init = tuple(jnp.zeros((DEPTH, x_prompt.shape[0]) + s.shape[2:], jnp.float32)
                        for s in sample_states)
    y_prompt, new_p = _trunk(x_prompt, c_prompt, prompt_init, P, final_norm_w)
    y_sample, new_s = _trunk(x_sample, c_sample, sample_states, P, final_norm_w)
    p_gdn, p_gdn_conv, p_hgrn, p_ssd, p_ssd_conv, p_mc, p_mn, p_mm = new_p
    s_gdn, s_gdn_conv, s_hgrn, s_ssd, s_ssd_conv, s_mc, s_mn, s_mm = new_s
    return (y_prompt, y_sample, p_gdn, p_gdn_conv, p_hgrn, p_ssd, p_ssd_conv, p_mc, p_mn, p_mm,
            s_gdn, s_gdn_conv, s_hgrn, s_ssd, s_ssd_conv, s_mc, s_mn, s_mm)


_drawn_inputs = setup_inputs


def setup_inputs(seed=0):
    import zlib

    import numpy as np

    out = dict(_drawn_inputs(seed))
    spreads = {}
    factors = {'gdn_norm_w': 6.805,
     'hg_norm_w': 5.467,
     'ssd_d': 22.369,
     'ssd_norm_w': 3.893,
     'ml_norm_w': 6.163,
     'norm2_w': 3.155}
    for name, (base, spread) in spreads.items():
        noise = np.random.default_rng([zlib.crc32(name.encode()), seed]).standard_normal(out[name].shape)
        drawn = base * np.exp(spread * noise) if base else spread * noise
        out[name] = __import__('jax').numpy.asarray(drawn.astype(out[name].dtype))
    for name, factor in factors.items():
        out[name] = (out[name] * factor).astype(out[name].dtype)
    return out
```

```python
from contextlib import ExitStack

import numpy as np

import concourse.bass as bass
from concourse import mybir

F32 = mybir.dt.float32
ALU = mybir.AluOpType
ACT = mybir.ActivationFunctionType
AX = mybir.AxisListType

P = 128
D = 1024
KD = D // P
T = 512
NB, ND = 8, 4
NS = NB * ND
TA = T + NS
HN = TA // 2
NT = T // P
FF = 2816
KF = FF // P
DK = 64
EPS = 1e-6
BIG = 1e30
R = 4
SLOT = 2048

GROUP_COLS = [0, 256, 512, 768, 1032, 1288, 1544, 1800, 2056, 2312, 2568, 2832, 3088, 3344, 3600]
C_GB, C_GA, C_DT, C_MI, C_MF, C_GATE = 1024, 1028, 2824, 3856, 3860, 3864
GQ, GK, GV, GZ, HQ, HF, HI, HG, SZ, SX, SB, SC, MQ, MK, MV, MO = 0, 2, 4, 6, 8, 10, 12, 14, 16, 18, 20, 21, 22, 24, 26, 28
BR = [GV, GV + 1, HI, HI + 1, SX, SX + 1, MV, MV + 1]
CONV = [0, 1, 2, 3, 4, 5, 18, 19, 20, 21]
R_G, R_S, R_M, NR = 0, 32, 64, 96
T_G, T_S, T_M, NCOL = 0, 4, 12, 16
LEVELS = [1, 2, 4, 8, 16, 32, 64]

K_ID, K_B64, K_ONE, K_MASK, K_NEG, K_NEGS, K_RST, K_OWN, K_SGN, K_N = 0, 128, 256, 384, 1280, 1408, 1440, 1984, 1992, 1993
V_ADAB, V_N1, V_N2, V_NF, V_GCW, V_GCB, V_SCW, V_SCB, V_1 = 0, 48, 56, 64, 72, 96, 102, 118, 122
V_SN, V_GN, V_HN, V_MN, V_2 = 122, 124, 125, 126, 127


def host_constants():
    c = np.zeros((P, K_N), np.float32)
    i = np.arange(P)
    c[:, K_ID:K_ID + P] = np.eye(P)
    c[:, K_B64:K_B64 + P] = i[:, None] // DK == i[None] // DK
    c[:, K_ONE:K_ONE + P] = 1
    m, l = i[:, None], i[None]
    for n, s in enumerate(LEVELS):
        c[:, K_MASK + n * P:K_MASK + (n + 1) * P] = (m // (2 * s) == l // (2 * s)) & (m % (2 * s) < s) & (l % (2 * s) >= s)
    c[:, K_NEG:K_NEG + P] = np.where(m <= l, 0, -BIG)
    m, l = m[:NS], l[:, :NS]
    c[:NS, K_NEGS:K_NEGS + NS] = np.where((m <= l) & (m // ND == l // ND), 0, -BIG)
    reset = np.ones(TA)
    reset[0:T:P] = 0
    reset[T::ND] = 0
    c[:, K_RST:K_RST + TA] = reset
    c[:NS, K_OWN:K_OWN + NB] = i[:NS, None] // ND == np.arange(NB)
    c[:, K_SGN] = np.where(i < R_M, 1, -1)
    return c


class Chain:

    def __init__(self, sem, stages):
        self.sem, self.stages = sem, stages
        self.at = {(t, name): n for n, (t, name, _) in enumerate(stages)}

    def begin(self, eng, t, name):
        n = self.at[(t, name)]
        if n:
            eng.wait_ge(self.sem, n)

    def after(self, eng, t, name):
        eng.wait_ge(self.sem, self.at[(t, name)] + 1)


def gdn_stages(t):
    s = [("tokens", "pe"), ("scale", "dve"), ("bcast", "pe"), ("diff", "dve"), ("decay", "act"), ("kk", "pe"),
         ("lower", "dve"), ("first", "pe"), ("t1", "act")]
    for n in levels_of(t)[1:]:
        s += [(f"x{n}", "pe"), (f"xc{n}", "act"), (f"y{n}", "pe"), (f"upd{n}", "dve")]
    s += [("qk", "pe"), ("aq", "dve"), ("sk", "pe"), ("skc", "act"), ("u", "pe"), ("uc", "dve")]
    if t == NT:
        s += [("ut", "pe"), ("utc", "dve")]
    s += [("out", "pe"), ("outc", "dve")]
    if t == NT:
        s += [("state", "pe"), ("statec", "dve")]
    return [(t, "g_" + n, e) for n, e in s]


def rest_stages(t):
    s = [("h_qk", "pe"), ("h_diag", "dve")]
    for n in levels_of(t):
        s += [(f"h_dec{n}", "act"), (f"h_sc{n}", "dve"), (f"h_qk{n}", "pe"), (f"h_add{n}", "dve")]
    s += [("h_dec", "act"), ("h_kd", "dve"), ("h_tok", "pe"), ("h_tokc", "dve"), ("h_out", "pe"), ("h_outc", "dve")]
    if t == NT:
        s += [("h_state", "pe"), ("h_statec", "dve")]
    s += [("s_bcast", "pe"), ("s_diff", "dve"), ("s_decay", "act"), ("s_cb", "pe"), ("s_att", "dve"), ("s_e", "pe"),
          ("s_q", "dve"), ("s_out", "pe"), ("s_outc", "dve")]
    if t == NT:
        s += [("s_state", "pe"), ("s_statec", "dve")]
    s += [("m_tok", "pe"), ("m_scale", "dve"), ("m_bcast", "pe"), ("m_diff", "dve"), ("m_decay", "act"), ("m_qk", "pe"),
          ("m_att", "dve"), ("m_out", "pe"), ("m_outc", "dve"), ("m_den", "pe"), ("m_denc", "dve")]
    if t == NT:
        s += [("m_state", "pe"), ("m_statec", "dve"), ("m_norm", "pe"), ("m_normc", "dve")]
    return [(t, n, e) for n, e in s]


def levels_of(t):
    return range(len(LEVELS)) if t < NT else range(2)


def merged(a, b):
    out, i, j = [], 0, 0
    while i < len(a) or j < len(b):
        if j >= len(b) or (i < len(a) and i * len(b) <= j * len(a)):
            out.append(("g",) + a[i])
            i += 1
        else:
            out.append(("r",) + b[j])
            j += 1
    return out


def trunk(nc, A, O):
    ctx = ExitStack()
    with ctx:
        ctx.enter_context(nc.allow_non_contiguous_dma(reason="state vectors, a few KB"))

        def sb(name, shape):
            return ctx.enter_context(nc.sbuf_tensor(name, shape, F32))

        def sem(name):
            return ctx.enter_context(nc.semaphore(name))

        ps = ctx.enter_context(nc.psum_tensor("ps", [P, 8, 512], F32))
        cst = sb("cst", [P, K_N])
        vt = sb("vt", [P, V_2])
        vrow = sb("vrow", [P, 2, P])
        xT = sb("xT", [P, KD, TA])
        hT = sb("hT", [P, KD, TA])
        pj = sb("pj", [P, 30, TA])
        ring = sb("ring", [P, R, SLOT])
        cT = sb("cT", [P, KD, NB + 1])
        mod = sb("mod", [P, 6 * KD, NB + 1])
        coef = sb("coef", [P, KD, NB + 1])
        rstd = sb("rstd", [P, TA])
        colp = sb("colp", [P, 4])
        hcol = sb("hcol", [P, 2, 6])
        dcol = sb("dcol", [P, 2])
        hrow = sb("hrow", [P, 264])
        cols = sb("cols", [P, NT + 1, 4, NCOL])
        Rr = sb("Rr", [P, TA])
        Er = sb("Er", [P, TA])
        Vr = sb("Vr", [P, TA])
        MTr = sb("MTr", [P, TA])
        kg = sb("kg", [P, 2, TA])
        S_g = sb("S_g", [P, 2, DK])
        S_h = sb("S_h", [P, 2, DK])
        S_s = sb("S_s", [P, 4, 32])
        S_c = sb("S_c", [P, 2, DK])
        S_n = sb("S_n", [P, 2, DK])
        Q_g = sb("Q_g", [P, 2, NB, DK])
        Q_r = sb("Q_r", [P, 2, NB, DK])
        Q_n = sb("Q_n", [P, 2, NB, DK])
        eG = sb("eG", [P, 2, NB])
        eR = sb("eR", [P, 4, NB])
        scr = sb("scr", [P, 4352 + 3584])

        def part(at, n):
            return scr[:, at:at + n]

        wsm = part(6256, KD * 2 * NR).rearrange("p (k e r) -> p k e r", k=KD, e=2)

        gT, gU, gX, gL, gD = (part(512 * n, 512) for n in range(5))
        gAt = part(4352 + 3584 - 512, 512)
        g_vb, g_kn, g_kd, g_u, g_sk, g_qs, g_kb = (part(2560 + 256 * n, 256) for n in range(7))
        g_Ue = part(0, 2048)
        B0 = 4352
        bD = part(B0, 1024)
        bX, bQl, bKl, bEf = part(B0 + 512, 512), part(B0 + 1024, 256), part(B0 + 1280, 256), part(B0 + 1536, 256)
        bKd, bV, bQ, bKt = part(B0 + 1792, 512), part(B0 + 2304, 256), part(B0 + 2560, 512), part(B0 + 1536, 256)
        b_Ue = part(B0, 2048)
        b_Kd2 = part(B0 + 2048, 512)

        ident = cst[:, K_ID:K_ID + P]
        b64 = cst[:, K_B64:K_B64 + P]
        ones = cst[:, K_ONE:K_ONE + P]

        def mask(n, p):
            return cst[0:p, K_MASK + n * P:K_MASK + n * P + p]

        def neg(t):
            return cst[:, K_NEG:K_NEG + P] if t < NT else cst[0:NS, K_NEGS:K_NEGS + NS]

        d_cst, d_vec, d_x, d_c, d_wsm, d_row, d_hist, d_st = (sem(n) for n in
            ("d_cst", "d_vec", "d_x", "d_c", "d_wsm", "d_row", "d_hist", "d_st"))
        d_q = [sem("d_q_gdn"), sem("d_q_hgrn"), sem("d_q_ssd"), sem("d_q_mlstm"), sem("d_wb")]
        w_in_slot = [sem(f"w_in_slot{n}") for n in range(R)]
        w_used = sem("w_used")
        zeroed = sem("zeroed")
        tile_done = sem("tile_done")
        tile_read = sem("tile_read")
        lin_done, lin_read = sem("lin_done"), sem("lin_read")
        stored = sem("stored")
        pre_s, gdn_s, rest_s, mid_s = sem("pre"), sem("gdn"), sem("rest"), sem("mid")

        pre = [("vec", "pe"), ("vecc", "dve"), ("silc", "act"), ("ct", "pe"), ("ctc", "dve")]
        for d in range(KD):
            pre += [(f"x{d}", "pe"), (f"xc{d}", "act")]
        pre += [("sq1", "dve"), ("ss1", "pe"), ("rs1", "act"), ("ada1", "pe"), ("mod1", "dve"), ("norm1", "dve"),
                ("proj", "pe"), ("projc", "act"), ("ada2", "pe"), ("mod2", "dve"),
                ("small", "pe"), ("hist", "dve"), ("tail", "pe"), ("tailc", "dve")]
        for n in range(len(CONV)):
            pre += [(f"conv{n}", "dve"), (f"silu{n}", "act")]
        pre += [("l2sq", "dve"), ("l2a", "pe"), ("l2ra", "act"), ("l2b", "pe"), ("l2rb", "act"), ("l2m", "dve")]
        pre += [("rz", "dve"), ("rabs", "act"), ("rln", "act"), ("rsp", "dve"), ("rexp", "act"), ("rv", "dve"), ("rcol", "pe"),
                ("rcolc", "dve")]
        pre += [("lb0", "dve"), ("lb1", "act"), ("lb2", "dve"), ("lb3", "pe"), ("lb4", "dve"), ("lb5", "act"), ("lb6", "dve")]
        for f in range(2):
            pre += [(f"f_ls{f}", "act"), (f"f_b{f}", "dve"), (f"f_ln{f}", "act"), (f"f_g{f}", "dve")]
        pre = Chain(pre_s, [(0, n, e) for n, e in pre])
        gdn_list = [s for t in range(NT + 1) for s in gdn_stages(t)]
        rest_list = [s for t in range(NT + 1) for s in rest_stages(t)]
        gdn, rest = Chain(gdn_s, gdn_list), Chain(rest_s, rest_list)
        order = [s for t in range(NT + 1) for s in merged(gdn_stages(t), rest_stages(t))]
        mid = []
        for n in range(4):
            mid += [(f"o_sq{n}", "dve"), (f"o_ss{n}", "pe"), (f"o_rs{n}", "act"), (f"o_n{n}", "dve")]
        mid += [("up", "pe"), ("upc", "dve"), ("wout", "pe"), ("res1", "dve"), ("sq2", "dve"), ("ss2", "pe"), ("rs2", "act"),
                ("norm2", "dve"), ("ffa", "pe"), ("ffac", "dve"), ("ffb", "pe"), ("res2", "dve"), ("sq3", "dve"), ("ss3", "pe"),
                ("rs3", "act"), ("norm3", "dve")]
        for t in range(NT + 1):
            mid += [(f"y{t}", "pe"), (f"yc{t}", "act")]
        mid = Chain(mid_s, [(0, n, e) for n, e in mid])

        phases = [("ada1", 8), ("mixer", 15), ("ada2", 16), ("gate", 16), ("wout", 4), ("ffa", 22), ("ffb", 16)]
        first, n = {}, 0
        for kind, count in phases:
            first[kind] = n
            n += count
        counts = dict(phases)
        tiles_before = {"mixer": 0, "gate": 30, "wout": 62, "ffa": 70, "ffb": 92}

        def over(eng, kind, body, peel=0):
            n0, count = first[kind], counts[kind]
            done = 0
            while done < peel:
                body((n0 + done) % R, done, n0 + done)
                done += 1
            full = (count - done) // R
            if full:
                with eng.Fori(0, full) as i:
                    for r in range(R):
                        body((n0 + done + r) % R, i * R + (done + r), i * R + (n0 + done + r))
                done += full * R
            while done < count:
                body((n0 + done) % R, done, n0 + done)
                done += 1

        def landed(eng, slot, n):
            if isinstance(n, int):
                eng.wait_ge(w_in_slot[slot], 32 * (n // R + 1))
            else:
                eng.wait_ge(w_in_slot[slot], n * (32 // R) + (32 - slot * (32 // R)))

        block = ctx.enter_context(nc.Block())

        @block.sync
        def _(sp):
            sp.dma_start(cst[:, :], A["const"]).then_inc(d_cst, 16)
            sp.dma_start(xtok(pj), A["x_prompt"][0].rearrange("(a p) d -> p a d", p=P)).then_inc(d_x, 16)
            sp.dma_start(xstok(pj), A["x_sample"].rearrange("b t d -> (b t) d")).then_inc(d_x, 16)
            sp.dma_start(ctok(pj)[0:1, :], A["c_prompt"]).then_inc(d_c, 16)
            sp.dma_start(ctok(pj)[1:NB + 1, :], A["c_sample"]).then_inc(d_c, 16)
            rows = lambda a, n: A[a].rearrange("o (r c) -> (o r) c", c=P)
            for name, at, n in (("ada_b", V_ADAB, 48), ("norm1_w", V_N1, 8), ("norm2_w", V_N2, 8),
                                ("gdn_conv_b", V_GCB, 6), ("ssd_conv_b", V_SCB, 4)):
                sp.dma_start(vrow[at:at + n, 0, :], rows(name, n)).then_inc(d_vec, 16)
            sp.dma_start(vrow[V_NF:V_NF + 8, 0, :], A["final_norm_w"].rearrange("(r c) -> r c", c=P)).then_inc(d_vec, 16)
            sp.dma_start(vrow[V_GCW:V_GCW + 24, 0, :], A["gdn_conv_w"].rearrange("o k (r c) -> (o k r) c", c=P)).then_inc(d_vec, 16)
            sp.dma_start(vrow[V_SCW:V_SCW + 16, 0, :], A["ssd_conv_w"].rearrange("o k (r c) -> (o k r) c", c=P)).then_inc(d_vec, 16)
            sp.dma_start(vrow[0:2, 1, :], rows("ssd_norm_w", 2)).then_inc(d_vec, 16)
            for n, name in enumerate(("gdn_norm_w", "hg_norm_w", "ml_norm_w")):
                for h in range(2):
                    sp.dma_start(vrow[2 + n:3 + n, 1, h * DK:(h + 1) * DK], A[name]).then_inc(d_vec, 16)
            sp.dma_start(hrow[0:1, 256:264], A["ssd_d"]).then_inc(d_vec, 16)
            sp.dma_start(hrow[0:1, 0:256], A["hg_lb_logits"]).then_inc(d_vec, 16)

            def load(kind, slot, idx, n):
                if not isinstance(n, int) or n >= R:
                    sp.wait_ge(w_used, n - (R - 1))
                full = ring[:, slot, :]
                if kind in ("ada1", "ada2", "mixer", "wout"):
                    src = {"ada1": "ada_w", "ada2": "ada_w", "mixer": "w_in", "wout": "w_out"}[kind]
                    src = A[src][0].rearrange("(k p) c -> p k c", p=P)
                    if kind == "mixer":
                        c0 = GROUP_COLS[idx]
                    else:
                        c0 = idx * 256 + (2048 if kind == "ada2" else 0)
                    dst = full.rearrange("p (k c) -> p k c", k=KD)
                    for h in range(2):
                        sp.dma_start(dst[:, 4 * h:4 * h + 4, :], src[:, 4 * h:4 * h + 4, bass.ds(c0, 256)]).then_inc(w_in_slot[slot], 16)
                elif kind == "gate":
                    dst = full.rearrange("p (k e c) -> p k e c", k=KD, e=2)
                    src = A["w_in"][0].rearrange("(k p) c -> p k c", p=P)
                    par, base = idx
                    for e in range(2):
                        c0 = base * P + (C_GATE + (2 * par + e) * D)
                        sp.dma_start(dst[:, :, e, :], src[:, :, bass.ds(c0, P)]).then_inc(w_in_slot[slot], 16)
                elif kind == "ffa":
                    dst = full.rearrange("p (k e c) -> p k e c", k=KD, e=2)
                    src = A["ffn_w_in"][0].rearrange("(k p) c -> p k c", p=P)
                    for e in range(2):
                        sp.dma_start(dst[:, :, e, :], src[:, :, bass.ds(idx * P + e * FF, P)]).then_inc(w_in_slot[slot], 16)
                else:
                    dst = full[:, 0:11 * P].rearrange("p (k c) -> p k c", c=P)
                    src = A["ffn_w_out"][0].rearrange("(k p) c -> p k c", p=P)
                    par, base = idx
                    for k0, k1 in ((0, 6), (6, 11)):
                        sp.dma_start(dst[:, k0:k1, :], src[:, 11 * par + k0:11 * par + k1, bass.ds(base * P, P)]).then_inc(w_in_slot[slot], 16)

            over(sp, "ada1", lambda slot, idx, n: load("ada1", slot, idx, n), peel=R)
            sp.wait_ge(zeroed, 1)
            for e, at, c0, w in ((0, R_G, C_GA, 4), (0, R_S, C_DT, 8), (0, R_M, C_MF, 4), (1, R_G, C_GB, 4), (1, R_M, C_MI, 4)):
                sp.dma_start(wsm[:, :, e, at:at + w], A["w_in"][0].rearrange("(k p) c -> p k c", p=P)[:, :, c0:c0 + w]).then_inc(d_wsm, 16)
            for at, name, c in ((R_G, "gdn_dt_bias", 0), (R_S, "ssd_dt_bias", 0), (R_M, "ml_b_f", 0),
                                (R_G, "gdn_a_log", 1), (R_S, "ssd_a_log", 1), (R_M, "ml_b_i", 2)):
                w = A[name].shape[1]
                sp.dma_start(colp[at:at + w, c:c + 1], A[name].rearrange("o h -> h o")).then_inc(d_row, 16)
            for idx in range(15):
                n = first["mixer"] + idx
                load("mixer", n % R, idx, n)
            pre.after(sp, 0, "norm1")
            sp.dma_start(hist(scr)[:, 0:768], A["state_gdn_conv"][0].rearrange("b k c -> (b k) c")).then_inc(d_hist, 16)
            sp.dma_start(hist(scr)[:, 768:1280], A["state_ssd_conv"][0].rearrange("b k c -> (b k) c")).then_inc(d_hist, 16)
            for p in range(2):
                for q in range(2):
                    at = slice(q * DK, (q + 1) * DK)
                    sp.dma_start(Q_g[at, p], A["state_gdn"][0, :, 2 * p + q].rearrange("b k v -> k b v")).then_inc(d_q[0], 16)
                    sp.dma_start(Q_r[at, p], A["state_hgrn"][0, :, 2 * p + q].rearrange("b k v -> k b v")).then_inc(d_q[1], 16)
            sp.dma_start(MTs(hrow)[64:68, 0:NB * 5:5], A["state_mlstm_m"][0].rearrange("b h -> h b")).then_inc(d_st, 16)
            over(sp, "ada2", lambda slot, idx, n: load("ada2", slot, idx, n))
            pre.after(sp, 0, "tailc")
            tl = tail(scr)
            for c0, c1, po, so in ((0, 768, O[3], O[11]), (768, 1280, O[6], O[14])):
                sp.dma_start(po[0, 0], tl[NS - 3:NS, c0:c1]).then_inc(stored, 16)
                for b in range(NB):
                    r0 = NS + ND * b + 1
                    sp.dma_start(so[0, b], tl[r0:r0 + 3, c0:c1]).then_inc(stored, 16)
            pre.after(sp, 0, f"f_g1")
            for r in range(R):
                n = first["gate"] + r
                load("gate", n % R, (r % 2, r // 2), n)
            rest.after(sp, NT, "h_statec")
            stored_at = [18 * 16]

            def store(dst, src):
                sp.dma_start(dst, src).then_inc(stored, 16)
                stored_at[0] += 16

            def heads(dst, S, w=DK):
                for p in range(2):
                    for q in range(2):
                        store(dst[2 * p + q], S[q * DK:(q + 1) * DK, p])

            def qheads(dst, S):
                for p in range(2):
                    for q in range(2):
                        store(dst[:, 2 * p + q].rearrange("b k v -> k b v"), S[q * DK:(q + 1) * DK, p])

            qheads(O[12][0], Q_r)
            sp.wait_ge(stored, stored_at[0])
            for g in range(2):
                for j in range(4):
                    sp.dma_start(Qs(Q_r)[g * DK:(g + 1) * DK, j], A["state_ssd"][0, :, 4 * g + j].rearrange("b n v -> n b v")).then_inc(d_q[2], 16)
            for p in range(2):
                for q in range(2):
                    sp.dma_start(Q_n[q * DK:(q + 1) * DK, p, :, 0], A["state_mlstm_n"][0, :, 2 * p + q].rearrange("b k -> k b")).then_inc(d_q[3], 16)
            rest.after(sp, NT, "s_statec")
            for g in range(2):
                for j in range(4):
                    store(O[13][0, :, 4 * g + j].rearrange("b n v -> n b v"), Qs(Q_r)[g * DK:(g + 1) * DK, j])
            sp.wait_ge(stored, stored_at[0])
            for p in range(2):
                for q in range(2):
                    sp.dma_start(Q_r[q * DK:(q + 1) * DK, p], A["state_mlstm_c"][0, :, 2 * p + q].rearrange("b k v -> k b v")).then_inc(d_q[3], 16)
            rest.after(sp, NT, "m_normc")
            gdn.after(sp, NT, "g_statec")
            qheads(O[10][0], Q_g)
            qheads(O[15][0], Q_r)
            for p in range(2):
                for q in range(2):
                    store(O[16][0, :, 2 * p + q].rearrange("b k -> k b"), Q_n[q * DK:(q + 1) * DK, p, :, 0])
                    store(O[8][0, 0, 2 * p + q].unsqueeze(1), S_n[q * DK:(q + 1) * DK, p, 0:1])
            store(O[9][0].rearrange("o h -> h o"), MTr[R_M:R_M + 4, T - 1:T])
            store(O[17][0].rearrange("b h -> h b"), MTr[R_M:R_M + 4, T + ND - 1:TA:ND])
            heads(O[2][0, 0], S_g)
            heads(O[4][0, 0], S_h)
            heads(O[7][0, 0], S_c)
            for g in range(2):
                for j in range(4):
                    store(O[5][0, 0, 4 * g + j], S_s[g * DK:(g + 1) * DK, j])
            sp.dma_start(wb(scr), A["w_branch"][0].rearrange("n (k p) c -> p (n k) c", p=P)[:, 0:WB_A, :]).then_inc(d_q[4], 16)
            mid.after(sp, 0, "o_n3")
            sp.dma_start(wb2(pj), A["w_branch"][0].rearrange("n (k p) c -> p (n k) c", p=P)[:, WB_A:8, :]).then_inc(d_q[4], 16)
            with sp.Fori(0, 3) as i:
                for r in range(R):
                    n = i * R + (first["gate"] + R + r)
                    load("gate", (first["gate"] + r) % R, (r % 2, i * 2 + (2 + r // 2)), n)
            over(sp, "wout", lambda slot, idx, n: load("wout", slot, idx, n))
            over(sp, "ffa", lambda slot, idx, n: load("ffa", slot, idx, n))
            with sp.Fori(0, 4) as i:
                for r in range(R):
                    n = i * R + (first["ffb"] + r)
                    load("ffb", (first["ffb"] + r) % R, (r % 2, i * 2 + r // 2), n)
            for t in range(NT + 1):
                mid.after(sp, 0, f"yc{t}")
                yt = ytok(pj, t)
                store(O[0][0, t * P:(t + 1) * P, :] if t < NT else O[1].rearrange("b t d -> (b t) d"), yt)
            sp.wait_ge(stored, stored_at[0])

        @block.gpsimd
        def _(pool):
            pool.memset(wsm[:, :, :, :], 0.0)
            pool.memset(colp[:, :], 0.0)
            pool.drain()
            for S in (S_g, S_h, S_s, S_c, S_n):
                pool.memset(S[:, :, :], 0.0)
            pool.drain().then_inc(zeroed, 1)

        @block.tensor
        def _(pe):
            def mm(out, lhsT, rhs, start=True, stop=True):
                return pe.matmul(out, lhsT, rhs, start=start, stop=stop, skip_group_check=True)

            def tr(out, in_):
                n = in_.shape[0]
                return pe.transpose(out, in_, ident[0:n, 0:n])

            pe.wait_ge(d_cst, 16)
            pe.wait_ge(d_vec, 16 * 17)
            tr(ps[:, 4, 0:V_1], vrow[0:V_1, 0, :])
            tr(ps[:, 4, V_1:V_2], vrow[0:V_2 - V_1, 1, :]).then_inc(pre_s, 1)
            pre.begin(pe, 0, "ct")
            for k in range(KD):
                last = tr(ps[:, 5, (NB + 1) * k:(NB + 1) * (k + 1)], ctok(pj)[0:NB + 1, k * P:(k + 1) * P])
            last.then_inc(pre_s, 1)
            pe.wait_ge(d_x, 32)
            for d in range(KD):
                pre.begin(pe, 0, f"x{d}")
                for a in range(NT):
                    tr(ps[:, 0, a * P:(a + 1) * P], xtok(pj)[:, a, d * P:(d + 1) * P])
                tr(ps[:, 1, 0:NS], xstok(pj)[:, d * P:(d + 1) * P]).then_inc(pre_s, 1)

            def sumsq(chain, name, src, weights):
                chain.begin(pe, 0, name)
                for h in range(2):
                    for k, s in enumerate(src):
                        last = mm(ps[:, 4 + h, 0:HN], weights, s[:, h * HN:(h + 1) * HN], k == 0, k == len(src) - 1)
                last.then_inc(chain.sem, 1)

            sumsq(pre, "ss1", [hT[:, k, :] for k in range(KD)], ones)

            def ada(kind, base):
                def body(slot, idx, n):
                    landed(pe, slot, n)
                    for c in range(2):
                        for k in range(KD):
                            last = mm(ps[:, 7, cur[0] * 9:cur[0] * 9 + 9],
                                      ring[:, slot, k * 256 + c * P:k * 256 + (c + 1) * P], cT[:, k, :], k == 0, k == KD - 1)
                        cur[0] += 1
                    last.then_inc(w_used, 1)
                cur = [base]
                for idx in range(counts[kind]):
                    n = first[kind] + idx
                    body(n % R, idx, n)

            pre.begin(pe, 0, "ada1")
            ada("ada1", 0)
            pe.drain().then_inc(pre_s, 1)

            def gemm_tile(pair, weights, src, sems):
                for h in range(2):
                    for k, (w, s) in enumerate(zip(weights, src)):
                        last = mm(ps[:, pair + h, 0:HN], w, s[:, h * HN:(h + 1) * HN], k == 0, k == len(src) - 1)
                last.then_inc(sems, 1)
                return last

            hs = [hT[:, k, :] for k in range(KD)]
            pre.begin(pe, 0, "proj")

            def proj(slot, idx, n):
                landed(pe, slot, n)
                for c in range(2):
                    if not isinstance(idx, int) or idx >= 1:
                        pe.wait_ge(tile_read, idx * 2 + (c - 1))
                    gemm_tile(2 * c, [ring[:, slot, k * 256 + c * P:k * 256 + (c + 1) * P] for k in range(KD)], hs, tile_done)
                pe.drain().then_inc(w_used, 1)
            over(pe, "mixer", proj, peel=3)
            pe.drain().then_inc(pre_s, 1)
            pre.begin(pe, 0, "ada2")
            ada("ada2", 16)
            pe.drain().then_inc(pre_s, 1)
            pre.begin(pe, 0, "small")
            pe.wait_ge(d_wsm, 80)
            for e in range(2):
                for h in range(2):
                    for k in range(KD):
                        mm(ps[0:NR, 2 * e + h, 0:HN], wsm[:, k, e, :], hT[:, k, h * HN:(h + 1) * HN], k == 0, k == KD - 1)
            pe.wait_ge(d_hist, 32)
            for n in range(len(CONV)):
                last = tr(ps[:, 6, n * 24:(n + 1) * 24], hist(scr)[:, n * P:(n + 1) * P])
            last.then_inc(pre_s, 1)
            pre.begin(pe, 0, "tail")
            for n, f in enumerate(CONV):
                last = tr(ps[0:2 * NS, 4 + n // 4, (n % 4) * P:(n % 4 + 1) * P], pj[:, f, T - NS:TA])
            last.then_inc(pre_s, 1)
            for name, f0 in (("l2a", 0), ("l2b", 2)):
                pre.begin(pe, 0, name)
                for f in range(2):
                    for h in range(2):
                        last = mm(ps[:, 4 + 2 * f + h, 0:HN], b64, part(544 * (f0 + f), TA)[:, h * HN:(h + 1) * HN])
                last.then_inc(pre_s, 1)
            pre.begin(pe, 0, "rcol")
            for t in range(NT + 1):
                c0, w = t * P, (P if t < NT else NS)
                for n, src in enumerate((RS(scr), RK(scr), Vr, RN(scr))):
                    last = tr(ps[0:w, 3 + t, n * NR:(n + 1) * NR], src[0:NR, c0:c0 + w])
            last.then_inc(pre_s, 1)
            pre.begin(pe, 0, "lb3")
            for p in range(2):
                mm(ps[:, 4, p:p + 1], hrow[0:1, p * P:(p + 1) * P], ones[0:1, 0:1])
                last = mm(ps[:, 4, 2 + p:3 + p], hrow2(scr)[0:1, p * P:(p + 1) * P], ones[0:1, 0:1])
            last.then_inc(pre_s, 1)

            def pick(h, n):
                return ident[0:NR, h:h + 1].to_broadcast([NR, n])

            def bcast2(out, h0, step, rows):
                for q in range(2):
                    last = mm(out[half(q)], pick(h0 + step * q, DK), rows)
                return last

            def half(q):
                return slice(q * DK, (q + 1) * DK)

            def gdn_pe():
                for t in range(NT + 1):
                    w = P if t < NT else NS
                    c = slice(t * P, t * P + w)
                    v = lambda b: b[0:w, 0:4 * w].rearrange("m (h l) -> m h l", h=4)
                    T_, U_, X_, L_, D_ = v(gT), v(gU), v(gX), v(gL), v(gD)
                    f = lambda b: b[:, 0:2 * w].rearrange("k (p l) -> k p l", p=2)
                    qs, kb, sk = f(g_qs), f(g_kb), f(g_sk)
                    B0_, B1_ = ps[:, 4, :], ps[:, 5, :]
                    gdn.begin(pe, t, "g_tokens")
                    for p in range(2):
                        tr(B0_[0:w, p * P:(p + 1) * P], pj[:, GK + p, c])
                        tr(B0_[0:w, 256 + p * P:256 + (p + 1) * P], pj[:, GV + p, c])
                    for p in range(2):
                        bcast2(B1_[:, p * w:(p + 1) * w], 2 * p, 1, Er[0:NR, c])
                        last = bcast2(B1_[:, 256 + p * w:256 + (p + 1) * w], 2 * p, 1, Vr[0:NR, c])
                    last.then_inc(gdn_s, 1)
                    yield
                    gdn.begin(pe, t, "g_bcast")
                    for q in range(2):
                        for p in range(2):
                            last = mm(B0_[0:w, (2 * q + p) * w:(2 * q + p + 1) * w], pick(2 * p + q, w), Rr[0:NR, c])
                    last.then_inc(gdn_s, 1)
                    yield
                    gdn.begin(pe, t, "g_kk")
                    for q in range(2):
                        for p in range(2):
                            last = mm(ps[0:w, 4 + q, p * w:(p + 1) * w], pj[half(q), GK + p, c], kb[half(q), p, :])
                    last.then_inc(gdn_s, 1)
                    yield
                    gdn.begin(pe, t, "g_first")
                    for h in range(4):
                        last = tr(B0_[0:w, h * w:(h + 1) * w], U_[:, h, :])
                    last.then_inc(gdn_s, 1)
                    yield
                    for n in levels_of(t)[1:]:
                        gdn.begin(pe, t, f"g_x{n}")
                        for h in range(4):
                            last = mm(B0_[0:w, h * w:(h + 1) * w], L_[:, h, :], T_[:, h, :])
                        last.then_inc(gdn_s, 1)
                        yield
                        gdn.begin(pe, t, f"g_y{n}")
                        for h in range(4):
                            mm(B0_[0:w, h * w:(h + 1) * w], U_[:, h, :], X_[:, h, :])
                        for h in range(4):
                            last = mm(B1_[0:w, h * w:(h + 1) * w], X_[:, h, :], U_[:, h, :])
                        last.then_inc(gdn_s, 1)
                        yield
                    gdn.begin(pe, t, "g_qk")
                    for q in range(2):
                        for p in range(2):
                            last = mm(ps[0:w, 4 + q, p * w:(p + 1) * w], pj[half(q), GK + p, c], pj[half(q), GQ + p, c])
                    last.then_inc(gdn_s, 1)
                    yield
                    gdn.begin(pe, t, "g_sk")
                    for q in range(2):
                        for p in range(2):
                            h = 2 * p + q
                            last = mm(B0_[half(q), p * w:(p + 1) * w], g_kn[0:w, h * DK:(h + 1) * DK], U_[:, 2 * q + p, :])
                    last.then_inc(gdn_s, 1)
                    yield
                    gdn.begin(pe, t, "g_u")
                    for q in range(2):
                        for p in range(2):
                            h, x = 2 * p + q, 2 * q + p
                            if t < NT:
                                o = ps[0:w, 4 + q, p * DK:(p + 1) * DK]
                                mm(o, U_[:, x, :], g_vb[0:w, h * DK:(h + 1) * DK], True, False)
                                last = mm(o, sk[half(q), p, :], S_g[half(q), p, :], False, True)
                            else:
                                if (p, q) == (0, 0):
                                    pe.wait_ge(d_q[0], 64)
                                o = ps[half(q), 4 + q, p * w:(p + 1) * w]
                                mm(o, g_vb[0:w, h * DK:(h + 1) * DK], U_[:, x, :], True, False)
                                for b in range(NB):
                                    last = mm(o[:, ND * b:ND * b + ND], Q_g[half(q), p, b, :], sk[half(q), p, ND * b:ND * b + ND],
                                              False, b == NB - 1)
                    last.then_inc(gdn_s, 1)
                    yield
                    if t == NT:
                        gdn.begin(pe, t, "g_ut")
                        for p in range(2):
                            last = tr(B0_[0:w, p * P:(p + 1) * P], g_sk[:, p * w:(p + 1) * w])
                        last.then_inc(gdn_s, 1)
                        yield
                    gdn.begin(pe, t, "g_out")
                    for q in range(2):
                        for p in range(2):
                            h, x = 2 * p + q, 2 * q + p
                            o = ps[half(q), 4 + q, p * w:(p + 1) * w]
                            mm(o, g_u[0:w, h * DK:(h + 1) * DK], D_[:, x, :], True, False)
                            if t < NT:
                                last = mm(o, S_g[half(q), p, :], qs[half(q), p, :], False, True)
                            else:
                                for b in range(NB):
                                    last = mm(o[:, ND * b:ND * b + ND], Q_g[half(q), p, b, :], qs[half(q), p, ND * b:ND * b + ND],
                                              False, b == NB - 1)
                    if t < NT:
                        for h in range(4):
                            last = mm(B0_[half(h % 2), 256 + (h // 2) * DK:256 + (h // 2 + 1) * DK],
                                      g_kd[0:w, h * DK:(h + 1) * DK], g_u[0:w, h * DK:(h + 1) * DK])
                    last.then_inc(gdn_s, 1)
                    yield
                    if t == NT:
                        gdn.begin(pe, t, "g_state")
                        for h in range(4):
                            last = mm(ps[half(h % 2), 4 + h // 2, :], g_kd[0:w, h * DK:(h + 1) * DK],
                                      g_Ue[0:w, h * 512:(h + 1) * 512])
                        last.then_inc(gdn_s, 1)
                        yield

            def rest_pe():
                for t in range(NT + 1):
                    w = P if t < NT else NS
                    c = slice(t * P, t * P + w)
                    f = lambda b: b[:, 0:2 * w].rearrange("k (p l) -> k p l", p=2)
                    v = lambda b: b[0:w, 0:4 * w].rearrange("m (h l) -> m h l", h=4)
                    B0_, B1_ = ps[:, 6, :], ps[:, 7, :]
                    vb = bV if t < NT else bVs(scr)

                    def scores(keys, queries, last=None):
                        for q in range(2):
                            for p in range(2):
                                last = mm(ps[0:w, 6 + q, p * w:(p + 1) * w], keys[half(q), p, :], queries[half(q), p, :])
                        last.then_inc(rest_s, 1)

                    def outputs(kd, vals, at, St, Qt, qs, col, banks=(6, 7)):
                        for q in range(2):
                            for p in range(2):
                                h, x = 2 * p + q, 2 * q + p
                                o = ps[half(q), banks[q], col + p * w:col + (p + 1) * w]
                                mm(o, vals(h), at[:, x, :], True, False)
                                if t < NT:
                                    last = mm(o, St[half(q), p, :], qs[half(q), p, :], False, True)
                                else:
                                    for b in range(NB):
                                        last = mm(o[:, ND * b:ND * b + ND], Qt[half(q), p, b, :],
                                                  qs[half(q), p, ND * b:ND * b + ND], False, b == NB - 1)
                        return last

                    def increments(kd, vals, bank, col):
                        for h in range(4):
                            last = mm(ps[half(h % 2), bank, col + (h // 2) * DK:col + (h // 2 + 1) * DK],
                                      kd[0:w, h * DK:(h + 1) * DK], vals(h))
                        return last

                    def q_increments(kd):
                        for h in range(4):
                            last = mm(ps[half(h % 2), 6 + h // 2, :], kd[0:w, h * DK:(h + 1) * DK],
                                      b_Ue[0:w, h * 512:(h + 1) * 512])
                        last.then_inc(rest_s, 1)

                    rest.begin(pe, t, "h_qk")
                    scores(kg[:, :, c], pj[:, HQ:HQ + 2, c])
                    yield
                    for n in levels_of(t):
                        rest.begin(pe, t, f"h_qk{n}")
                        scores(f(bKl), f(bQl))
                        yield
                    rest.begin(pe, t, "h_tok")
                    for p in range(2):
                        tr(B0_[0:w, p * P:(p + 1) * P], f(bKt)[:, p, :])
                        last = tr(B0_[0:w, 256 + p * P:256 + (p + 1) * P], pj[:, HI + p, c])
                    last.then_inc(rest_s, 1)
                    yield
                    rest.begin(pe, t, "h_out")
                    if t == NT:
                        pe.wait_ge(d_q[1], 64)
                    hv = lambda h: vb[0:w, h * DK:(h + 1) * DK]
                    last = outputs(None, hv, v(bD), S_h, Q_r, f(bQ), 0)
                    if t < NT:
                        last = increments(bKd, hv, 6, 256)
                    last.then_inc(rest_s, 1)
                    yield
                    if t == NT:
                        rest.begin(pe, t, "h_state")
                        q_increments(b_Kd2)
                        yield
                    rest.begin(pe, t, "s_bcast")
                    for g in range(2):
                        for j in range(4):
                            last = mm(ps[0:w, 6 + g, j * w:(j + 1) * w], pick(R_S + 4 * g + j, w), Rr[0:NR, c])
                    last.then_inc(rest_s, 1)
                    yield
                    rest.begin(pe, t, "s_cb")
                    for g in range(2):
                        mm(ps[0:w, 6 + g, 0:w], pj[half(g), SB, c], pj[half(g), SC, c])
                    tr(B0_[0:w, 128:256], pj[:, SB, c])
                    for g in range(2):
                        last = tr(B0_[0:w, 256 + g * P:256 + (g + 1) * P], pj[:, SX + g, c])
                    last.then_inc(rest_s, 1)
                    yield
                    rest.begin(pe, t, "s_e")
                    for j in range(4):
                        last = bcast2(B0_[:, j * w:(j + 1) * w], R_S + j, 4, Er[0:NR, c])
                    last.then_inc(rest_s, 1)
                    yield
                    rest.begin(pe, t, "s_out")
                    if t == NT:
                        pe.wait_ge(d_q[2], 128)
                    att = bD[0:w, 0:8 * w].rearrange("m (h l) -> m h l", h=8)
                    qs = bQ[:, 0:4 * w].rearrange("k (j l) -> k j l", j=4)
                    for g in range(2):
                        for j in range(4):
                            h = 4 * g + j
                            o = ps[32 * j:32 * j + 32, 6 + g, 0:w]
                            mm(o, vb[0:w, h * 32:(h + 1) * 32], att[:, h, :], True, False)
                            if t < NT:
                                last = mm(o, S_s[half(g), j, :], qs[half(g), j, :], False, True)
                            else:
                                for b in range(NB):
                                    last = mm(o[:, ND * b:ND * b + ND], Qs(Q_r)[half(g), j, b, :],
                                              qs[half(g), j, ND * b:ND * b + ND], False, b == NB - 1)
                    if t < NT:
                        for h in range(8):
                            last = mm(B0_[half(h // 4), 256 + (h % 4) * 32:256 + (h % 4 + 1) * 32],
                                      bKd[0:w, h * DK:(h + 1) * DK], vb[0:w, h * 32:(h + 1) * 32])
                    last.then_inc(rest_s, 1)
                    yield
                    if t == NT:
                        rest.begin(pe, t, "s_state")
                        for h in range(8):
                            j = h % 4
                            last = mm(ps[half(h // 4), 6 + j // 2, (j % 2) * 256:(j % 2 + 1) * 256],
                                      b_Kd2[0:w, h * DK:(h + 1) * DK], b_Ue[0:w, h * 256:(h + 1) * 256])
                        last.then_inc(rest_s, 1)
                        yield
                    rest.begin(pe, t, "m_tok")
                    for p in range(2):
                        tr(B0_[0:w, p * P:(p + 1) * P], pj[:, MK + p, c])
                        tr(B0_[0:w, 256 + p * P:256 + (p + 1) * P], pj[:, MV + p, c])
                    for p in range(2):
                        last = bcast2(B1_[:, p * w:(p + 1) * w], R_M + 2 * p, 1, Er[0:NR, c])
                    last.then_inc(rest_s, 1)
                    yield
                    rest.begin(pe, t, "m_bcast")
                    for q in range(2):
                        for p in range(2):
                            last = mm(B0_[0:w, (2 * q + p) * w:(2 * q + p + 1) * w], pick(R_M + 2 * p + q, w), Rr[0:NR, c])
                    last.then_inc(rest_s, 1)
                    yield
                    rest.begin(pe, t, "m_qk")
                    scores(pj[:, MK:MK + 2, c], pj[:, MQ:MQ + 2, c])
                    yield
                    rest.begin(pe, t, "m_out")
                    if t == NT:
                        pe.wait_ge(d_q[3], 128)
                    mv = lambda h: vb[0:w, h * DK:(h + 1) * DK]
                    on = lambda h: ones[0:w, 0:DK]
                    outputs(None, mv, v(bD), S_c, Q_r, f(bQ), 0)
                    outputs(None, on, v(bD), S_n, Q_n, f(bQ), 256).then_inc(rest_s, 1)
                    yield
                    rest.begin(pe, t, "m_den")
                    for p in range(2):
                        last = bcast2(B0_[:, p * w:(p + 1) * w], R_M + 2 * p, 1, Vr[0:NR, c])
                    if t < NT:
                        increments(bKd, mv, 7, 0)
                        last = increments(bKd, on, 7, 128)
                    last.then_inc(rest_s, 1)
                    yield
                    if t == NT:
                        for name in ("m_state", "m_norm"):
                            rest.begin(pe, t, name)
                            q_increments(b_Kd2)
                            yield

            gens = {"g": gdn_pe(), "r": rest_pe()}
            pre.after(pe, 0, "f_g1")
            for chain, t, name, engine in order:
                if engine == "pe":
                    next(gens[chain])

            mid_first(pe, gdn, rest)
            for n in range(4):
                mid.begin(pe, 0, f"o_ss{n}")
                for f in range(2):
                    for h in range(2):
                        last = mm(ps[:, 4 + 2 * f + h, 0:HN], ones if n == 2 else b64, rstd2(scr)[:, f, h * HN:(h + 1) * HN])
                last.then_inc(mid_s, 1)
            mid.begin(pe, 0, "up")
            pe.wait_ge(d_q[4], 32)

            def wbr(n, d):
                return (wb(scr)[:, n, :] if n < WB_A else wb2(pj)[:, n - WB_A, :]), d

            def gate_tile(slot, e, par, d, tile, last_of_slot):
                n = 2 * par + e
                if tile is not None:
                    pe.wait_ge(tile_read, tile)
                gemm_tile(2 * e, [ring[:, slot, k * 256 + e * P:k * 256 + (e + 1) * P] for k in range(KD)], hs, tile_done)
                if last_of_slot:
                    pe.drain().then_inc(w_used, 1)
                for h in range(2):
                    for kk in range(2):
                        src, _ = wbr(2 * n + kk, d)
                        last = mm(ps[:, 4 + 2 * e + h, 0:HN], src[:, d * P:(d + 1) * P], pj[:, BR[2 * n + kk], h * HN:(h + 1) * HN],
                                  kk == 0, kk == 1)
                last.then_inc(lin_done, 1)

            for d in range(KD):
                for par in range(2):
                    n = first["gate"] + 2 * d + par
                    landed(pe, n % R, n)
                    for e in range(2):
                        tile = 4 * d + 2 * par + e
                        if tile >= 2:
                            pe.wait_ge(lin_read, tile - 1)
                        gate_tile(n % R, e, par, d, 30 + tile - 1 if tile >= 2 else None, e == 1)
            pe.drain().then_inc(mid_s, 1)

            mid.begin(pe, 0, "wout")
            ms = [merged_t(pj, k) for k in range(KD)]

            def wout(slot, idx, n):
                landed(pe, slot, n)
                for c in range(2):
                    if idx >= 1:
                        pe.wait_ge(tile_read, tiles_before["wout"] + 2 * idx + c - 1)
                    gemm_tile(2 * c, [ring[:, slot, k * 256 + c * P:k * 256 + (c + 1) * P] for k in range(KD)], ms, tile_done)
                pe.drain().then_inc(w_used, 1)
            for idx in range(counts["wout"]):
                n = first["wout"] + idx
                wout(n % R, idx, n)
            pe.drain().then_inc(mid_s, 1)
            sumsq(mid, "ss2", hs, ones)
            mid.begin(pe, 0, "ffa")

            def ffa(slot, idx, n, par):
                landed(pe, slot, n)
                if not isinstance(idx, int) or idx >= 2:
                    pe.wait_ge(tile_read, idx + (tiles_before["ffa"] - 1))
                    pe.wait_ge(lin_read, idx + (32 - 1))
                gemm_tile(2 * par, [ring[:, slot, k * 256:k * 256 + P] for k in range(KD)], hs, tile_done)
                gemm_tile(4 + 2 * par, [ring[:, slot, k * 256 + P:k * 256 + 2 * P] for k in range(KD)], hs, lin_done)
                pe.drain().then_inc(w_used, 1)
            for idx in range(2):
                n = first["ffa"] + idx
                ffa(n % R, idx, n, idx % 2)
            with pe.Fori(0, 5) as i:
                for r in range(R):
                    ffa((first["ffa"] + 2 + r) % R, i * R + (2 + r), i * R + (first["ffa"] + 2 + r), r % 2)
            pe.drain().then_inc(mid_s, 1)

            mid.begin(pe, 0, "ffb")

            def ffb(d, n, par, first_tile):
                if not first_tile:
                    pe.wait_ge(tile_read, d + (tiles_before["ffb"] - 1))
                for e in range(2):
                    slot = (first["ffb"] + 2 * par + e) % R
                    landed(pe, slot, n + e)
                    for h in range(2):
                        for k in range(11):
                            last = mm(ps[:, 2 * par + h, 0:HN], ring[:, slot, k * P:(k + 1) * P],
                                      pj[:, 8 + 11 * e + k, h * HN:(h + 1) * HN], e == 0 and k == 0, e == 1 and k == 10)
                    if e == 1:
                        last.then_inc(tile_done, 1)
                    pe.drain().then_inc(w_used, 1)
            for d in range(2):
                ffb(d, first["ffb"] + 2 * d, d % 2, True)
            with pe.Fori(0, 3) as i:
                for r in range(2):
                    ffb(i * 2 + (2 + r), i * 4 + (first["ffb"] + 4 + 2 * r), r, False)
            pe.drain().then_inc(mid_s, 1)
            sumsq(mid, "ss3", hs, ones)
            for t in range(NT + 1):
                w = P if t < NT else NS
                mid.begin(pe, 0, f"y{t}")
                for k in range(KD):
                    last = tr(ps[0:w, k // 4, (k % 4) * P:(k % 4 + 1) * P], hT[:, k, t * P:t * P + w])
                last.then_inc(mid_s, 1)

        @block.scalar
        def _(act):
            pre.begin(act, 0, "silc")
            act.wait_ge(d_c, 32)
            act.activation(ctok(pj)[0:NB + 1, :], ctok(pj)[0:NB + 1, :], ACT.Silu).then_inc(pre_s, 1)
            for d in range(KD):
                pre.begin(act, 0, f"xc{d}")
                act.activation(xT[:, d, 0:T], ps[:, 0, :], ACT.Copy)
                act.activation(xT[:, d, T:TA], ps[:, 1, 0:NS], ACT.Copy)
                act.drain().then_inc(pre_s, 1)

            def rsqrt(chain, name, dst, src, scale):
                chain.begin(act, 0, name)
                act.wait_ge(zeroed, 2)
                act.activation(dst, src, ACT.Ln, scale=scale, bias=colp[:, 3:4])
                act.drain()
                act.activation(dst, dst, ACT.Exp, scale=-0.5)
                act.drain().then_inc(chain.sem, 1)

            two = lambda b: b.rearrange("p (h n) -> p h n", h=2)
            rsqrt(pre, "rs1", two(rstd[:, :]), ps[:, 4:6, 0:HN], 1.0 / D)

            def projc(i, c):
                act.wait_ge(tile_done, i * 2 + (c + 1))
                act.activation(pj[:, bass.ds(i * 2 + c, 1), :].rearrange("p o (h n) -> p (o h) n", h=2),
                               ps[:, 2 * c:2 * c + 2, 0:HN], ACT.Copy).then_inc(tile_read, 1)
            with act.Fori(0, 15) as i:
                for c in range(2):
                    projc(i, c)
            pre.begin(act, 0, "projc")
            act.drain().then_inc(pre_s, 1)
            for n, f in enumerate(CONV):
                pre.begin(act, 0, f"silu{n}")
                act.activation(pj[:, f, :], part(2048 + 544 * (n % 2), TA), ACT.Silu)
                if n == 0:
                    for m in (HQ, HQ + 1, GZ, GZ + 1, HG, HG + 1, SZ, SZ + 1):
                        act.activation(pj[:, m, :], pj[:, m, :], ACT.Silu)
                    for m in (MO, MO + 1):
                        act.activation(pj[:, m, :], pj[:, m, :], ACT.Sigmoid)
                    for m in range(2):
                        act.activation(kg[:, m, :], pj[:, HF + m, :], ACT.Sigmoid, scale=-1.0)
                act.drain().then_inc(pre_s, 1)
            for name, f0 in (("l2ra", 0), ("l2rb", 2)):
                pre.begin(act, 0, name)
                for f in range(2):
                    act.activation(two(part(2176 + 544 * (f0 + f), TA)), ps[:, 4 + 2 * f:6 + 2 * f, 0:HN], ACT.Ln, bias=colp[:, 3:4])
                    act.drain()
                for f in range(2):
                    x = part(2176 + 544 * (f0 + f), TA)
                    act.activation(x, x, ACT.Exp, scale=-0.5)
                act.drain().then_inc(pre_s, 1)
            pre.begin(act, 0, "rabs")
            act.wait_ge(d_row, 96)
            z, e, ln = (rowbuf(scr, n) for n in range(3))
            act.activation(e, z, ACT.Abs)
            act.activation(colp[0:NR, 1:2], colp[0:NR, 1:2], ACT.Exp)
            act.drain()
            act.activation(e, e, ACT.Exp, scale=-1.0)
            act.drain().then_inc(pre_s, 1)
            pre.begin(act, 0, "rln")
            act.activation(ln, e, ACT.Ln, bias=1.0)
            act.activation(two(Vr[0:32, :]), ps[0:32, 2:4, 0:HN], ACT.Sigmoid)
            act.drain().then_inc(pre_s, 1)
            pre.begin(act, 0, "rexp")
            act.activation(Er[0:NR, :], Er[0:NR, :], ACT.Exp)
            act.activation(RK(scr)[0:NR, :], RK(scr)[0:NR, :], ACT.Exp)
            act.activation(Vr[R_M:NR, :], MTr[R_M:NR, :], ACT.Exp, scale=-1.0)
            act.drain().then_inc(pre_s, 1)
            pre.begin(act, 0, "lb1")
            act.activation(hrow[0:1, 0:256], hrow[0:1, 0:256], ACT.Exp)
            act.drain().then_inc(pre_s, 1)
            pre.begin(act, 0, "lb5")
            act.activation(hcol[:, :, 3:5], hcol[:, :, 3:5], ACT.Ln).then_inc(pre_s, 1)
            for f in range(2):
                a_, b_ = part(544 * 2 * f, TA), part(544 * (2 * f + 1), TA)
                pre.begin(act, 0, f"f_ls{f}")
                act.activation(a_, pj[:, HF + f, :], ACT.Abs)
                act.drain()
                act.activation(a_, a_, ACT.Exp, scale=-1.0)
                act.drain()
                act.activation(a_, a_, ACT.Ln, bias=1.0)
                act.drain().then_inc(pre_s, 1)
                pre.begin(act, 0, f"f_ln{f}")
                act.activation(b_, b_, ACT.Abs)
                act.drain()
                act.activation(b_, b_, ACT.Exp, scale=-1.0)
                act.drain()
                act.activation(b_, b_, ACT.Ln, bias=1.0)
                act.drain().then_inc(pre_s, 1)

            def gdn_act():
                for t in range(NT + 1):
                    w = P if t < NT else NS
                    gdn.begin(act, t, "g_decay")
                    act.activation(gD[0:w, 0:4 * w], gD[0:w, 0:4 * w], ACT.Exp).then_inc(gdn_s, 1)
                    yield
                    gdn.begin(act, t, "g_t1")
                    act.activation(gT[0:w, 0:4 * w], ps[0:w, 4, 0:4 * w], ACT.Copy).then_inc(gdn_s, 1)
                    yield
                    for n in levels_of(t)[1:]:
                        gdn.begin(act, t, f"g_xc{n}")
                        act.activation(gX[0:w, 0:4 * w], ps[0:w, 4, 0:4 * w], ACT.Copy).then_inc(gdn_s, 1)
                        yield
                    gdn.begin(act, t, "g_skc")
                    act.activation(g_sk[:, 0:2 * w], ps[:, 4, 0:2 * w], ACT.Copy).then_inc(gdn_s, 1)
                    yield

            def rest_act():
                for t in range(NT + 1):
                    w = P if t < NT else NS
                    for n in levels_of(t):
                        rest.begin(act, t, f"h_dec{n}")
                        act.activation(bEf[:, 0:2 * w], bEf[:, 0:2 * w], ACT.Abs)
                        act.drain()
                        act.activation(bEf[:, 0:2 * w], bEf[:, 0:2 * w], ACT.Exp, scale=-1.0).then_inc(rest_s, 1)
                        yield
                    rest.begin(act, t, "h_dec")
                    act.activation(bQ[:, 0:2 * w].rearrange("k (p l) -> k p l", p=2), pj[:, HF:HF + 2, t * P:t * P + w], ACT.Exp)
                    act.activation(bEf[:, 0:2 * w], bEf[:, 0:2 * w], ACT.Exp)
                    act.drain().then_inc(rest_s, 1)
                    yield
                    rest.begin(act, t, "s_decay")
                    act.activation(bD[0:w, 0:8 * w], bD[0:w, 0:8 * w], ACT.Exp).then_inc(rest_s, 1)
                    yield
                    rest.begin(act, t, "m_decay")
                    act.activation(bD[0:w, 0:4 * w], bD[0:w, 0:4 * w], ACT.Exp).then_inc(rest_s, 1)
                    yield

            gens = {"g": gdn_act(), "r": rest_act()}
            for chain, t, name, engine in order:
                if engine == "act":
                    next(gens[chain])
            for n in range(4):
                mid.begin(act, 0, f"o_rs{n}")
                for f in range(2):
                    act.activation(two(rstd2(scr)[:, f, :]), ps[:, 4 + 2 * f:6 + 2 * f, 0:HN], ACT.Ln,
                                   scale=1.0 / (P if n == 2 else DK), bias=colp[:, 3:4])
                act.drain()
                for f in range(2):
                    act.activation(rstd2(scr)[:, f, :], rstd2(scr)[:, f, :], ACT.Exp, scale=-0.5)
                act.drain().then_inc(mid_s, 1)

            def gate(i, e):
                act.wait_ge(tile_done, i * 2 + (tiles_before["gate"] + e + 1))
                act.wait_ge(lin_read, i * 2 + (e - 1))
                act.activation(two(gbuf(pj)[:, e, :]), ps[:, 2 * e:2 * e + 2, 0:HN], ACT.Sigmoid).then_inc(tile_read, 1)
            for e in range(2):
                act.wait_ge(tile_done, tiles_before["gate"] + e + 1)
                act.activation(two(gbuf(pj)[:, e, :]), ps[:, 2 * e:2 * e + 2, 0:HN], ACT.Sigmoid).then_inc(tile_read, 1)
            with act.Fori(1, 16) as i:
                for e in range(2):
                    gate(i, e)
            rsqrt(mid, "rs2", two(rstd[:, :]), ps[:, 4:6, 0:HN], 1.0 / D)

            def ff_silu(i, e):
                act.wait_ge(tile_done, i * 2 + (tiles_before["ffa"] + e + 1))
                act.wait_ge(lin_read, i * 2 + (32 + e - 1))
                act.activation(two(fbuf(scr)[:, e, :]), ps[:, 2 * e:2 * e + 2, 0:HN], ACT.Silu).then_inc(tile_read, 1)
            with act.Fori(0, 11) as i:
                for e in range(2):
                    ff_silu(i, e)
            rsqrt(mid, "rs3", two(rstd[:, :]), ps[:, 4:6, 0:HN], 1.0 / D)
            for t in range(NT + 1):
                w = P if t < NT else NS
                mid.begin(act, 0, f"yc{t}")
                for h in range(2):
                    act.activation(ytok(pj, t)[:, h * 512:(h + 1) * 512], ps[0:w, h, :], ACT.Copy)
                act.drain().then_inc(mid_s, 1)

        @block.vector
        def _(dve):
            MUL, ADD, SUB = ALU.mult, ALU.add, ALU.subtract

            def tt(out, a, b, op):
                r = dve.tensor_tensor(out, a, b, op)
                dve.drain()
                return r

            def ts(out, a, s1, s2, op0, op1=None):
                r = dve.tensor_scalar(out, a, s1, s2, op0, *([op1] if op1 is not None else []))
                dve.drain()
                return r

            def stt(out, a, s, b, op0, op1):
                r = dve.scalar_tensor_tensor(out=out, in0=a, scalar=s, in1=b, op0=op0, op1=op1)
                dve.drain()
                return r

            def cp(out, a):
                r = dve.tensor_copy(out, a)
                dve.drain()
                return r

            def done(chain):
                dve.drain().then_inc(chain.sem, 1)

            dve.wait_ge(zeroed, 1)
            dve.memset(colp[:, 3:4], EPS)
            for b in (MTr, Vr):
                dve.memset(b[:, :], 0.0)
            dve.memset(hrow[64:96, :], 0.0)
            dve.drain().then_inc(zeroed, 1)
            pre.begin(dve, 0, "vecc")
            cp(vt[:, :], ps[:, 4, 0:V_2])
            done(pre)
            pre.begin(dve, 0, "ctc")
            cp(cT[:, :, :].rearrange("p k b -> p (k b)"), ps[:, 5, 0:KD * (NB + 1)])
            done(pre)

            def squares(chain, name):
                chain.begin(dve, 0, name)
                for k in range(KD):
                    dve.tensor_tensor(hT[:, k, :], xT[:, k, :], xT[:, k, :], MUL)
                done(chain)

            squares(pre, "sq1")
            def modulation(name, c0, c1):
                pre.begin(dve, 0, name)
                tt(mod[:, c0:c1, :], ps[:, 7, c0 * 9:c1 * 9].rearrange("p (c b) -> p c b", b=9),
                   vt[:, V_ADAB + c0:V_ADAB + c1].unsqueeze(2).to_broadcast([P, c1 - c0, 9]), ADD)
                done(pre)

            modulation("mod1", 0, 16)

            def modulate(chain, name, w0, c0):
                chain.begin(dve, 0, name)
                ts(coef[:, :, :], mod[:, c0 + KD:c0 + 2 * KD, :], 1.0, None, ADD)
                tt(coef[:, :, :], coef[:, :, :], vt[:, w0:w0 + KD].unsqueeze(2).to_broadcast([P, KD, 9]), MUL)
                for k in range(KD):
                    dve.tensor_tensor(hT[:, k, :], xT[:, k, :], rstd[:, :], MUL)
                dve.drain()
                for k in range(KD):
                    s = hT[:, k, T:TA].rearrange("p (b t) -> p b t", t=ND)
                    sc = coef[:, k, 1:9].unsqueeze(2).to_broadcast([P, NB, ND])
                    sh = mod[:, c0 + k, 1:9].unsqueeze(2).to_broadcast([P, NB, ND])
                    dve.tensor_scalar(hT[:, k, 0:T], hT[:, k, 0:T], coef[:, k, 0:1], mod[:, c0 + k, 0:1], MUL, ADD)
                    tt(s, s, sc, MUL)
                    dve.tensor_tensor(s, s, sh, ADD)
                done(chain)

            modulate(pre, "norm1", V_N1, 0)
            modulation("mod2", 16, 48)

            sp7 = spad(scr)
            pre.begin(dve, 0, "hist")
            cp(sp7[:, :, :, 0:3], ps[:, 6, 0:240].rearrange("p (f b k) -> p f b k", f=10, k=3))
            for n, f in enumerate(CONV):
                dve.tensor_copy(sp7[:, n, :, 3:7], pj[:, f, T:TA].rearrange("p (b t) -> p b t", t=ND))
            done(pre)
            pre.begin(dve, 0, "tailc")
            for n in range(3):
                wd = 512 if n < 2 else 256
                dve.tensor_copy(tail(scr)[:, n * 512:n * 512 + wd], ps[0:2 * NS, 4 + n, 0:wd])
            done(pre)
            for n, f in enumerate(CONV):
                pre.begin(dve, 0, f"conv{n}")
                acc = part(2048 + 544 * (n % 2), TA)
                if n < 6:
                    w_ = [vt[:, V_GCW + k * 6 + n:V_GCW + k * 6 + n + 1] for k in range(4)]
                    b_ = vt[:, V_GCB + n:V_GCB + n + 1]
                else:
                    w_ = [vt[:, V_SCW + k * 4 + n - 6:V_SCW + k * 4 + n - 5] for k in range(4)]
                    b_ = vt[:, V_SCB + n - 6:V_SCB + n - 5]
                sa = acc[:, T:TA].rearrange("p (b t) -> p b t", t=ND)
                dve.tensor_scalar(acc[:, 0:T], pj[:, f, 0:T], w_[3], b_, MUL, ADD)
                ts(sa, sp7[:, n, :, 3:7], w_[3], b_, MUL, ADD)
                for k in (2, 1, 0):
                    d = 3 - k
                    dve.scalar_tensor_tensor(out=acc[:, d:T], in0=pj[:, f, 0:T - d], scalar=w_[k], in1=acc[:, d:T], op0=MUL, op1=ADD)
                    stt(sa, sp7[:, n, :, k:k + 4], w_[k], sa, MUL, ADD)
                done(pre)
            pre.begin(dve, 0, "l2sq")
            for n, f in enumerate((GQ, GQ + 1, GK, GK + 1)):
                dve.tensor_tensor(part(544 * n, TA), pj[:, f, :], pj[:, f, :], MUL)
            done(pre)
            pre.begin(dve, 0, "l2m")
            for n, f in enumerate((GQ, GQ + 1, GK, GK + 1)):
                dve.scalar_tensor_tensor(out=pj[:, f, :], in0=pj[:, f, :], scalar=DK ** -0.5 if n < 2 else 1.0,
                                         in1=part(2176 + 544 * n, TA), op0=MUL, op1=MUL)
            done(pre)

            z, e, ln, t1, t2 = (rowbuf(scr, n) for n in range(5))
            rs, rk, rn = RS(scr), RK(scr), RN(scr)
            two = lambda b: b.rearrange("p (h n) -> p h n", h=2)
            pre.begin(dve, 0, "rz")
            dve.wait_ge(d_row, 96)
            dve.wait_ge(d_st, 16)
            ts(two(z), ps[0:NR, 0:2, 0:HN], colp[0:NR, 0:1], cst[0:NR, K_SGN:K_SGN + 1], ADD, MUL)
            done(pre)
            pre.begin(dve, 0, "rsp")
            dve.wait_ge(stored, 18 * 16)
            ts(t1, e, 1.0, 1.0, ADD, SUB)
            tt(t1, e, t1, SUB)
            tt(ln, ln, t1, ADD)
            stt(z, z, 0.0, ln, ALU.max, ADD)
            cp(Vr[32:64, :], z[32:64, :])
            ts(colp[0:NR, 1:2], colp[0:NR, 1:2], -1.0, None, MUL)
            ts(t1, z, colp[0:NR, 1:2], None, MUL)
            dve.tensor_tensor_scan(Rr[0:NR, :], cst[0:NR, K_RST:K_RST + TA], t1, 0.0, MUL, ADD)
            dve.drain()
            m4 = slice(R_M, R_M + 4)
            iv = t2
            ts(two(iv[R_M:NR, :]), ps[R_M:NR, 2:4, 0:HN], colp[R_M:NR, 2:3], None, ADD)
            dve.tensor_tensor_scan(MTr[m4, 0:T], t1[m4, 0:T], iv[m4, 0:T], 0.0, ADD, ALU.max)
            dve.drain()
            isq = MTs(hrow)[m4, 0:40].rearrange("p (b t) -> p b t", t=5)
            fsq = MTs(hrow)[m4, 40:80].rearrange("p (b t) -> p b t", t=5)
            osq = MTs(hrow)[m4, 80:120]
            cp(isq[:, :, 1:5], iv[m4, T:TA].rearrange("p (b t) -> p b t", t=ND))
            dve.memset(fsq, -BIG)
            dve.drain()
            cp(fsq[:, :, 1:5], t1[m4, T:TA].rearrange("p (b t) -> p b t", t=ND))
            dve.tensor_tensor_scan(osq, MTs(hrow)[m4, 40:80], MTs(hrow)[m4, 0:40], 0.0, ADD, ALU.max)
            dve.drain()
            cp(MTr[m4, T:TA].rearrange("p (b t) -> p b t", t=ND), osq.rearrange("p (b t) -> p b t", t=5)[:, :, 1:5])
            mp = ln
            dve.memset(mp, 0.0)
            dve.drain()
            for t in range(1, NT):
                cp(mp[m4, t * P:(t + 1) * P], MTr[m4, t * P - 1:t * P].to_broadcast([4, P]))
            cp(mp[m4, T:TA].rearrange("p (b t) -> p b t", t=ND), isq[:, :, 0:1].to_broadcast([4, NB, ND]))
            cp(rs[0:NR, :], Rr[0:NR, :])
            tt(rs[m4, :], Rr[m4, :], iv[m4, :], SUB)
            tt(Rr[m4, :], Rr[m4, :], MTr[m4, :], SUB)
            tt(Er[0:NR, :], Rr[0:NR, :], mp, ADD)
            for c0, n, l in ((0, NT, P), (T, NB, ND)):
                v = lambda b: b[0:NR, c0:c0 + n * l].rearrange("p (n l) -> p n l", l=l)
                tt(v(rk), v(Rr)[:, :, l - 1:l].to_broadcast([NR, n, l]), v(rs), SUB)
            done(pre)
            pre.begin(dve, 0, "rv")
            ts(Vr[R_M:NR, :], Vr[R_M:NR, :], 1e38, None, ALU.min)
            stt(rn[0:NR, :], Vr[0:NR, :], -1.0, Er[0:NR, :], MUL, MUL)
            done(pre)
            pre.begin(dve, 0, "rcolc")
            for t in range(NT + 1):
                w = P if t < NT else NS
                for r0, c0, n in ((R_G, T_G, 4), (R_S, T_S, 8), (R_M, T_M, 4)):
                    dve.tensor_copy(cols[0:w, t, :, c0:c0 + n], ps[0:w, 3 + t, 0:4 * NR].rearrange("p (k r) -> p k r", k=4)[:, :, r0:r0 + n])
            done(pre)

            pre.begin(dve, 0, "lb0")
            tt(hrow[0:1, 0:256], hrow[0:1, 0:256], hrow[0:1, 0:256], SUB)
            cp(hrow2(scr)[0:1, 0:256].rearrange("o (h v) -> o h v", v=32), hrow[0:1, 256:264].unsqueeze(2).to_broadcast([1, 8, 32]))
            done(pre)
            pre.begin(dve, 0, "lb2")
            dve.reciprocal(hrow2(scr)[0:1, 256:512], hrow[0:1, 0:256])
            dve.drain()
            tt(hrow[0:1, 0:256], hrow[0:1, 0:256], hrow2(scr)[0:1, 256:512], MUL)
            tt(hrow[0:1, 0:256], hrow[0:1, 0:256], hrow[0:1, 0:256], SUB)
            done(pre)
            pre.begin(dve, 0, "lb4")
            lbc = hcol[:, :, 0]
            cp(lbc, ps[:, 4, 0:2])
            cp(dcol[:, :], ps[:, 4, 2:4])
            ts(hcol[:, :, 1], lbc, -1.0, 1.0, MUL, ADD)
            ts(hcol[:, :, 2], lbc, 0.0, None, ALU.is_gt)
            ts(hcol[:, :, 3], lbc, 2.0 ** -60, None, ALU.max)
            ts(hcol[:, :, 4], hcol[:, :, 1], 2.0 ** -60, None, ALU.max)
            done(pre)
            pre.begin(dve, 0, "lb6")
            tt(hcol[:, :, 3], hcol[:, :, 3], hcol[:, :, 2], MUL)
            ts(hcol[:, :, 5], hcol[:, :, 2], BIG, -BIG, MUL, ADD)
            tt(hcol[:, :, 3], hcol[:, :, 3], hcol[:, :, 5], ADD)
            for f in range(2):
                dve.tensor_scalar(kg[:, f, :], kg[:, f, :], hcol[:, f, 1:2], None, MUL)
            done(pre)
            for f in range(2):
                a_, b_ = part(544 * 2 * f, TA), part(544 * (2 * f + 1), TA)
                fz = pj[:, HF + f, :]
                pre.begin(dve, 0, f"f_b{f}")
                stt(a_, fz, 0.0, a_, ALU.min, SUB)
                ts(a_, a_, hcol[:, f, 4:5], None, ADD)
                ts(b_, a_, hcol[:, f, 3:4], None, SUB)
                done(pre)
                pre.begin(dve, 0, f"f_g{f}")
                ts(a_, a_, hcol[:, f, 3:4], None, ALU.max)
                tt(a_, a_, b_, ADD)
                dve.tensor_tensor_scan(pj[:, HF + f, :], cst[:, K_RST:K_RST + TA], a_, 0.0, MUL, ADD)
                done(pre)

            def col(t, kind, row, n, w, width):
                return cols[0:w, t, kind, row:row + n].unsqueeze(2).to_broadcast([w, n, width])

            def half(q):
                return slice(q * DK, (q + 1) * DK)

            def decays(t, w, D_, bank, row, chain):
                for q in range(2):
                    dve.tensor_tensor(D_[:, 2 * q:2 * q + 2, :], ps[0:w, bank, 2 * q * w:(2 * q + 2) * w].rearrange("m (p l) -> m p l", p=2),
                                      cols[0:w, t, 0, row + q:row + q + 3:2].unsqueeze(2).to_broadcast([w, 2, w]), SUB)
                dve.drain()
                dve.tensor_tensor(D_, D_, neg(t).unsqueeze(1).to_broadcast([w, 4, w]), ADD).then_inc(chain.sem, 1)

            def keep_last(dst, src, t, w, n):
                if t < NT:
                    dve.tensor_copy(dst[:, 0:n, 0:1], src[:, :, w - 1:w])
                else:
                    dve.tensor_copy(dst[:, 0:n, :], src[:, :, ND - 1:w:ND])

            def spread(dst, src, n, v):
                own = cst[0:NS, K_OWN:K_OWN + NB].unsqueeze(2).to_broadcast([NS, NB, v])
                for h in range(n):
                    dve.tensor_tensor(dst[0:NS, h * NB * v:(h + 1) * NB * v].rearrange("m (b v) -> m b v", b=NB),
                                      src(h).unsqueeze(1).to_broadcast([NS, NB, v]), own, MUL)

            def grow(S, e, inc, shape, chain):
                tt(S, S, e, MUL)
                dve.tensor_tensor(S, S, inc, ADD)

            def gdn_dve():
                for t in range(NT + 1):
                    w = P if t < NT else NS
                    c = slice(t * P, t * P + w)
                    v = lambda b: b[0:w, 0:4 * w].rearrange("m (h l) -> m h l", h=4)
                    U_, L_, D_, A_ = v(gU), v(gL), v(gD), v(gAt)
                    f = lambda b: b[:, 0:2 * w].rearrange("k (p l) -> k p l", p=2)
                    tok = lambda b: b[0:w, 0:256].rearrange("m (h v) -> m h v", h=4)
                    m4_ = lambda n: mask(n, w).unsqueeze(1).to_broadcast([w, 4, w])
                    gdn.begin(dve, t, "g_scale")
                    ktok, vtok = (ps[0:w, 4, o:o + 256].rearrange("m (h v) -> m h v", h=4) for o in (0, 256))
                    dve.tensor_tensor(tok(g_vb), vtok, col(t, 2, T_G, 4, w, DK), MUL)
                    dve.tensor_tensor(tok(g_kn), ktok, col(t, 3, T_G, 4, w, DK), MUL)
                    dve.tensor_tensor(tok(g_kd), ktok, col(t, 1, T_G, 4, w, DK), MUL)
                    Eb = ps[:, 5, 0:2 * w].rearrange("k (p l) -> k p l", p=2)
                    Bb = ps[:, 5, 256:256 + 2 * w].rearrange("k (p l) -> k p l", p=2)
                    dve.tensor_tensor(f(g_qs), pj[:, GQ:GQ + 2, c], Eb, MUL)
                    keep_last(eG, Eb, t, w, 2)
                    dve.tensor_tensor(f(g_kb), pj[:, GK:GK + 2, c], Bb, MUL)
                    done(gdn)
                    yield
                    gdn.begin(dve, t, "g_diff")
                    decays(t, w, D_, 4, T_G, gdn)
                    yield
                    gdn.begin(dve, t, "g_lower")
                    tt(gAt[0:w, 0:4 * w].rearrange("m (q x) -> m q x", q=2), ps[0:w, 4:6, 0:2 * w],
                       gD[0:w, 0:4 * w].rearrange("m (q x) -> m q x", q=2), MUL)
                    dve.tensor_tensor(U_, A_, m4_(0), MUL)
                    tt(L_, A_, m4_(1), MUL)
                    tt(U_, ident[0:w, 0:w].unsqueeze(1).to_broadcast([w, 4, w]), U_, SUB)
                    done(gdn)
                    yield
                    lv = levels_of(t)
                    for n in lv[1:]:
                        gdn.begin(dve, t, f"g_upd{n}")
                        dve.tensor_tensor(gU[0:w, 0:4 * w], gU[0:w, 0:4 * w], ps[0:w, 5, 0:4 * w], SUB)
                        if n != lv[-1]:
                            dve.tensor_tensor(gT[0:w, 0:4 * w], gT[0:w, 0:4 * w], ps[0:w, 4, 0:4 * w], SUB)
                            dve.tensor_tensor(L_, A_, m4_(n + 1), MUL)
                        done(gdn)
                        yield
                    gdn.begin(dve, t, "g_aq")
                    D2 = gD[0:w, 0:4 * w].rearrange("m (q x) -> m q x", q=2)
                    dve.tensor_tensor(D2, ps[0:w, 4:6, 0:2 * w], D2, MUL).then_inc(gdn_s, 1)
                    yield
                    gdn.begin(dve, t, "g_uc")
                    if t < NT:
                        ut = g_u[0:w, 0:256].rearrange("m (p q v) -> m q p v", p=2, q=2)
                        for q in range(2):
                            dve.tensor_copy(ut[:, q], ps[0:w, 4 + q, 0:2 * DK].rearrange("m (p v) -> m p v", p=2))
                        done(gdn)
                        yield
                    else:
                        for q in range(2):
                            dve.tensor_copy(g_sk[half(q), 0:2 * w], ps[half(q), 4 + q, 0:2 * w])
                        done(gdn)
                        yield
                        gdn.begin(dve, t, "g_utc")
                        cp(g_u[0:w, 0:256], ps[0:w, 4, 0:256])
                        spread(g_Ue, lambda h: g_u[0:w, h * DK:(h + 1) * DK], 4, DK)
                        done(gdn)
                        yield
                    gdn.begin(dve, t, "g_outc")
                    for q in range(2):
                        dve.tensor_copy(pj[half(q), GV:GV + 2, c], ps[half(q), 4 + q, 0:2 * w].rearrange("k (p l) -> k p l", p=2))
                    if t < NT:
                        grow(S_g[:, :, :], eG[:, :, 0:1].to_broadcast([P, 2, DK]),
                             ps[:, 4, 256:256 + 2 * DK].rearrange("k (p v) -> k p v", p=2), None, gdn)
                        done(gdn)
                        yield
                    else:
                        done(gdn)
                        yield
                        gdn.begin(dve, t, "g_statec")
                        grow(Q_g[:, :, :, :], eG[:, :, :].unsqueeze(3).to_broadcast([P, 2, NB, DK]),
                             ps[:, 4:6, :].rearrange("k p (b v) -> k p b v", b=NB), None, gdn)
                        done(gdn)
                        yield

            def rest_dve():
                for t in range(NT + 1):
                    w = P if t < NT else NS
                    c = slice(t * P, t * P + w)
                    v = lambda b: b[0:w, 0:4 * w].rearrange("m (h l) -> m h l", h=4)
                    f = lambda b: b[:, 0:2 * w].rearrange("k (p l) -> k p l", p=2)
                    hv = lambda b: b[0:w, 0:4 * w].rearrange("m (q x) -> m q x", q=2)
                    tok = lambda b: b[0:w, 0:256].rearrange("m (h v) -> m h v", h=4)
                    D_ = v(bD)
                    kdb = bKd if t < NT else b_Kd2[:, :]
                    vb = bV if t < NT else bVs(scr)
                    g = pj[:, HF:HF + 2, c]

                    def level_diff(n):
                        s = LEVELS[n]
                        for p in range(2):
                            x = g[:, p, :].rearrange("k (b i) -> k b i", i=2 * s)
                            dve.tensor_tensor(f(bEf)[:, p, :].rearrange("k (b i) -> k b i", i=2 * s), x,
                                              x[:, :, s - 1:s].to_broadcast([P, w // (2 * s), 2 * s]), SUB)

                    rest.begin(dve, t, "h_diag")
                    for q in range(2):
                        dve.tensor_tensor(D_[:, 2 * q:2 * q + 2, :], ps[0:w, 6 + q, 0:2 * w].rearrange("m (p l) -> m p l", p=2),
                                          ident[0:w, 0:w].unsqueeze(1).to_broadcast([w, 2, w]), MUL)
                    level_diff(0)
                    done(rest)
                    yield
                    for n in levels_of(t):
                        rest.begin(dve, t, f"h_sc{n}")
                        dve.tensor_tensor(f(bQl), pj[:, HQ:HQ + 2, c], f(bEf), MUL)
                        dve.tensor_tensor(f(bKl), kg[:, :, c], f(bEf), MUL)
                        done(rest)
                        yield
                        rest.begin(dve, t, f"h_add{n}")
                        X_ = v(bX)
                        for q in range(2):
                            dve.tensor_tensor(X_[:, 2 * q:2 * q + 2, :], ps[0:w, 6 + q, 0:2 * w].rearrange("m (p l) -> m p l", p=2),
                                              mask(n, w).unsqueeze(1).to_broadcast([w, 2, w]), MUL)
                        if n != levels_of(t)[-1]:
                            level_diff(n + 1)
                        else:
                            for p in range(2):
                                if t < NT:
                                    dve.tensor_tensor(f(bEf)[:, p, :], g[:, p, w - 1:w].to_broadcast([P, w]), g[:, p, :], SUB)
                                else:
                                    x = g[:, p, :].rearrange("k (b i) -> k b i", i=ND)
                                    dve.tensor_tensor(f(bEf)[:, p, :].rearrange("k (b i) -> k b i", i=ND),
                                                      x[:, :, ND - 1:ND].to_broadcast([P, NB, ND]), x, SUB)
                        dve.drain()
                        dve.tensor_tensor(D_, D_, X_, ADD)
                        done(rest)
                        yield
                    rest.begin(dve, t, "h_kd")
                    dve.tensor_tensor(f(bKt), kg[:, :, c], f(bEf), MUL)
                    keep_last(eR, f(bQ), t, w, 2)
                    dve.drain()
                    dve.tensor_tensor(f(bQ), f(bQ), pj[:, HQ:HQ + 2, c], MUL)
                    done(rest)
                    yield
                    rest.begin(dve, t, "h_tokc")
                    dve.tensor_copy(kdb[0:w, 0:256], ps[0:w, 6, 0:256])
                    dve.tensor_copy(vb[0:w, 0:256], ps[0:w, 6, 256:512])
                    done(rest)
                    yield
                    rest.begin(dve, t, "h_outc")
                    for q in range(2):
                        dve.tensor_copy(pj[half(q), HI:HI + 2, c], ps[half(q), 6 + q, 0:2 * w].rearrange("k (p l) -> k p l", p=2))
                    if t < NT:
                        grow(S_h[:, :, :], eR[:, 0:2, 0:1].to_broadcast([P, 2, DK]),
                             ps[:, 6, 256:256 + 2 * DK].rearrange("k (p v) -> k p v", p=2), None, rest)
                        done(rest)
                        yield
                    else:
                        spread(b_Ue, lambda h: vb[0:w, h * DK:(h + 1) * DK], 4, DK)
                        done(rest)
                        yield
                        rest.begin(dve, t, "h_statec")
                        grow(Q_r[:, :, :, :], eR[:, 0:2, :].unsqueeze(3).to_broadcast([P, 2, NB, DK]),
                             ps[:, 6:8, :].rearrange("k p (b v) -> k p b v", b=NB), None, rest)
                        done(rest)
                        yield
                    rest.begin(dve, t, "s_diff")
                    D8 = bD[0:w, 0:8 * w].rearrange("m (h l) -> m h l", h=8)
                    for g_ in range(2):
                        dve.tensor_tensor(D8[:, 4 * g_:4 * g_ + 4, :], ps[0:w, 6 + g_, 0:4 * w].rearrange("m (j l) -> m j l", j=4),
                                          col(t, 0, T_S + 4 * g_, 4, w, w), SUB)
                    dve.drain()
                    dve.tensor_tensor(D8, D8, neg(t).unsqueeze(1).to_broadcast([w, 8, w]), ADD)
                    done(rest)
                    yield
                    rest.begin(dve, t, "s_att")
                    for g_ in range(2):
                        dve.tensor_tensor(D8[:, 4 * g_:4 * g_ + 4, :], D8[:, 4 * g_:4 * g_ + 4, :],
                                          ps[0:w, 6 + g_, 0:w].unsqueeze(1).to_broadcast([w, 4, w]), MUL)
                        dve.tensor_tensor(kdb[0:w, g_ * 256:(g_ + 1) * 256].rearrange("m (j n) -> m j n", j=4),
                                          ps[0:w, 6, 128 + g_ * DK:128 + (g_ + 1) * DK].unsqueeze(1).to_broadcast([w, 4, DK]),
                                          col(t, 1, T_S + 4 * g_, 4, w, DK), MUL)
                    for b in [vb]:
                        dve.tensor_tensor(b[0:w, 0:256].rearrange("m (h v) -> m h v", h=8),
                                          ps[0:w, 6, 256:512].rearrange("m (h v) -> m h v", h=8), col(t, 2, T_S, 8, w, 32), MUL)
                    done(rest)
                    yield
                    rest.begin(dve, t, "s_q")
                    E4 = ps[:, 6, 0:4 * w].rearrange("k (j l) -> k j l", j=4)
                    dve.tensor_tensor(bQ[:, 0:4 * w].rearrange("k (j l) -> k j l", j=4), E4,
                                      pj[:, SC, c].unsqueeze(1).to_broadcast([P, 4, w]), MUL)
                    keep_last(eR, E4, t, w, 4)
                    done(rest)
                    yield
                    rest.begin(dve, t, "s_outc")
                    for g_ in range(2):
                        dve.scalar_tensor_tensor(out=pj[:, SX + g_, c], in0=pj[:, SX + g_, c], scalar=dcol[:, g_:g_ + 1],
                                                 in1=ps[:, 6 + g_, 0:w], op0=MUL, op1=ADD)
                    if t < NT:
                        grow(S_s[:, :, :], eR[:, :, 0:1].to_broadcast([P, 4, 32]),
                             ps[:, 6, 256:384].rearrange("k (j v) -> k j v", j=4), None, rest)
                        done(rest)
                        yield
                    else:
                        spread(b_Ue, lambda h: vb[0:w, h * 32:(h + 1) * 32], 8, 32)
                        done(rest)
                        yield
                        rest.begin(dve, t, "s_statec")
                        for j in range(4):
                            grow(Qs(Q_r)[:, j], eR[:, j, :].unsqueeze(2).to_broadcast([P, NB, 32]),
                                 ps[:, 6 + j // 2, (j % 2) * 256:(j % 2 + 1) * 256].rearrange("k (b v) -> k b v", b=NB), None, rest)
                        done(rest)
                        yield
                    rest.begin(dve, t, "m_scale")
                    ktok = ps[0:w, 6, 0:256].rearrange("m (h v) -> m h v", h=4)
                    dve.tensor_tensor(tok(kdb), ktok, col(t, 1, T_M, 4, w, DK), MUL)
                    for b in [vb]:
                        dve.tensor_copy(b[0:w, 0:256], ps[0:w, 6, 256:512])
                    Eb = ps[:, 7, 0:2 * w].rearrange("k (p l) -> k p l", p=2)
                    dve.scalar_tensor_tensor(out=f(bQ), in0=pj[:, MQ:MQ + 2, c], scalar=DK ** -0.5, in1=Eb, op0=MUL, op1=MUL)
                    keep_last(eR, Eb, t, w, 2)
                    if t == NT:
                        dve.wait_ge(d_q[3], 128)
                        for p in range(2):
                            dve.tensor_copy(Q_n[:, p, :, 1:DK], Q_n[:, p, :, 0:1].to_broadcast([P, NB, DK - 1]))
                    done(rest)
                    yield
                    rest.begin(dve, t, "m_diff")
                    decays(t, w, D_, 6, T_M, rest)
                    yield
                    rest.begin(dve, t, "m_att")
                    for q in range(2):
                        dve.scalar_tensor_tensor(out=bD[0:w, 2 * q * w:(2 * q + 2) * w], in0=ps[0:w, 6 + q, 0:2 * w], scalar=DK ** -0.5,
                                                 in1=bD[0:w, 2 * q * w:(2 * q + 2) * w], op0=MUL, op1=MUL)
                    done(rest)
                    yield
                    rest.begin(dve, t, "m_outc")
                    den = bKt
                    for q in range(2):
                        dve.tensor_copy(pj[half(q), MV:MV + 2, c], ps[half(q), 6 + q, 0:2 * w].rearrange("k (p l) -> k p l", p=2))
                        dve.tensor_copy(den[half(q), 0:2 * w], ps[half(q), 6 + q, 256:256 + 2 * w])
                    done(rest)
                    yield
                    rest.begin(dve, t, "m_denc")
                    stt(den[:, 0:2 * w], den[:, 0:2 * w], -1.0, den[:, 0:2 * w], MUL, ALU.max)
                    tt(den[:, 0:2 * w], den[:, 0:2 * w], ps[:, 6, 0:2 * w], ALU.max)
                    dve.reciprocal(den[:, 0:2 * w], den[:, 0:2 * w])
                    dve.drain()
                    tt(pj[:, MV:MV + 2, c], pj[:, MV:MV + 2, c], f(den), MUL)
                    if t < NT:
                        for S, o in ((S_c, 0), (S_n, 128)):
                            grow(S[:, :, :], eR[:, 0:2, 0:1].to_broadcast([P, 2, DK]),
                                 ps[:, 7, o:o + 2 * DK].rearrange("k (p v) -> k p v", p=2), None, rest)
                        done(rest)
                        yield
                    else:
                        spread(b_Ue, lambda h: vb[0:w, h * DK:(h + 1) * DK], 4, DK)
                        done(rest)
                        yield
                        for name, Q in (("m_statec", Q_r), ("m_normc", Q_n)):
                            rest.begin(dve, t, name)
                            grow(Q[:, :, :, :], eR[:, 0:2, :].unsqueeze(3).to_broadcast([P, 2, NB, DK]),
                                 ps[:, 6:8, :].rearrange("k p (b v) -> k p b v", b=NB), None, rest)
                            if name == "m_statec":
                                spread(b_Ue, lambda h: ones[0:w, 0:DK], 4, DK)
                            done(rest)
                            yield

            gens = {"g": gdn_dve(), "r": rest_dve()}
            for chain, t, name, engine in order:
                if engine == "dve":
                    next(gens[chain])

            mid_first(dve, gdn, rest)
            for n in range(4):
                gate_t = (GZ, HG, SZ, MO)[n]
                mid.begin(dve, 0, f"o_sq{n}")
                for f in range(2):
                    o = pj[:, BR[2 * n + f], :]
                    if n == 2:
                        tt(o, o, pj[:, gate_t + f, :], MUL)
                    dve.tensor_tensor(rstd2(scr)[:, f, :], o, o, MUL)
                done(mid)
                mid.begin(dve, 0, f"o_n{n}")
                for f in range(2):
                    o = pj[:, BR[2 * n + f], :]
                    wn = (V_GN, V_HN, V_SN + f, V_MN)[n]
                    stt(o, o, vt[:, wn:wn + 1], rstd2(scr)[:, f, :], MUL, MUL)
                    if n != 2:
                        tt(o, o, pj[:, gate_t + f, :], MUL)
                done(mid)

            for d in range(KD):
                for n in range(4):
                    tile = 4 * d + n
                    e = n % 2
                    dve.wait_ge(lin_done, tile + 1)
                    dve.wait_ge(tile_read, tiles_before["gate"] + tile + 1)
                    lift = ps[:, 4 + 2 * e:6 + 2 * e, 0:HN]
                    out = merged_t(pj, d)
                    if n == 0:
                        dve.tensor_tensor(two(out), two(gbuf(pj)[:, e, :]), lift, MUL)
                        dve.drain().then_inc(lin_read, 1)
                    else:
                        tt(two(mtmp(scr)), two(gbuf(pj)[:, e, :]), lift, MUL)
                        dve.tensor_tensor(out, out, mtmp(scr), ADD)
                        dve.drain().then_inc(lin_read, 1)
            mid.begin(dve, 0, "upc")
            done(mid)

            def residual(tile0, d, c0):
                par = d % 2
                dve.wait_ge(tile_done, tile0 + d + 1)
                gt = mod[:, c0 + d, :]
                n1 = T - HN
                dve.scalar_tensor_tensor(out=xT[:, d, 0:HN], in0=ps[:, 2 * par, 0:HN], scalar=gt[:, 0:1], in1=xT[:, d, 0:HN], op0=MUL, op1=ADD)
                dve.scalar_tensor_tensor(out=xT[:, d, HN:T], in0=ps[:, 2 * par + 1, 0:n1], scalar=gt[:, 0:1], in1=xT[:, d, HN:T], op0=MUL, op1=ADD)
                m = mtmp(scr)[:, 0:NS].rearrange("p (b t) -> p b t", t=ND)
                tt(m, ps[:, 2 * par + 1, n1:HN].rearrange("p (b t) -> p b t", t=ND), gt[:, 1:9].unsqueeze(2).to_broadcast([P, NB, ND]), MUL)
                dve.tensor_tensor(xT[:, d, T:TA], xT[:, d, T:TA], mtmp(scr)[:, 0:NS], ADD)
                dve.drain().then_inc(tile_read, 1)

            for d in range(KD):
                residual(tiles_before["wout"], d, 16)
            mid.begin(dve, 0, "res1")
            done(mid)
            squares(mid, "sq2")
            modulate(mid, "norm2", V_N2, 24)

            def ff_mul(i, e):
                dve.wait_ge(lin_done, i * 2 + (32 + e + 1))
                dve.wait_ge(tile_read, i * 2 + (tiles_before["ffa"] + e + 1))
                dve.tensor_tensor(pj[:, bass.ds(i * 2 + (8 + e), 1), :].rearrange("p o (h n) -> p (o h) n", h=2),
                                  two(fbuf(scr)[:, e, :]), ps[:, 4 + 2 * e:6 + 2 * e, 0:HN], MUL).then_inc(lin_read, 1)
            with dve.Fori(0, 11) as i:
                for e in range(2):
                    ff_mul(i, e)
            mid.begin(dve, 0, "ffac")
            done(mid)
            for d in range(KD):
                residual(tiles_before["ffb"], d, 40)
            mid.begin(dve, 0, "res2")
            done(mid)
            squares(mid, "sq3")
            mid.begin(dve, 0, "norm3")
            for k in range(KD):
                dve.scalar_tensor_tensor(out=hT[:, k, :], in0=xT[:, k, :], scalar=vt[:, V_NF + k:V_NF + k + 1], in1=rstd[:, :], op0=MUL, op1=MUL)
            done(mid)


def xtok(pj):
    return pj[:, :, :].rearrange("p a b -> p (a b)")[:, 0:NT * D].rearrange("p (a d) -> p a d", d=D)


def xstok(pj):
    return pj[:, :, :].rearrange("p a b -> p (a b)")[0:NS, NT * D:NT * D + D]


def ctok(pj):
    return pj[:, :, :].rearrange("p a b -> p (a b)")[:, NT * D + D:NT * D + 2 * D]


def ytok(pj, t):
    return pj[:, :, :].rearrange("p a b -> p (a b)")[0:(P if t < NT else NS), t * D:(t + 1) * D]


def hist(scr):
    return scr[0:3 * NB, 3136:3136 + 1280]


def spad(scr):
    return scr[:, 4416:4416 + 560].rearrange("p (f b k) -> p f b k", f=10, k=7)


def tail(scr):
    return scr[0:2 * NS, 4976:4976 + 1280]


def rowbuf(scr, n):
    return scr[0:NR, 544 * n:544 * (n + 1)]


def RS(scr):
    return scr[:, 544 * 8:544 * 9]


def RK(scr):
    return scr[:, 544 * 9:544 * 10]


def RN(scr):
    return scr[:, 544 * 10:544 * 11]


def MTs(hrow):
    return hrow


def hrow2(scr):
    return scr[:, 0:512]


def Qs(Q):
    return Q[:, :, :, :].rearrange("k p b v -> k (p b v)").rearrange("k (j b v) -> k j b v", j=4, b=NB)


def bVs(scr):
    return scr[:, 4352 + 2816:4352 + 2816 + 256]


WB_A = 6


def wb(scr):
    return scr[:, 0:WB_A * D].rearrange("p (n c) -> p n c", c=D)


def wb2(pj):
    return pj[:, MQ:MQ + 4, :].rearrange("p a b -> p (a b)")[:, 0:2 * D].rearrange("p (n c) -> p n c", c=D)


def rstd2(scr):
    return scr[:, 6848:7936].rearrange("p (f n) -> p f n", f=2)


def mtmp(scr):
    return scr[:, 7168:7168 + TA]


def fbuf(scr):
    return scr[:, 0:2 * TA].rearrange("p (e n) -> p e n", e=2)


GBUF = 14


def gbuf(pj):
    return pj[:, GBUF:GBUF + 2, :]


MERGED = [0, 1, 2, 3, 6, 7, 8, 9]


def merged_t(pj, d):
    return pj[:, MERGED[d], :]


def mid_first(eng, gdn, rest):
    gdn.after(eng, NT, "g_statec")
    rest.after(eng, NT, "m_normc")


_INS = ['x_prompt', 'x_sample', 'c_prompt', 'c_sample', 'state_gdn', 'state_gdn_conv', 'state_hgrn', 'state_ssd',
        'state_ssd_conv', 'state_mlstm_c', 'state_mlstm_n', 'state_mlstm_m', 'ada_w', 'ada_b', 'norm1_w', 'norm2_w', 'w_in',
        'gdn_conv_w', 'gdn_conv_b', 'gdn_a_log', 'gdn_dt_bias', 'gdn_norm_w', 'hg_lb_logits', 'hg_norm_w', 'ssd_conv_w',
        'ssd_conv_b', 'ssd_a_log', 'ssd_dt_bias', 'ssd_d', 'ssd_norm_w', 'ml_b_i', 'ml_b_f', 'ml_norm_w', 'w_branch',
        'w_out', 'ffn_w_in', 'ffn_w_out', 'final_norm_w']


def _state_shapes(b):
    return [(1, b, 4, 64, 64), (1, b, 3, 768), (1, b, 4, 64, 64), (1, b, 8, 64, 32), (1, b, 3, 512), (1, b, 4, 64, 64),
            (1, b, 4, 64), (1, b, 4)]


_OUTS = [(1, T, D), (NB, ND, D)] + _state_shapes(1) + _state_shapes(NB)


def kernel(**inputs):
    import concourse.bacc as _bacc
    from concourse.bass_utils import run_bass_kernel_spmd as _run

    nc = _bacc.Bacc("TRN2", target_bir_lowering=False, num_devices=1)
    arrays, args = {}, {}
    for name in _INS + ["const"]:
        a = host_constants() if name == "const" else np.ascontiguousarray(inputs[name])
        arrays[f"in_{name}_dram"] = a
        args[name] = nc.dram_tensor(f"in_{name}_dram", a.shape, mybir.dt.from_np(a.dtype), kind="ExternalInput").ap()
    outs = [nc.dram_tensor(f"out_{i}_dram", shape, F32, kind="ExternalOutput").ap() for i, shape in enumerate(_OUTS)]
    trunk(nc, args, outs)
    r = _run(nc, [arrays], core_ids=[0])
    return tuple(r.results[0][f"out_{i}_dram"] for i in range(len(_OUTS)))
```

```python
from contextlib import ExitStack

import numpy as np

import concourse.bass as bass
from concourse import mybir

F32 = mybir.dt.float32
ALU = mybir.AluOpType
ACT = mybir.ActivationFunctionType
AX = mybir.AxisListType

P = 128
D = 1024
KD = D // P
T = 512
B0, C0, SCR = 4864, 8448, 11264
NB, ND = 8, 4
NS = NB * ND
TA = T + NS
HN = TA // 2
NT = T // P
FF = 2816
KF = FF // P
DK = 64
EPS = 1e-6
BIG = 1e30
R = 4
SLOT = 2048

MIX_ORDER = [0, 1, 2, 9, 10, 4, 5, 6, 11, 12, 13, 3, 8, 7, 14]
GROUP_COLS = [0, 256, 512, 768, 1032, 1288, 1544, 1800, 2056, 2312, 2568, 2832, 3088, 3344, 3600]
C_GB, C_GA, C_DT, C_MI, C_MF, C_GATE = 1024, 1028, 2824, 3856, 3860, 3864
GQ, GK, GV, GZ, HQ, HF, HI, HG, SZ, SX, SB, SC, MQ, MK, MV, MO = 0, 2, 4, 6, 8, 10, 12, 14, 16, 18, 20, 21, 22, 24, 26, 28
BR = [GV, GV + 1, HI, HI + 1, SX, SX + 1, MV, MV + 1]
CONV_G, CONV_S = [0, 1, 2, 3, 4, 5], [18, 19, 20, 21]
R_G, R_S, R_M, NR = 0, 32, 64, 96
T_G, T_S, T_M, NCOL = 0, 4, 12, 16
LEVELS = [1, 2, 4, 8, 16, 32, 64]

K_ID, K_B64, K_ONE, K_MASK, K_NEG, K_NEGS, K_RST, K_OWN, K_SGN, K_N = 0, 128, 256, 384, 1280, 1408, 1440, 1984, 1992, 1993
V_ADAB, V_N1, V_N2, V_NF, V_GCW, V_GCB, V_SCW, V_SCB, V_1 = 0, 48, 56, 64, 72, 96, 102, 118, 122
V_SN, V_GN, V_HN, V_MN, V_2 = 122, 124, 125, 126, 127


def host_constants():
    c = np.zeros((P, K_N), np.float32)
    i = np.arange(P)
    c[:, K_ID:K_ID + P] = np.eye(P)
    c[:, K_B64:K_B64 + P] = i[:, None] // DK == i[None] // DK
    c[:, K_ONE:K_ONE + P] = 1
    m, l = i[:, None], i[None]
    for n, s in enumerate(LEVELS):
        c[:, K_MASK + n * P:K_MASK + (n + 1) * P] = (m // (2 * s) == l // (2 * s)) & (m % (2 * s) < s) & (l % (2 * s) >= s)
    c[:, K_NEG:K_NEG + P] = np.where(m <= l, 0, -BIG)
    m, l = m[:NS], l[:, :NS]
    c[:NS, K_NEGS:K_NEGS + NS] = np.where((m <= l) & (m // ND == l // ND), 0, -BIG)
    reset = np.ones(TA)
    reset[0:T:P] = 0
    reset[T::ND] = 0
    c[:, K_RST:K_RST + TA] = reset
    c[:NS, K_OWN:K_OWN + NB] = i[:NS, None] // ND == np.arange(NB)
    c[:, K_SGN] = np.where(i < R_M, 1, -1)
    return c


class Chain:

    def __init__(self, sem, stages):
        self.sem, self.stages = sem, stages
        self.at = {(t, name): n for n, (t, name, _) in enumerate(stages)}

    def begin(self, eng, t, name):
        n = self.at[(t, name)]
        if n:
            eng.wait_ge(self.sem, n)

    def after(self, eng, t, name):
        eng.wait_ge(self.sem, self.at[(t, name)] + 1)


PRE = -1


def gdn_stages(t):
    if t == PRE:
        s = [("tail", "pe"), ("tailc", "dve")]
        for n in range(6):
            s += [(f"conv{n}", "dve"), (f"silu{n}", "act")]
        s += [("l2sq", "dve")]
        for n in range(4):
            s += [(f"l2_{n}", "pe"), (f"l2r{n}", "act")]
        return [(t, "g_" + n, e) for n, e in s + [("l2m", "dve")]]
    s = [("tokens", "pe"), ("scale", "dve"), ("bcast", "pe"), ("diff", "dve"), ("decay", "act"), ("kk", "pe"),
         ("lower", "dve"), ("first", "pe"), ("t1", "act")]
    for n in levels_of(t)[1:]:
        s += [(f"x{n}", "pe"), (f"xc{n}", "act"), (f"y{n}", "pe"), (f"upd{n}", "dve")]
    s += [("qk", "pe"), ("aq", "dve"), ("sk", "pe"), ("skc", "act"), ("u", "pe"), ("uc", "dve")]
    if t == NT:
        s += [("ut", "pe"), ("utc", "dve")]
    s += [("out", "pe"), ("outc", "dve")]
    if t == NT:
        s += [("state", "pe"), ("statec", "dve")]
    return [(t, "g_" + n, e) for n, e in s]


def hgrn_stages(t):
    if t == PRE:
        s = [("lb0", "dve"), ("lb1", "act"), ("lb2", "dve"), ("lb3", "pe"), ("lb4", "dve"), ("lb5", "act"), ("silu", "act"),
             ("lb6", "dve")]
        for f in range(2):
            s += [(f"ls{f}", "act"), (f"b{f}", "dve"), (f"ln{f}", "act"), (f"g{f}", "dve")]
        return [(t, "h_" + n, e) for n, e in s]
    s = [("qk", "pe"), ("diag", "dve")]
    for n in levels_of(t):
        s += [(f"dec{n}", "act"), (f"sc{n}", "dve"), (f"qk{n}", "pe"), (f"add{n}", "dve")]
    s += [("dec", "act"), ("kd", "dve"), ("tok", "pe"), ("tokc", "dve"), ("out", "pe"), ("outc", "dve")]
    if t == NT:
        s += [("state", "pe"), ("statec", "dve")]
    return [(t, "h_" + n, e) for n, e in s]


def ssd_stages(t):
    if t == PRE:
        s = [("w_a", "pe"), ("rz", "dve"), ("w_b", "pe"), ("rb", "act"), ("ri", "dve"), ("rexp", "act"), ("rv", "dve")]
        for n in range(3):
            s += [(f"rcol{n}", "pe"), (f"rcolc{n}", "dve")]
        s += [("tail", "pe"), ("tailc", "dve")]
        for n in range(4):
            s += [(f"conv{n}", "dve"), (f"silu{n}", "act")]
        return [(t, "s_" + n, e) for n, e in s]
    s = [("bcast", "pe"), ("diff", "dve"), ("decay", "act"), ("cb", "pe"), ("att", "dve"), ("e", "pe"),
         ("q", "dve"), ("out", "pe"), ("outc", "dve")]
    if t == NT:
        s += [("state", "pe"), ("statec", "dve")]
    return [(t, "s_" + n, e) for n, e in s]


def mlstm_stages(t):
    s = [("tok", "pe"), ("scale", "dve"), ("bcast", "pe"), ("diff", "dve"), ("decay", "act"), ("qk", "pe"),
         ("att", "dve"), ("out", "pe"), ("outc", "dve"), ("den", "pe"), ("denc", "dve")]
    if t == NT:
        s += [("state", "pe"), ("statec", "dve"), ("norm", "pe"), ("normc", "dve")]
    return [(t, "m_" + n, e) for n, e in s]


def levels_of(t):
    return range(len(LEVELS)) if t < NT else range(2)


U_MIX = 4 * len(MIX_ORDER)
U_ADA = 8
U_GATE = 64
UNITS = U_MIX + U_ADA + U_GATE


def units_through(f):
    return 4 * MIX_ORDER.index(f // 2) + 2 * (f % 2) + 2


NEEDS = {
    ("g", PRE, "g_tail"): [("x", units_through(5))],
    ("g", 0, "g_tokens"): [("s", PRE, "s_rcolc2")],
    ("h", PRE, "h_silu"): [("x", units_through(13)), ("s", PRE, "s_w_b")],
    ("h", PRE, "h_lb2"): [("s", PRE, "s_w_b")],
    ("s", PRE, "s_tail"): [("x", units_through(21))],
    ("s", 0, "m_tok"): [("x", units_through(27))],
}
COST = {"pe": 1.2, "dve": 1.2, "act": 0.9}
COSTS = {"g_scale": 2.3, "g_diff": 1.4, "g_lower": 2.6, "g_upd": 2.0, "g_aq": 0.7, "g_uc": 0.5, "h_diag": 1.0, "h_sc": 0.9,
         "h_add": 1.8, "s_diff": 2.4, "s_att": 2.6, "s_conv": 3.6, "g_conv": 3.6, "s_ri": 16.0, "g_l2sq": 2.4, "g_l2m": 2.4,
         "h_b": 2.2, "h_g": 3.0, "h_ls": 2.6, "h_ln": 2.6, "h_silu": 3.0, "s_rb": 3.0, "g_y": 1.9, "s_w_a": 7.0, "s_w_b": 7.0,
         "g_tail": 1.8, "g_silu": 0.8, "s_silu": 0.8}


def cost(name, engine):
    for k in range(len(name), 2, -1):
        if name[:k] in COSTS:
            return COSTS[name[:k]]
    return COST[engine]


def shared_order(chains):
    free = {"pe": 0.0, "dve": 0.0, "act": 0.0}
    at = {c: 0 for c in chains}
    when = {}
    ready = {c: 0.0 for c in chains}
    out, unit, part_, evac = [], 0, 0, []
    while unit < UNITS or any(at[c] < len(chains[c]) for c in chains):
        best = None
        for c in chains:
            if at[c] >= len(chains[c]):
                continue
            t, name, eng = chains[c][at[c]]
            needs = [when.get(("x", n[1]) if n[0] == "x" else n) for n in NEEDS.get((c, t, name), [])]
            if None in needs:
                continue
            start = max([free[eng], ready[c]] + needs)
            if best is None or start < best[0] - 1e-9:
                best = (start, c, t, name, eng)
        if evac:
            start = max(free["act"], evac[0][0])
            if best is None or start <= best[0]:
                best = (start, "x", evac[0][1], "read", "act")
        if unit < UNITS:
            start = max(free["pe"], when.get(("x", unit - 1), 0.0) if unit >= 2 else 0.0)
            if not (unit >= 2 and ("x", unit - 1) not in when) and (best is None or start < best[0]):
                best = (start, "x", unit, f"part{part_}", "pe")
        start, c, t, name, eng = best
        if c == "x" and eng == "act":
            free[eng] = start + 0.5
            when[("x", t + 1)] = free[eng]
            evac.pop(0)
        elif c == "x":
            free[eng] = start + 1.85
            if part_ == 1:
                evac.append((free[eng], unit))
                unit, part_ = unit + 1, 0
            else:
                part_ = 1
        else:
            free[eng] = start + cost(name, eng)
            ready[c] = free[eng] + 0.1
            when[(c, t, name)] = ready[c]
            at[c] += 1
        out.append((c, t, name, eng))
    while evac:
        out.append(("x", evac.pop(0)[1], "read", "act"))
    return out


def trunk(nc, A, O):
    ctx = ExitStack()
    with ctx:
        ctx.enter_context(nc.allow_non_contiguous_dma(reason="state vectors, a few KB"))

        def sb(name, shape):
            return ctx.enter_context(nc.sbuf_tensor(name, shape, F32))

        def sem(name):
            return ctx.enter_context(nc.semaphore(name))

        ps = ctx.enter_context(nc.psum_tensor("ps", [P, 8, 512], F32))
        cst = sb("cst", [P, K_N])
        vt = sb("vt", [P, V_2])
        hT = sb("hT", [P, KD, TA])
        pj = sb("pj", [P, 30, TA])
        ring = sb("ring", [P, R, SLOT])
        cT = sb("cT", [P, KD, NB + 1])
        mod = sb("mod", [P, 6 * KD, NB + 1])
        coef = sb("coef", [P, KD, NB + 1])
        rstd = sb("rstd", [P, TA])
        colp = sb("colp", [P, 4])
        hcol = sb("hcol", [P, 2, 6])
        dcol = sb("dcol", [P, 2])
        hrow = sb("hrow", [P, 264])
        cols = sb("cols", [P, NT + 1, 4, NCOL])
        Rr = sb("Rr", [P, TA])
        Er = sb("Er", [P, TA])
        Vr = sb("Vr", [P, TA])
        MTr = sb("MTr", [P, TA])
        kg = sb("kg", [P, 2, TA])
        S_g = sb("S_g", [P, 2, DK])
        S_h = sb("S_h", [P, 2, DK])
        S_s = sb("S_s", [P, 4, 32])
        S_c = sb("S_c", [P, 2, DK])
        S_n = sb("S_n", [P, 2, DK])
        Q = sb("Q", [P, 5, 1024])
        Q_g, Q_h, Q_s, Q_c, Q_n = (Q[:, n, :].rearrange("k (p b v) -> k p b v", p=2, b=NB) for n in range(5))
        eG = sb("eG", [P, 2, NB])
        eH = sb("eH", [P, 2, NB])
        eR = sb("eR", [P, 4, NB])
        scr = sb("scr", [P, SCR])
        gates_out = nc.dram_tensor("gates_scratch", [32, 2, P, HN], F32, kind="Internal").ap()
        x_out = nc.dram_tensor("x_scratch", [P, KD * TA], F32, kind="Internal").ap()

        def part(at, n):
            return scr[:, at:at + n]

        xT0 = part(0, KD * TA).rearrange("p (k n) -> p k n", n=TA)
        xT = Q[:, :, :].rearrange("p a b -> p (a b)")[:, 0:KD * TA].rearrange("p (k n) -> p k n", n=TA)
        vrow = part(5000, 2 * P).rearrange("p (a c) -> p a c", a=2)
        wsm = part(C0, KD * 2 * NR).rearrange("p (k e r) -> p k e r", k=KD, e=2)

        gT, gU, gX, gL, gD = (part(512 * n, 512) for n in range(5))
        g_vb, g_kn, g_kd, g_u, g_sk, g_qs, g_kb = (part(2560 + 256 * n, 256) for n in range(7))
        gAt = part(4352, 512)
        g_Ue = part(0, 2048)
        g_acc, g_hist, g_spad, g_tail = part(0, 1088), part(1088, 768), part(1856, 336), part(2192, 768)
        bD, bKd, bV, bQ, bDen = part(B0, 1024), part(B0 + 2048, 512), part(B0 + 2560, 256), part(B0 + 2816, 512), part(B0 + 1536, 256)
        b_Ue = part(B0, 2048)
        s_acc, s_spad, s_tail, s_hist = part(B0, 1088), part(B0 + 1088, 224), part(B0 + 1312, 512), part(B0 + 2720, 512)
        hD, hX, hQl, hKl, hEf = part(C0, 512), part(C0 + 512, 512), part(C0 + 1024, 256), part(C0 + 1280, 256), part(C0 + 1536, 256)
        hV, hQ, hKd = part(C0 + 2048, 256), part(C0 + 2304, 256), part(C0 + 2560, 256)
        h_Ue = part(C0, 2048)
        hrow2 = part(C0 + 1600, 512)

        ident = cst[:, K_ID:K_ID + P]
        b64 = cst[:, K_B64:K_B64 + P]
        ones = cst[:, K_ONE:K_ONE + P]

        def mask(n, p):
            return cst[0:p, K_MASK + n * P:K_MASK + n * P + p]

        def neg(t):
            return cst[:, K_NEG:K_NEG + P] if t < NT else cst[0:NS, K_NEGS:K_NEGS + NS]

        d_cst, d_vec, d_x, d_c, d_wsm, d_row, d_hist, d_st = (sem(n) for n in
            ("d_cst", "d_vec", "d_x", "d_c", "d_wsm", "d_row", "d_hist", "d_st"))
        d_q = {n: sem(f"d_q_{n}") for n in ("gdn", "hgrn", "ssd", "mlstm")}
        d_wb, d_xout, d_xin = sem("d_wb"), sem("d_xout"), sem("d_xin")
        d_tail_g, d_tail_s = sem("d_tail_g"), sem("d_tail_s")
        g_out = [sem("g_out0"), sem("g_out1")]
        g_in = [sem(f"g_in{n}") for n in range(4)]
        w_in_slot = [sem(f"w_in_slot{n}") for n in range(R)]
        w_used = sem("w_used")
        zeroed = sem("zeroed")
        x_done, x_read = sem("x_done"), sem("x_read")
        tile_done = sem("tile_done")
        tile_read = sem("tile_read")
        lin_done, lin_read = sem("lin_done"), sem("lin_read")
        gate_ready = sem("gate_ready")
        half_used = sem("half_used")
        stored = sem("stored")
        pre_s, gdn_s, hgrn_s, rest_s, mid_s = sem("pre"), sem("gdn"), sem("hgrn"), sem("rest"), sem("mid")

        pre = [("vec", "pe"), ("vecc", "dve"), ("silc", "act"), ("ct", "pe"), ("ctc", "dve")]
        for d in range(KD):
            pre += [(f"x{d}", "pe"), (f"xc{d}", "act")]
        pre += [("sq1", "dve"), ("ss1", "pe"), ("rs1", "act"), ("ada1", "pe"), ("mod1", "dve"), ("norm1", "dve")]
        pre = Chain(pre_s, [(0, n, e) for n, e in pre])
        tiles = range(NT + 1)
        gdn = Chain(gdn_s, [s for t in (PRE, *tiles) for s in gdn_stages(t)])
        hgrn = Chain(hgrn_s, [s for t in (PRE, *tiles) for s in hgrn_stages(t)])
        rest = Chain(rest_s, [s for t in (PRE, *tiles) for s in ssd_stages(t)] + [s for t in tiles for s in mlstm_stages(t)])
        order = shared_order({"g": gdn.stages, "h": hgrn.stages, "s": rest.stages})
        mid = [("mod2", "dve"), ("silus", "act")]
        for n in range(4):
            mid += [(f"o_sq{n}", "dve"), (f"o_ss{n}", "pe"), (f"o_rs{n}", "act"), (f"o_n{n}", "dve")]
        mid += [("up", "pe"), ("upc", "dve"), ("wout", "pe"), ("res1", "dve"), ("sq2", "dve"), ("ss2", "pe"), ("rs2", "act"),
                ("norm2", "dve"), ("ffa", "pe"), ("ffac", "dve"), ("ffb", "pe"), ("res2", "dve"), ("sq3", "dve"), ("ss3", "pe"),
                ("rs3", "act"), ("norm3", "dve")]
        for t in range(NT + 1):
            mid += [(f"y{t}", "pe"), (f"yc{t}", "act")]
        mid = Chain(mid_s, [(0, n, e) for n, e in mid])

        phases = [("ada1", 8), ("mixer", 15), ("ada2", 16), ("gate", 16), ("wout", 4), ("ffa", 22), ("ffb", 16)]
        first, n = {}, 0
        for kind, count in phases:
            first[kind] = n
            n += count
        counts = dict(phases)
        tiles_before = {"wout": 0, "ffa": 8, "ffb": 30}

        def landed(eng, slot, n):
            if isinstance(n, int):
                eng.wait_ge(w_in_slot[slot], 32 * (n // R + 1))
            else:
                eng.wait_ge(w_in_slot[slot], n * (32 // R) + (32 - slot * (32 // R)))

        block = ctx.enter_context(nc.Block())

        @block.sync
        def _(sp):
            sp.dma_start(cst[:, :], A["const"]).then_inc(d_cst, 16)
            sp.dma_start(xtok(pj), A["x_prompt"][0].rearrange("(a p) d -> p a d", p=P)).then_inc(d_x, 16)
            sp.dma_start(xstok(pj), A["x_sample"].rearrange("b t d -> (b t) d")).then_inc(d_x, 16)
            sp.dma_start(ctok(pj)[0:1, :], A["c_prompt"]).then_inc(d_c, 16)
            sp.dma_start(ctok(pj)[1:NB + 1, :], A["c_sample"]).then_inc(d_c, 16)
            rows = lambda a, n: A[a].rearrange("o (r c) -> (o r) c", c=P)
            for name, at, n in (("ada_b", V_ADAB, 48), ("norm1_w", V_N1, 8), ("norm2_w", V_N2, 8),
                                ("gdn_conv_b", V_GCB, 6), ("ssd_conv_b", V_SCB, 4)):
                sp.dma_start(vrow[at:at + n, 0, :], rows(name, n)).then_inc(d_vec, 16)
            sp.dma_start(vrow[V_NF:V_NF + 8, 0, :], A["final_norm_w"].rearrange("(r c) -> r c", c=P)).then_inc(d_vec, 16)
            sp.dma_start(vrow[V_GCW:V_GCW + 24, 0, :], A["gdn_conv_w"].rearrange("o k (r c) -> (o k r) c", c=P)).then_inc(d_vec, 16)
            sp.dma_start(vrow[V_SCW:V_SCW + 16, 0, :], A["ssd_conv_w"].rearrange("o k (r c) -> (o k r) c", c=P)).then_inc(d_vec, 16)
            sp.dma_start(vrow[0:2, 1, :], rows("ssd_norm_w", 2)).then_inc(d_vec, 16)
            for n, name in enumerate(("gdn_norm_w", "hg_norm_w", "ml_norm_w")):
                for h in range(2):
                    sp.dma_start(vrow[2 + n:3 + n, 1, h * DK:(h + 1) * DK], A[name]).then_inc(d_vec, 16)
            sp.dma_start(hrow[0:1, 256:264], A["ssd_d"]).then_inc(d_vec, 16)
            sp.dma_start(hrow[0:1, 0:256], A["hg_lb_logits"]).then_inc(d_vec, 16)

            def kp(name):
                return A[name][0].rearrange("(k p) c -> p k c", p=P)

            def load(kind, slot, idx):
                full = ring[:, slot, :]
                if kind in ("ada1", "ada2", "mixer", "wout"):
                    src = kp({"ada1": "ada_w", "ada2": "ada_w", "mixer": "w_in", "wout": "w_out"}[kind])
                    if kind == "mixer":
                        c0 = GROUP_COLS[MIX_ORDER[idx]]
                    else:
                        c0 = idx * 256 + (2048 if kind == "ada2" else 0)
                    dst = full.rearrange("p (k c) -> p k c", k=KD)
                    for h in range(2):
                        sp.dma_start(dst[:, 4 * h:4 * h + 4, :], src[:, 4 * h:4 * h + 4, bass.ds(c0, 256)]).then_inc(w_in_slot[slot], 16)
                elif kind == "gate":
                    dst = full.rearrange("p (k e c) -> p k e c", k=KD, e=2)
                    for e in range(2):
                        c0 = C_GATE + (2 * (idx % 2) + e) * D + idx // 2 * P
                        sp.dma_start(dst[:, :, e, :], kp("w_in")[:, :, c0:c0 + P]).then_inc(w_in_slot[slot], 16)
                elif kind == "ffa":
                    dst = full.rearrange("p (k e c) -> p k e c", k=KD, e=2)
                    for e in range(2):
                        sp.dma_start(dst[:, :, e, :], kp("ffn_w_in")[:, :, bass.ds(idx * P + e * FF, P)]).then_inc(w_in_slot[slot], 16)
                else:
                    dst = full[:, 0:11 * P].rearrange("p (k c) -> p k c", c=P)
                    e, d = idx
                    for k0, k1 in ((0, 6), (6, 11)):
                        sp.dma_start(dst[:, k0:k1, :], kp("ffn_w_out")[:, 11 * e + k0:11 * e + k1, bass.ds(d * P, P)]).then_inc(w_in_slot[slot], 16)

            def slot_of(kind, idx):
                return (first[kind] + idx) % R

            for idx in range(counts["ada1"]):
                if idx >= R:
                    sp.wait_ge(w_used, idx - R + 1)
                load("ada1", slot_of("ada1", idx), idx)
            sp.wait_ge(zeroed, 1)
            for e, at, c0, w in ((0, R_G, C_GA, 4), (0, R_S, C_DT, 8), (0, R_M, C_MF, 4), (1, R_G, C_GB, 4), (1, R_M, C_MI, 4)):
                sp.dma_start(wsm[:, :, e, at:at + w], kp("w_in")[:, :, c0:c0 + w]).then_inc(d_wsm, 16)
            for at, name, c in ((R_G, "gdn_dt_bias", 0), (R_S, "ssd_dt_bias", 0), (R_M, "ml_b_f", 0),
                                (R_G, "gdn_a_log", 1), (R_S, "ssd_a_log", 1), (R_M, "ml_b_i", 2)):
                w = A[name].shape[1]
                sp.dma_start(colp[at:at + w, c:c + 1], A[name].rearrange("o h -> h o")).then_inc(d_row, 16)
            sp.dma_start(hrow[64:68, 0:NB * 5:5], A["state_mlstm_m"][0].rearrange("b h -> h b")).then_inc(d_st, 16)
            window = [("ada1", n) for n in range(8)] + [("mixer", n) for n in range(15)] + [("ada2", n) for n in range(16)] \
                + [("gate", n) for n in range(16)] + [("wout", n) for n in range(R)]
            reader = {"mixer": lambda i: 4 * i + 4, "ada2": lambda i: U_MIX + i // 2 + 1, "gate": lambda i: U_MIX + U_ADA + 4 * i + 4}
            for n in range(8, len(window)):
                kind, idx = window[n]
                held, hidx = window[n - R]
                if held == "ada1":
                    sp.wait_ge(w_used, hidx + 1)
                else:
                    sp.wait_ge(x_done, reader[held](hidx))
                load(kind, n % R, idx)
                if n == 11:
                    pre.after(sp, 0, "xc7")
                    sp.dma_start(x_out, part(0, KD * TA)).then_inc(d_xout, 16)
                    sp.dma_start(s_hist[0:3 * NB, :], A["state_ssd_conv"][0].rearrange("b k c -> (b k) c")).then_inc(d_hist, 16)
                    pre.after(sp, 0, "norm1")
                    sp.wait_ge(d_xout, 16)
                    sp.dma_start(g_hist[0:3 * NB, :], A["state_gdn_conv"][0].rearrange("b k c -> (b k) c")).then_inc(d_hist, 16)
                if n == 14:
                    for p in range(2):
                        for q in range(2):
                            at, h = slice(q * DK, (q + 1) * DK), 2 * p + q
                            for Qx, name, d in ((Q_g, "state_gdn", "gdn"), (Q_h, "state_hgrn", "hgrn"), (Q_c, "state_mlstm_c", "mlstm")):
                                sp.dma_start(Qx[at, p], A[name][0, :, h].rearrange("b k v -> k b v")).then_inc(d_q[d], 16)
                            sp.dma_start(Q_n[at, p, :, 0], A["state_mlstm_n"][0, :, h].rearrange("b k -> k b")).then_inc(d_q["mlstm"], 16)
                    for g in range(2):
                        for j in range(4):
                            sp.dma_start(Qs(Q_s)[g * DK:(g + 1) * DK, j], A["state_ssd"][0, :, 4 * g + j].rearrange("b n v -> n b v")).then_inc(d_q["ssd"], 16)
            stored_at = [0]

            def store(dst, src):
                sp.dma_start(dst, src).then_inc(stored, 16)
                stored_at[0] += 16

            def heads(dst, S):
                for p in range(2):
                    for q in range(2):
                        store(dst[2 * p + q], S[q * DK:(q + 1) * DK, p])

            def qheads(dst, S):
                for p in range(2):
                    for q in range(2):
                        store(dst[:, 2 * p + q].rearrange("b k v -> k b v"), S[q * DK:(q + 1) * DK, p])

            hgrn.after(sp, NT, "h_statec")
            qheads(O[12][0], Q_h)
            heads(O[4][0, 0], S_h)
            gdn.after(sp, NT, "g_statec")
            qheads(O[10][0], Q_g)
            heads(O[2][0, 0], S_g)
            rest.after(sp, NT, "m_normc")
            for h in range(2):
                sp.dma_start(wb(scr)[:, 4 * h:4 * h + 4, :], A["w_branch"][0].rearrange("n (k p) c -> p (n k) c", p=P)[:, 4 * h:4 * h + 4, :]).then_inc(d_wb, 16)
            for g in range(2):
                for j in range(4):
                    store(O[13][0, :, 4 * g + j].rearrange("b n v -> n b v"), Qs(Q_s)[g * DK:(g + 1) * DK, j])
                    store(O[5][0, 0, 4 * g + j], S_s[g * DK:(g + 1) * DK, j])
            qheads(O[15][0], Q_c)
            heads(O[7][0, 0], S_c)
            for p in range(2):
                for q in range(2):
                    store(O[16][0, :, 2 * p + q].rearrange("b k -> k b"), Q_n[q * DK:(q + 1) * DK, p, :, 0])
                    store(O[8][0, 0, 2 * p + q].unsqueeze(1), S_n[q * DK:(q + 1) * DK, p, 0:1])
            store(O[9][0].rearrange("o h -> h o"), MTr[R_M:R_M + 4, T - 1:T])
            store(O[17][0].rearrange("b h -> h b"), MTr[R_M:R_M + 4, T + ND - 1:TA:ND])
            mid.after(sp, 0, "o_n2")
            for h in range(2):
                sp.wait_ge(g_out[h], 16 * 32)

            def gate_back(k):
                sp.dma_start(gbuf(pj)[:, k % 4, :].rearrange("p (h n) -> p h n", h=2), gates_out[k].rearrange("h p n -> p h n")).then_inc(g_in[k % 4], 16)
            for k in range(4):
                gate_back(k)
            sp.wait_ge(stored, stored_at[0])
            sp.dma_start(Q[:, :, :].rearrange("p a b -> p (a b)")[:, 0:KD * TA], x_out).then_inc(d_xin, 16)
            for k in range(4, 32):
                sp.wait_ge(lin_read, k - 3)
                gate_back(k)
            for idx in range(R):
                sp.wait_ge(tile_done, 2 * idx + 2)
                load("ffa", slot_of("ffa", idx), idx)
            with sp.Fori(0, 4) as i:
                for r in range(R):
                    sp.wait_ge(lin_done, i * R + (32 + r + 1))
                    load("ffa", slot_of("ffa", r), i * R + (R + r))
            for idx in range(5 * R, counts["ffa"]):
                sp.wait_ge(lin_done, 32 + idx - R + 1)
                load("ffa", slot_of("ffa", idx), idx)
            for idx in range(R):
                sp.wait_ge(lin_done, 32 + counts["ffa"] - R + idx + 1)
                load("ffb", slot_of("ffb", idx), (idx % 2, idx // 2))
            with sp.Fori(0, 3) as i:
                for r in range(R):
                    if r % 2:
                        sp.wait_ge(tile_done, i * 2 + (tiles_before["ffb"] + r // 2 + 1))
                    else:
                        sp.wait_ge(half_used, i * 2 + (r // 2 + 1))
                    load("ffb", slot_of("ffb", r), (r % 2, i * 2 + (2 + r // 2)))
            for t in range(NT + 1):
                mid.after(sp, 0, f"yc{t}")
                yt = ytok(pj, t)
                store(O[0][0, t * P:(t + 1) * P, :] if t < NT else O[1].rearrange("b t d -> (b t) d"), yt)
            sp.wait_ge(stored, stored_at[0])
            sp.wait_ge(d_tail_g, 9 * 16)
            sp.wait_ge(d_tail_s, 9 * 16)

        @block.gpsimd
        def _(pool):
            pool.memset(wsm[:, :, :, :], 0.0)
            pool.memset(colp[:, :], 0.0)
            pool.drain()
            for S in (S_g, S_h, S_s, S_c, S_n):
                pool.memset(S[:, :, :], 0.0)
            pool.drain().then_inc(zeroed, 1)
            for chain, name, tl, po, so, d in ((gdn, "g_tailc", g_tail, O[3], O[11], d_tail_g), (rest, "s_tailc", s_tail, O[6], O[14], d_tail_s)):
                chain.after(pool, PRE, name)
                pool.dma_start(po[0, 0], tl[NS - 3:NS, :]).then_inc(d, 16)
                for b in range(NB):
                    r0 = NS + ND * b + 1
                    pool.dma_start(so[0, b], tl[r0:r0 + 3, :]).then_inc(d, 16)
            for u in range(U_GATE):
                pool.wait_ge(x_read, U_MIX + U_ADA + u + 1)
                pool.dma_start(gates_out[u // 2, u % 2], rstd[:, (u % 2) * HN:(u % 2 + 1) * HN]).then_inc(g_out[u % 2], 16)
            for h in range(2):
                pool.wait_ge(g_out[h], 16 * (U_GATE // 2))

        @block.tensor
        def _(pe):
            def mm(out, lhsT, rhs, start=True, stop=True):
                return pe.matmul(out, lhsT, rhs, start=start, stop=stop, skip_group_check=True)

            def tr(out, in_):
                n = in_.shape[0]
                return pe.transpose(out, in_, ident[0:n, 0:n])

            pe.wait_ge(d_cst, 16)
            pe.wait_ge(d_vec, 16 * 17)
            tr(ps[:, 4, 0:V_1], vrow[0:V_1, 0, :])
            tr(ps[:, 4, V_1:V_2], vrow[0:V_2 - V_1, 1, :]).then_inc(pre_s, 1)
            pre.begin(pe, 0, "ct")
            for k in range(KD):
                last = tr(ps[:, 5, (NB + 1) * k:(NB + 1) * (k + 1)], ctok(pj)[0:NB + 1, k * P:(k + 1) * P])
            last.then_inc(pre_s, 1)
            pe.wait_ge(d_x, 32)
            for d in range(KD):
                pre.begin(pe, 0, f"x{d}")
                for a in range(NT):
                    tr(ps[:, 0, a * P:(a + 1) * P], xtok(pj)[:, a, d * P:(d + 1) * P])
                tr(ps[:, 1, 0:NS], xstok(pj)[:, d * P:(d + 1) * P]).then_inc(pre_s, 1)

            def sumsq(chain, name, src, weights):
                chain.begin(pe, 0, name)
                for h in range(2):
                    for k, s in enumerate(src):
                        last = mm(ps[:, 4 + h, 0:HN], weights, s[:, h * HN:(h + 1) * HN], k == 0, k == len(src) - 1)
                last.then_inc(chain.sem, 1)

            sumsq(pre, "ss1", [hT[:, k, :] for k in range(KD)], ones)

            def ada_chunk(out, slot, c):
                for k in range(KD):
                    last = mm(out, ring[:, slot, k * 256 + c * P:k * 256 + (c + 1) * P], cT[:, k, :], k == 0, k == KD - 1)
                return last

            pre.begin(pe, 0, "ada1")
            for idx in range(counts["ada1"]):
                landed(pe, idx % R, idx)
                for c in range(2):
                    last = ada_chunk(ps[:, 7, (2 * idx + c) * 9:(2 * idx + c + 1) * 9], idx % R, c)
                last.then_inc(w_used, 1)
            pe.drain().then_inc(pre_s, 1)
            pre.after(pe, 0, "norm1")

            def gemm_tile(pair, weights, src, sems):
                for h in range(2):
                    for k, (w, s) in enumerate(zip(weights, src)):
                        last = mm(ps[:, pair + h, 0:HN], w, s[:, h * HN:(h + 1) * HN], k == 0, k == len(src) - 1)
                last.then_inc(sems, 1)
                return last

            hs = [hT[:, k, :] for k in range(KD)]

            def unit_part(u, part_):
                if part_ == 0 and u >= 2:
                    pe.wait_ge(x_read, u - 1)
                if u < U_MIX or u >= U_MIX + U_ADA:
                    v, kind = (u, "mixer") if u < U_MIX else (u - U_MIX - U_ADA, "gate")
                    n, c, h = first[kind] + v // 4, v // 2 % 2, v % 2
                    if part_ == 0:
                        landed(pe, n % R, n)
                    for k in range(4 * part_, 4 * part_ + 4):
                        at = k * 256 + c * P
                        last = mm(ps[:, u % 2, 0:HN], ring[:, n % R, at:at + P], hT[:, k, h * HN:(h + 1) * HN], k == 0, k == KD - 1)
                else:
                    n = first["ada2"] + 2 * (u - U_MIX) + part_
                    landed(pe, n % R, n)
                    for c in range(2):
                        at = 9 * (2 * part_ + c)
                        last = ada_chunk(ps[:, u % 2, at:at + 9], n % R, c)
                if part_ == 1:
                    last.then_inc(x_done, 1)

            def pick(h, n):
                return ident[0:NR, h:h + 1].to_broadcast([NR, n])

            def bcast2(out, h0, step, rows):
                for q in range(2):
                    last = mm(out[half(q)], pick(h0 + step * q, DK), rows)
                return last

            def half(q):
                return slice(q * DK, (q + 1) * DK)

            def tails(feats, hist, bank, tail_at):
                for n in range(len(feats)):
                    tr(ps[:, bank + 1, 256 + n * 24:256 + (n + 1) * 24], hist[0:3 * NB, n * P:(n + 1) * P])
                for n, f in enumerate(feats):
                    last = tr(ps[0:2 * NS, bank + n // 4, (n % 4) * P:(n % 4 + 1) * P], pj[:, f, T - NS:TA])
                return last

            def gdn_pe():
                gdn.begin(pe, PRE, "g_tail")
                pe.wait_ge(x_read, units_through(GV + 1))
                pe.wait_ge(d_hist, 32)
                tails(CONV_G, g_hist, 4, 0).then_inc(gdn_s, 1)
                yield
                for n in range(4):
                    gdn.begin(pe, PRE, f"g_l2_{n}")
                    for h in range(2):
                        last = mm(ps[:, 4 + h, 0:HN], b64, part(544 * n, TA)[:, h * HN:(h + 1) * HN])
                    last.then_inc(gdn_s, 1)
                    yield
                for t in range(NT + 1):
                    w = P if t < NT else NS
                    c = slice(t * P, t * P + w)
                    v = lambda b: b[0:w, 0:4 * w].rearrange("m (h l) -> m h l", h=4)
                    T_, U_, X_, L_, D_ = v(gT), v(gU), v(gX), v(gL), v(gD)
                    f = lambda b: b[:, 0:2 * w].rearrange("k (p l) -> k p l", p=2)
                    qs, kb, sk = f(g_qs), f(g_kb), f(g_sk)
                    B0_, B1_ = ps[:, 4, :], ps[:, 5, :]
                    gdn.begin(pe, t, "g_tokens")
                    if t == 0:
                        rest.after(pe, PRE, "s_rcolc2")
                    for p in range(2):
                        tr(B0_[0:w, p * P:(p + 1) * P], pj[:, GK + p, c])
                        tr(B0_[0:w, 256 + p * P:256 + (p + 1) * P], pj[:, GV + p, c])
                    for p in range(2):
                        bcast2(B1_[:, p * w:(p + 1) * w], 2 * p, 1, Er[0:NR, c])
                        last = bcast2(B1_[:, 256 + p * w:256 + (p + 1) * w], 2 * p, 1, Vr[0:NR, c])
                    last.then_inc(gdn_s, 1)
                    yield
                    gdn.begin(pe, t, "g_bcast")
                    for q in range(2):
                        for p in range(2):
                            last = mm(B0_[0:w, (2 * q + p) * w:(2 * q + p + 1) * w], pick(2 * p + q, w), Rr[0:NR, c])
                    last.then_inc(gdn_s, 1)
                    yield
                    gdn.begin(pe, t, "g_kk")
                    for q in range(2):
                        for p in range(2):
                            last = mm(ps[0:w, 4 + q, p * w:(p + 1) * w], pj[half(q), GK + p, c], kb[half(q), p, :])
                    last.then_inc(gdn_s, 1)
                    yield
                    gdn.begin(pe, t, "g_first")
                    for h in range(4):
                        last = tr(B0_[0:w, h * w:(h + 1) * w], U_[:, h, :])
                    last.then_inc(gdn_s, 1)
                    yield
                    for n in levels_of(t)[1:]:
                        gdn.begin(pe, t, f"g_x{n}")
                        for h in range(4):
                            last = mm(B0_[0:w, h * w:(h + 1) * w], L_[:, h, :], T_[:, h, :])
                        last.then_inc(gdn_s, 1)
                        yield
                        gdn.begin(pe, t, f"g_y{n}")
                        for h in range(4):
                            mm(B0_[0:w, h * w:(h + 1) * w], U_[:, h, :], X_[:, h, :])
                        for h in range(4):
                            last = mm(B1_[0:w, h * w:(h + 1) * w], X_[:, h, :], U_[:, h, :])
                        last.then_inc(gdn_s, 1)
                        yield
                    gdn.begin(pe, t, "g_qk")
                    for q in range(2):
                        for p in range(2):
                            last = mm(ps[0:w, 4 + q, p * w:(p + 1) * w], pj[half(q), GK + p, c], pj[half(q), GQ + p, c])
                    last.then_inc(gdn_s, 1)
                    yield
                    gdn.begin(pe, t, "g_sk")
                    for q in range(2):
                        for p in range(2):
                            h = 2 * p + q
                            last = mm(B0_[half(q), p * w:(p + 1) * w], g_kn[0:w, h * DK:(h + 1) * DK], U_[:, 2 * q + p, :])
                    last.then_inc(gdn_s, 1)
                    yield
                    gdn.begin(pe, t, "g_u")
                    for q in range(2):
                        for p in range(2):
                            h, x = 2 * p + q, 2 * q + p
                            if t < NT:
                                o = ps[0:w, 4 + q, p * DK:(p + 1) * DK]
                                mm(o, U_[:, x, :], g_vb[0:w, h * DK:(h + 1) * DK], True, False)
                                last = mm(o, sk[half(q), p, :], S_g[half(q), p, :], False, True)
                            else:
                                if (p, q) == (0, 0):
                                    pe.wait_ge(d_q["gdn"], 64)
                                o = ps[half(q), 4 + q, p * w:(p + 1) * w]
                                mm(o, g_vb[0:w, h * DK:(h + 1) * DK], U_[:, x, :], True, False)
                                for b in range(NB):
                                    last = mm(o[:, ND * b:ND * b + ND], Q_g[half(q), p, b, :], sk[half(q), p, ND * b:ND * b + ND],
                                              False, b == NB - 1)
                    last.then_inc(gdn_s, 1)
                    yield
                    if t == NT:
                        gdn.begin(pe, t, "g_ut")
                        for p in range(2):
                            last = tr(B0_[0:w, p * P:(p + 1) * P], g_sk[:, p * w:(p + 1) * w])
                        last.then_inc(gdn_s, 1)
                        yield
                    gdn.begin(pe, t, "g_out")
                    for q in range(2):
                        for p in range(2):
                            h, x = 2 * p + q, 2 * q + p
                            o = ps[half(q), 4 + q, p * w:(p + 1) * w]
                            mm(o, g_u[0:w, h * DK:(h + 1) * DK], D_[:, x, :], True, False)
                            if t < NT:
                                last = mm(o, S_g[half(q), p, :], qs[half(q), p, :], False, True)
                            else:
                                for b in range(NB):
                                    last = mm(o[:, ND * b:ND * b + ND], Q_g[half(q), p, b, :], qs[half(q), p, ND * b:ND * b + ND],
                                              False, b == NB - 1)
                    if t < NT:
                        for h in range(4):
                            last = mm(B0_[half(h % 2), 256 + (h // 2) * DK:256 + (h // 2 + 1) * DK],
                                      g_kd[0:w, h * DK:(h + 1) * DK], g_u[0:w, h * DK:(h + 1) * DK])
                    last.then_inc(gdn_s, 1)
                    yield
                    if t == NT:
                        gdn.begin(pe, t, "g_state")
                        for h in range(4):
                            last = mm(ps[half(h % 2), 4 + h // 2, :], g_kd[0:w, h * DK:(h + 1) * DK],
                                      g_Ue[0:w, h * 512:(h + 1) * 512])
                        last.then_inc(gdn_s, 1)
                        yield

            def scores(t, bank, keys, queries):
                w = P if t < NT else NS
                for q in range(2):
                    for p in range(2):
                        last = mm(ps[0:w, bank + q, p * w:(p + 1) * w], keys[half(q), p, :], queries[half(q), p, :])
                return last

            def outputs(t, bank, vals, at, St, Qt, qs, col):
                w = P if t < NT else NS
                for q in range(2):
                    for p in range(2):
                        h, x = 2 * p + q, 2 * q + p
                        o = ps[half(q), bank + q, col + p * w:col + (p + 1) * w]
                        mm(o, vals(h), at[:, x, :], True, False)
                        if t < NT:
                            last = mm(o, St[half(q), p, :], qs[half(q), p, :], False, True)
                        else:
                            for b in range(NB):
                                last = mm(o[:, ND * b:ND * b + ND], Qt[half(q), p, b, :],
                                          qs[half(q), p, ND * b:ND * b + ND], False, b == NB - 1)
                return last

            def increments(kd, vals, bank, col):
                for h in range(4):
                    last = mm(ps[half(h % 2), bank, col + (h // 2) * DK:col + (h // 2 + 1) * DK],
                              kd[:, h * DK:(h + 1) * DK], vals(h))
                return last

            def q_increments(kd, Ue, bank):
                for h in range(4):
                    last = mm(ps[half(h % 2), bank + h // 2, :], kd[0:NS, h * DK:(h + 1) * DK], Ue[0:NS, h * 512:(h + 1) * 512])
                return last

            def hgrn_pe():
                hgrn.begin(pe, PRE, "h_lb3")
                for p in range(2):
                    mm(ps[:, 6, p:p + 1], hrow[0:1, p * P:(p + 1) * P], ones[0:1, 0:1])
                    last = mm(ps[:, 6, 2 + p:3 + p], hrow2[0:1, p * P:(p + 1) * P], ones[0:1, 0:1])
                last.then_inc(hgrn_s, 1)
                yield
                for t in range(NT + 1):
                    w = P if t < NT else NS
                    c = slice(t * P, t * P + w)
                    f = lambda b: b[:, 0:2 * w].rearrange("k (p l) -> k p l", p=2)
                    v = lambda b: b[0:w, 0:4 * w].rearrange("m (h l) -> m h l", h=4)
                    hgrn.begin(pe, t, "h_qk")
                    scores(t, 6, kg[:, :, c], pj[:, HQ:HQ + 2, c]).then_inc(hgrn_s, 1)
                    yield
                    for n in levels_of(t):
                        hgrn.begin(pe, t, f"h_qk{n}")
                        scores(t, 6, f(hKl), f(hQl)).then_inc(hgrn_s, 1)
                        yield
                    hgrn.begin(pe, t, "h_tok")
                    for p in range(2):
                        tr(ps[0:w, 6, p * P:(p + 1) * P], f(hEf)[:, p, :])
                        last = tr(ps[0:w, 6, 256 + p * P:256 + (p + 1) * P], pj[:, HI + p, c])
                    last.then_inc(hgrn_s, 1)
                    yield
                    hgrn.begin(pe, t, "h_out")
                    if t == NT:
                        pe.wait_ge(d_q["hgrn"], 64)
                    vals = lambda h: hV[0:w, h * DK:(h + 1) * DK]
                    last = outputs(t, 6, vals, v(hD), S_h, Q_h, f(hQ), 0)
                    if t < NT:
                        last = increments(hKd, vals, 6, 256)
                    last.then_inc(hgrn_s, 1)
                    yield
                    if t == NT:
                        hgrn.begin(pe, t, "h_state")
                        q_increments(hKd, h_Ue, 6).then_inc(hgrn_s, 1)
                        yield

            def rest_pe():
                for e, name in enumerate(("s_w_a", "s_w_b")):
                    rest.begin(pe, PRE, name)
                    pe.wait_ge(d_wsm, 80)
                    for h in range(2):
                        for k in range(KD):
                            last = mm(ps[0:NR, 2 + h, 0:HN], wsm[:, k, e, :], hT[:, k, h * HN:(h + 1) * HN], k == 0, k == KD - 1)
                    last.then_inc(rest_s, 1)
                    yield
                for n in range(3):
                    rest.begin(pe, PRE, f"s_rcol{n}")
                    for t in range(2 * n, min(2 * n + 2, NT + 1)):
                        c0, w = t * P, (P if t < NT else NS)
                        for m, src in enumerate((RS(scr), RK(scr), Vr, RN(scr))):
                            last = tr(ps[0:w, 2 + t % 2, m * NR:(m + 1) * NR], src[0:NR, c0:c0 + w])
                    last.then_inc(rest_s, 1)
                    yield
                rest.begin(pe, PRE, "s_tail")
                pe.wait_ge(x_read, units_through(SC))
                pe.wait_ge(d_hist, 32)
                tails(CONV_S, s_hist, 2, 0).then_inc(rest_s, 1)
                yield
                for t in range(NT + 1):
                    w = P if t < NT else NS
                    c = slice(t * P, t * P + w)
                    rest.begin(pe, t, "s_bcast")
                    for g in range(2):
                        for j in range(4):
                            last = mm(ps[0:w, 2 + g, j * w:(j + 1) * w], pick(R_S + 4 * g + j, w), Rr[0:NR, c])
                    last.then_inc(rest_s, 1)
                    yield
                    rest.begin(pe, t, "s_cb")
                    for g in range(2):
                        mm(ps[0:w, 2 + g, 0:w], pj[half(g), SB, c], pj[half(g), SC, c])
                    tr(ps[0:w, 2, 128:256], pj[:, SB, c])
                    for g in range(2):
                        last = tr(ps[0:w, 2, 256 + g * P:256 + (g + 1) * P], pj[:, SX + g, c])
                    last.then_inc(rest_s, 1)
                    yield
                    rest.begin(pe, t, "s_e")
                    for j in range(4):
                        last = bcast2(ps[:, 2, j * w:(j + 1) * w], R_S + j, 4, Er[0:NR, c])
                    last.then_inc(rest_s, 1)
                    yield
                    rest.begin(pe, t, "s_out")
                    if t == NT:
                        pe.wait_ge(d_q["ssd"], 128)
                    att = bD[0:w, 0:8 * w].rearrange("m (h l) -> m h l", h=8)
                    qs = bQ[:, 0:4 * w].rearrange("k (j l) -> k j l", j=4)
                    for g in range(2):
                        for j in range(4):
                            h = 4 * g + j
                            o = ps[32 * j:32 * j + 32, 2 + g, 0:w]
                            mm(o, bV[0:w, h * 32:(h + 1) * 32], att[:, h, :], True, False)
                            if t < NT:
                                last = mm(o, S_s[half(g), j, :], qs[half(g), j, :], False, True)
                            else:
                                for b in range(NB):
                                    last = mm(o[:, ND * b:ND * b + ND], Qs(Q_s)[half(g), j, b, :],
                                              qs[half(g), j, ND * b:ND * b + ND], False, b == NB - 1)
                    if t < NT:
                        for h in range(8):
                            last = mm(ps[half(h // 4), 2, 256 + (h % 4) * 32:256 + (h % 4 + 1) * 32],
                                      bKd[0:w, h * DK:(h + 1) * DK], bV[0:w, h * 32:(h + 1) * 32])
                    last.then_inc(rest_s, 1)
                    yield
                    if t == NT:
                        rest.begin(pe, t, "s_state")
                        for h in range(8):
                            j = h % 4
                            last = mm(ps[half(h // 4), 2 + j // 2, (j % 2) * 256:(j % 2 + 1) * 256],
                                      bKd[0:w, h * DK:(h + 1) * DK], b_Ue[0:w, h * 256:(h + 1) * 256])
                        last.then_inc(rest_s, 1)
                        yield
                for t in range(NT + 1):
                    w = P if t < NT else NS
                    c = slice(t * P, t * P + w)
                    f = lambda b: b[:, 0:2 * w].rearrange("k (p l) -> k p l", p=2)
                    v = lambda b: b[0:w, 0:4 * w].rearrange("m (h l) -> m h l", h=4)
                    rest.begin(pe, t, "m_tok")
                    if t == 0:
                        pe.wait_ge(x_read, units_through(MV + 1))
                    for p in range(2):
                        tr(ps[0:w, 2, p * P:(p + 1) * P], pj[:, MK + p, c])
                        tr(ps[0:w, 2, 256 + p * P:256 + (p + 1) * P], pj[:, MV + p, c])
                    for p in range(2):
                        last = bcast2(ps[:, 3, p * w:(p + 1) * w], R_M + 2 * p, 1, Er[0:NR, c])
                    last.then_inc(rest_s, 1)
                    yield
                    rest.begin(pe, t, "m_bcast")
                    for q in range(2):
                        for p in range(2):
                            last = mm(ps[0:w, 2, (2 * q + p) * w:(2 * q + p + 1) * w], pick(R_M + 2 * p + q, w), Rr[0:NR, c])
                    last.then_inc(rest_s, 1)
                    yield
                    rest.begin(pe, t, "m_qk")
                    scores(t, 2, pj[:, MK:MK + 2, c], pj[:, MQ:MQ + 2, c]).then_inc(rest_s, 1)
                    yield
                    rest.begin(pe, t, "m_out")
                    if t == NT:
                        pe.wait_ge(d_q["mlstm"], 128)
                    vals = lambda h: bV[0:w, h * DK:(h + 1) * DK]
                    on = lambda h: ones[0:w, 0:DK]
                    outputs(t, 2, vals, v(bD), S_c, Q_c, f(bQ), 0)
                    outputs(t, 2, on, v(bD), S_n, Q_n, f(bQ), 256).then_inc(rest_s, 1)
                    yield
                    rest.begin(pe, t, "m_den")
                    for p in range(2):
                        last = bcast2(ps[:, 2, p * w:(p + 1) * w], R_M + 2 * p, 1, Vr[0:NR, c])
                    if t < NT:
                        increments(bKd, vals, 3, 0)
                        last = increments(bKd, on, 3, 128)
                    last.then_inc(rest_s, 1)
                    yield
                    if t == NT:
                        for name in ("m_state", "m_norm"):
                            rest.begin(pe, t, name)
                            q_increments(bKd, b_Ue, 2).then_inc(rest_s, 1)
                            yield

            gens = {"g": gdn_pe(), "h": hgrn_pe(), "s": rest_pe()}
            for chain, t, name, engine in order:
                if engine == "pe" and chain == "x":
                    unit_part(t, int(name[-1]))
                elif engine == "pe":
                    next(gens[chain])

            for n in range(4):
                mid.begin(pe, 0, f"o_ss{n}")
                for f in range(2):
                    for h in range(2):
                        last = mm(ps[:, 4 + 2 * f + h, 0:HN], ones if n == 2 else b64, rstd2(scr)[:, f, h * HN:(h + 1) * HN])
                last.then_inc(mid_s, 1)
            mid.begin(pe, 0, "up")
            pe.wait_ge(d_wb, 32)
            for k in range(32):
                d, n = k // 4, k % 4
                if k >= 4:
                    pe.wait_ge(lin_read, k - 3)
                for h in range(2):
                    for kk in range(2):
                        last = mm(ps[:, 2 * (k % 4) + h, 0:HN], wb(scr)[:, 2 * n + kk, d * P:(d + 1) * P],
                                  pj[:, BR[2 * n + kk], h * HN:(h + 1) * HN], kk == 0, kk == 1)
                last.then_inc(lin_done, 1)
            pe.drain().then_inc(mid_s, 1)

            mid.begin(pe, 0, "wout")
            ms = [merged_t(pj, k) for k in range(KD)]

            def wout(slot, idx, n):
                landed(pe, slot, n)
                for c in range(2):
                    if idx >= 1:
                        pe.wait_ge(tile_read, tiles_before["wout"] + 2 * idx + c - 1)
                    gemm_tile(2 * c, [ring[:, slot, k * 256 + c * P:k * 256 + (c + 1) * P] for k in range(KD)], ms, tile_done)
            for idx in range(counts["wout"]):
                n = first["wout"] + idx
                wout(n % R, idx, n)
            pe.drain().then_inc(mid_s, 1)
            sumsq(mid, "ss2", hs, ones)
            mid.begin(pe, 0, "ffa")

            def ffa(slot, idx, n, par):
                landed(pe, slot, n)
                if not isinstance(idx, int) or idx >= 2:
                    pe.wait_ge(tile_read, idx + (tiles_before["ffa"] - 1))
                    pe.wait_ge(lin_read, idx + (32 - 1))
                gemm_tile(2 * par, [ring[:, slot, k * 256:k * 256 + P] for k in range(KD)], hs, tile_done)
                gemm_tile(4 + 2 * par, [ring[:, slot, k * 256 + P:k * 256 + 2 * P] for k in range(KD)], hs, lin_done)
            for idx in range(2):
                n = first["ffa"] + idx
                ffa(n % R, idx, n, idx % 2)
            with pe.Fori(0, 5) as i:
                for r in range(R):
                    ffa((first["ffa"] + 2 + r) % R, i * R + (2 + r), i * R + (first["ffa"] + 2 + r), r % 2)
            pe.drain().then_inc(mid_s, 1)

            mid.begin(pe, 0, "ffb")

            def ffb(d, n, par, first_tile):
                if not first_tile:
                    pe.wait_ge(tile_read, d + (tiles_before["ffb"] - 1))
                for e in range(2):
                    slot = (first["ffb"] + 2 * par + e) % R
                    landed(pe, slot, n + e)
                    for h in range(2):
                        for k in range(11):
                            last = mm(ps[:, 2 * par + h, 0:HN], ring[:, slot, k * P:(k + 1) * P],
                                      pj[:, 8 + 11 * e + k, h * HN:(h + 1) * HN], e == 0 and k == 0, e == 1 and k == 10)
                    last.then_inc(tile_done if e == 1 else half_used, 1)
            for d in range(2):
                ffb(d, first["ffb"] + 2 * d, d % 2, True)
            with pe.Fori(0, 3) as i:
                for r in range(2):
                    ffb(i * 2 + (2 + r), i * 4 + (first["ffb"] + 4 + 2 * r), r, False)
            pe.drain().then_inc(mid_s, 1)
            sumsq(mid, "ss3", hs, ones)
            for t in range(NT + 1):
                w = P if t < NT else NS
                mid.begin(pe, 0, f"y{t}")
                for k in range(KD):
                    last = tr(ps[0:w, k // 4, (k % 4) * P:(k % 4 + 1) * P], hT[:, k, t * P:t * P + w])
                last.then_inc(mid_s, 1)

        @block.scalar
        def _(act):
            pre.begin(act, 0, "silc")
            act.wait_ge(d_c, 32)
            act.activation(ctok(pj)[0:NB + 1, :], ctok(pj)[0:NB + 1, :], ACT.Silu).then_inc(pre_s, 1)
            for d in range(KD):
                pre.begin(act, 0, f"xc{d}")
                act.activation(xT0[:, d, 0:T], ps[:, 0, :], ACT.Copy)
                act.activation(xT0[:, d, T:TA], ps[:, 1, 0:NS], ACT.Copy)
                act.drain().then_inc(pre_s, 1)

            def rsqrt(chain, name, dst, src, scale):
                chain.begin(act, 0, name)
                act.wait_ge(zeroed, 2)
                act.activation(dst, src, ACT.Ln, scale=scale, bias=colp[:, 3:4])
                act.drain()
                act.activation(dst, dst, ACT.Exp, scale=-0.5)
                act.drain().then_inc(chain.sem, 1)

            two = lambda b: b.rearrange("p (h n) -> p h n", h=2)
            rsqrt(pre, "rs1", two(rstd[:, :]), ps[:, 4:6, 0:HN], 1.0 / D)

            def read_unit(u):
                act.wait_ge(x_done, u + 1)
                if u < U_MIX:
                    f, h = 2 * MIX_ORDER[u // 4] + u // 2 % 2, u % 2
                    act.activation(pj[:, f, h * HN:(h + 1) * HN], ps[:, u % 2, 0:HN], ACT.Copy).then_inc(x_read, 1)
                elif u < U_MIX + U_ADA:
                    c0 = 16 + 4 * (u - U_MIX)
                    act.activation(mod[:, c0:c0 + 4, :].rearrange("p c b -> p (c b)"), ps[:, u % 2, 0:36], ACT.Copy).then_inc(x_read, 1)
                else:
                    v = u - U_MIX - U_ADA
                    if v >= 2:
                        act.wait_ge(g_out[v % 2], 16 * (v // 2))
                    act.activation(rstd[:, (v % 2) * HN:(v % 2 + 1) * HN], ps[:, u % 2, 0:HN], ACT.Copy).then_inc(x_read, 1)

            def gdn_act():
                for n, f in enumerate(CONV_G):
                    gdn.begin(act, PRE, f"g_silu{n}")
                    act.activation(pj[:, f, :], g_acc[:, 544 * (n % 2):544 * (n % 2 + 1)], ACT.Silu).then_inc(gdn_s, 1)
                    yield
                for n in range(4):
                    gdn.begin(act, PRE, f"g_l2r{n}")
                    x = part(2176 + 544 * n, TA)
                    act.activation(two(x), ps[:, 4:6, 0:HN], ACT.Ln, bias=colp[:, 3:4])
                    act.drain()
                    act.activation(x, x, ACT.Exp, scale=-0.5).then_inc(gdn_s, 1)
                    yield
                for t in range(NT + 1):
                    w = P if t < NT else NS
                    gdn.begin(act, t, "g_decay")
                    act.activation(gD[0:w, 0:4 * w], gD[0:w, 0:4 * w], ACT.Exp).then_inc(gdn_s, 1)
                    yield
                    gdn.begin(act, t, "g_t1")
                    act.activation(gT[0:w, 0:4 * w], ps[0:w, 4, 0:4 * w], ACT.Copy).then_inc(gdn_s, 1)
                    yield
                    for n in levels_of(t)[1:]:
                        gdn.begin(act, t, f"g_xc{n}")
                        act.activation(gX[0:w, 0:4 * w], ps[0:w, 4, 0:4 * w], ACT.Copy).then_inc(gdn_s, 1)
                        yield
                    gdn.begin(act, t, "g_skc")
                    act.activation(g_sk[:, 0:2 * w], ps[:, 4, 0:2 * w], ACT.Copy).then_inc(gdn_s, 1)
                    yield

            def hgrn_act():
                hgrn.begin(act, PRE, "h_lb1")
                act.activation(hrow[0:1, 0:256], hrow[0:1, 0:256], ACT.Exp).then_inc(hgrn_s, 1)
                yield
                hgrn.begin(act, PRE, "h_lb5")
                act.activation(hcol[:, :, 3:5], hcol[:, :, 3:5], ACT.Ln).then_inc(hgrn_s, 1)
                yield
                hgrn.begin(act, PRE, "h_silu")
                act.wait_ge(x_read, units_through(HI + 1))
                rest.after(act, PRE, "s_w_b")
                for m in range(2):
                    act.activation(kg[:, m, :], pj[:, HF + m, :], ACT.Sigmoid, scale=-1.0)
                for m in range(2):
                    act.activation(pj[:, HQ + m, :], pj[:, HQ + m, :], ACT.Silu)
                act.drain().then_inc(hgrn_s, 1)
                yield
                a_, b_ = part(C0, TA), part(C0 + 544, TA)
                for f in range(2):
                    for name, x, src in ((f"h_ls{f}", a_, pj[:, HF + f, :]), (f"h_ln{f}", b_, b_)):
                        hgrn.begin(act, PRE, name)
                        act.activation(x, src, ACT.Abs)
                        act.drain()
                        act.activation(x, x, ACT.Exp, scale=-1.0)
                        act.drain()
                        act.activation(x, x, ACT.Ln, bias=1.0).then_inc(hgrn_s, 1)
                        yield
                for t in range(NT + 1):
                    w = P if t < NT else NS
                    for n in levels_of(t):
                        hgrn.begin(act, t, f"h_dec{n}")
                        act.activation(hEf[:, 0:2 * w], hEf[:, 0:2 * w], ACT.Abs)
                        act.drain()
                        act.activation(hEf[:, 0:2 * w], hEf[:, 0:2 * w], ACT.Exp, scale=-1.0).then_inc(hgrn_s, 1)
                        yield
                    hgrn.begin(act, t, "h_dec")
                    act.activation(hQ[:, 0:2 * w].rearrange("k (p l) -> k p l", p=2), pj[:, HF:HF + 2, t * P:t * P + w], ACT.Exp)
                    act.activation(hEf[:, 0:2 * w], hEf[:, 0:2 * w], ACT.Exp)
                    act.drain().then_inc(hgrn_s, 1)
                    yield

            def rest_act():
                rest.begin(act, PRE, "s_rb")
                act.wait_ge(d_row, 96)
                z, e, ln = (rowbuf(scr, n) for n in range(3))
                act.activation(two(Vr[0:32, :]), ps[0:32, 2:4, 0:HN], ACT.Sigmoid)
                act.activation(e, z, ACT.Abs)
                act.activation(colp[0:NR, 1:2], colp[0:NR, 1:2], ACT.Exp)
                act.drain()
                act.activation(e, e, ACT.Exp, scale=-1.0)
                act.drain()
                act.activation(ln, e, ACT.Ln, bias=1.0)
                act.drain().then_inc(rest_s, 1)
                yield
                rest.begin(act, PRE, "s_rexp")
                act.activation(Er[0:NR, :], Er[0:NR, :], ACT.Exp)
                act.activation(RK(scr), RK(scr), ACT.Exp)
                act.activation(Vr[R_M:NR, :], MTr[R_M:NR, :], ACT.Exp, scale=-1.0)
                act.drain().then_inc(rest_s, 1)
                yield
                for n, f in enumerate(CONV_S):
                    rest.begin(act, PRE, f"s_silu{n}")
                    act.activation(pj[:, f, :], s_acc[:, 544 * (n % 2):544 * (n % 2 + 1)], ACT.Silu).then_inc(rest_s, 1)
                    yield
                for name, n in (("s_decay", 8), ("m_decay", 4)):
                    for t in range(NT + 1):
                        w = P if t < NT else NS
                        rest.begin(act, t, name)
                        act.activation(bD[0:w, 0:n * w], bD[0:w, 0:n * w], ACT.Exp).then_inc(rest_s, 1)
                        yield

            gens = {"g": gdn_act(), "h": hgrn_act(), "s": rest_act()}
            for chain, t, name, engine in order:
                if engine == "act" and chain == "x":
                    read_unit(t)
                elif engine == "act":
                    next(gens[chain])
            mid.begin(act, 0, "silus")
            for m in (GZ, GZ + 1, HG, HG + 1, SZ, SZ + 1):
                act.activation(pj[:, m, :], pj[:, m, :], ACT.Silu)
            for m in (MO, MO + 1):
                act.activation(pj[:, m, :], pj[:, m, :], ACT.Sigmoid)
            act.drain().then_inc(mid_s, 1)
            for n in range(4):
                mid.begin(act, 0, f"o_rs{n}")
                for f in range(2):
                    act.activation(two(rstd2(scr)[:, f, :]), ps[:, 4 + 2 * f:6 + 2 * f, 0:HN], ACT.Ln,
                                   scale=1.0 / (P if n == 2 else DK), bias=colp[:, 3:4])
                act.drain()
                for f in range(2):
                    act.activation(rstd2(scr)[:, f, :], rstd2(scr)[:, f, :], ACT.Exp, scale=-0.5)
                act.drain().then_inc(mid_s, 1)

            for k in range(32):
                act.wait_ge(g_in[k % 4], 16 * (k // 4 + 1))
                act.activation(gbuf(pj)[:, k % 4, :], gbuf(pj)[:, k % 4, :], ACT.Sigmoid).then_inc(gate_ready, 1)
            rsqrt(mid, "rs2", two(rstd[:, :]), ps[:, 4:6, 0:HN], 1.0 / D)

            def ff_silu(i, e):
                act.wait_ge(tile_done, i * 2 + (tiles_before["ffa"] + e + 1))
                act.wait_ge(lin_read, i * 2 + (32 + e - 1))
                act.activation(two(fbuf(scr)[:, e, :]), ps[:, 2 * e:2 * e + 2, 0:HN], ACT.Silu).then_inc(tile_read, 1)
            with act.Fori(0, 11) as i:
                for e in range(2):
                    ff_silu(i, e)
            rsqrt(mid, "rs3", two(rstd[:, :]), ps[:, 4:6, 0:HN], 1.0 / D)
            for t in range(NT + 1):
                w = P if t < NT else NS
                mid.begin(act, 0, f"yc{t}")
                for h in range(2):
                    act.activation(ytok(pj, t)[:, h * 512:(h + 1) * 512], ps[0:w, h, :], ACT.Copy)
                act.drain().then_inc(mid_s, 1)

        @block.vector
        def _(dve):
            MUL, ADD, SUB = ALU.mult, ALU.add, ALU.subtract

            def tt(out, a, b, op):
                r = dve.tensor_tensor(out, a, b, op)
                dve.drain()
                return r

            def ts(out, a, s1, s2, op0, op1=None):
                r = dve.tensor_scalar(out, a, s1, s2, op0, *([op1] if op1 is not None else []))
                dve.drain()
                return r

            def stt(out, a, s, b, op0, op1):
                r = dve.scalar_tensor_tensor(out=out, in0=a, scalar=s, in1=b, op0=op0, op1=op1)
                dve.drain()
                return r

            def cp(out, a):
                r = dve.tensor_copy(out, a)
                dve.drain()
                return r

            def done(chain):
                dve.drain().then_inc(chain.sem, 1)

            dve.wait_ge(zeroed, 1)
            dve.memset(colp[:, 3:4], EPS)
            for b in (MTr, Vr):
                dve.memset(b[:, :], 0.0)
            dve.memset(hrow[64:96, :], 0.0)
            dve.drain().then_inc(zeroed, 1)
            pre.begin(dve, 0, "vecc")
            cp(vt[:, :], ps[:, 4, 0:V_2])
            done(pre)
            pre.begin(dve, 0, "ctc")
            cp(cT[:, :, :].rearrange("p k b -> p (k b)"), ps[:, 5, 0:KD * (NB + 1)])
            done(pre)

            def squares(chain, name, x):
                chain.begin(dve, 0, name)
                for k in range(KD):
                    dve.tensor_tensor(hT[:, k, :], x[:, k, :], x[:, k, :], MUL)
                done(chain)

            squares(pre, "sq1", xT0)
            def ada_bias(c0, c1):
                return vt[:, V_ADAB + c0:V_ADAB + c1].unsqueeze(2).to_broadcast([P, c1 - c0, 9])

            pre.begin(dve, 0, "mod1")
            tt(mod[:, 0:16, :], ps[:, 7, 0:144].rearrange("p (c b) -> p c b", b=9), ada_bias(0, 16), ADD)
            done(pre)

            def modulate(chain, name, x, w0, c0):
                chain.begin(dve, 0, name)
                ts(coef[:, :, :], mod[:, c0 + KD:c0 + 2 * KD, :], 1.0, None, ADD)
                tt(coef[:, :, :], coef[:, :, :], vt[:, w0:w0 + KD].unsqueeze(2).to_broadcast([P, KD, 9]), MUL)
                for k in range(KD):
                    dve.tensor_tensor(hT[:, k, :], x[:, k, :], rstd[:, :], MUL)
                dve.drain()
                for k in range(KD):
                    s = hT[:, k, T:TA].rearrange("p (b t) -> p b t", t=ND)
                    sc = coef[:, k, 1:9].unsqueeze(2).to_broadcast([P, NB, ND])
                    sh = mod[:, c0 + k, 1:9].unsqueeze(2).to_broadcast([P, NB, ND])
                    dve.tensor_scalar(hT[:, k, 0:T], hT[:, k, 0:T], coef[:, k, 0:1], mod[:, c0 + k, 0:1], MUL, ADD)
                    tt(s, s, sc, MUL)
                    dve.tensor_tensor(s, s, sh, ADD)
                done(chain)

            modulate(pre, "norm1", xT0, V_N1, 0)
            def tail_copies(feats, bank, tl, spad):
                n = len(feats)
                for b in range(0, n, 4):
                    wd = P * min(4, n - b)
                    dve.tensor_copy(tl[0:2 * NS, b * P:b * P + wd], ps[0:2 * NS, bank + b // 4, 0:wd])
                sp7 = spad.rearrange("p (f b k) -> p f b k", f=n, k=7)
                dve.tensor_copy(sp7[:, :, :, 0:3], ps[:, bank + 1, 256:256 + 24 * n].rearrange("p (f b k) -> p f b k", f=n, k=3))
                for m, f in enumerate(feats):
                    dve.tensor_copy(sp7[:, m, :, 3:7], pj[:, f, T:TA].rearrange("p (b t) -> p b t", t=ND))

            def conv(f, acc, hist7, w_, b_):
                sa = acc[:, T:TA].rearrange("p (b t) -> p b t", t=ND)
                dve.tensor_scalar(acc[:, 0:T], pj[:, f, 0:T], w_[3], b_, MUL, ADD)
                ts(sa, hist7[:, :, 3:7], w_[3], b_, MUL, ADD)
                for k in (2, 1, 0):
                    d = 3 - k
                    dve.scalar_tensor_tensor(out=acc[:, d:T], in0=pj[:, f, 0:T - d], scalar=w_[k], in1=acc[:, d:T], op0=MUL, op1=ADD)
                    stt(sa, hist7[:, :, k:k + 4], w_[k], sa, MUL, ADD)

            two = lambda b: b.rearrange("p (h n) -> p h n", h=2)

            def gdn_pre():
                gdn.begin(dve, PRE, "g_tailc")
                tail_copies(CONV_G, 4, g_tail, g_spad)
                done(gdn)
                yield
                for n, f in enumerate(CONV_G):
                    gdn.begin(dve, PRE, f"g_conv{n}")
                    conv(f, g_acc[:, 544 * (n % 2):544 * (n % 2 + 1)], g_spad.rearrange("p (f b k) -> p f b k", f=6, k=7)[:, n],
                         [vt[:, V_GCW + k * 6 + n:V_GCW + k * 6 + n + 1] for k in range(4)], vt[:, V_GCB + n:V_GCB + n + 1])
                    done(gdn)
                    yield
                gdn.begin(dve, PRE, "g_l2sq")
                dve.wait_ge(d_tail_g, 9 * 16)
                for n, f in enumerate((GQ, GQ + 1, GK, GK + 1)):
                    dve.tensor_tensor(part(544 * n, TA), pj[:, f, :], pj[:, f, :], MUL)
                done(gdn)
                yield
                gdn.begin(dve, PRE, "g_l2m")
                for n, f in enumerate((GQ, GQ + 1, GK, GK + 1)):
                    dve.scalar_tensor_tensor(out=pj[:, f, :], in0=pj[:, f, :], scalar=DK ** -0.5 if n < 2 else 1.0,
                                             in1=part(2176 + 544 * n, TA), op0=MUL, op1=MUL)
                done(gdn)
                yield

            def rest_pre():
                z, e, ln, t1, t2 = (rowbuf(scr, n) for n in range(5))
                rs, rk, rn = RS(scr), RK(scr), RN(scr)
                rest.begin(dve, PRE, "s_rz")
                dve.wait_ge(d_row, 96)
                ts(two(z), ps[0:NR, 2:4, 0:HN], colp[0:NR, 0:1], cst[0:NR, K_SGN:K_SGN + 1], ADD, MUL)
                done(rest)
                yield
                rest.begin(dve, PRE, "s_ri")
                dve.wait_ge(d_st, 16)
                ts(t1, e, 1.0, 1.0, ADD, SUB)
                tt(t1, e, t1, SUB)
                tt(ln, ln, t1, ADD)
                stt(z, z, 0.0, ln, ALU.max, ADD)
                cp(Vr[32:64, :], z[32:64, :])
                ts(colp[0:NR, 1:2], colp[0:NR, 1:2], -1.0, None, MUL)
                ts(t1, z, colp[0:NR, 1:2], None, MUL)
                dve.tensor_tensor_scan(Rr[0:NR, :], cst[0:NR, K_RST:K_RST + TA], t1, 0.0, MUL, ADD)
                m4 = slice(R_M, R_M + 4)
                iv = t2
                ts(two(iv[R_M:NR, :]), ps[R_M:NR, 2:4, 0:HN], colp[R_M:NR, 2:3], None, ADD)
                dve.tensor_tensor_scan(MTr[m4, 0:T], t1[m4, 0:T], iv[m4, 0:T], 0.0, ADD, ALU.max)
                isq = hrow[m4, 0:40].rearrange("p (b t) -> p b t", t=5)
                fsq = hrow[m4, 40:80].rearrange("p (b t) -> p b t", t=5)
                osq = hrow[m4, 80:120]
                cp(isq[:, :, 1:5], iv[m4, T:TA].rearrange("p (b t) -> p b t", t=ND))
                dve.memset(fsq, -BIG)
                dve.drain()
                cp(fsq[:, :, 1:5], t1[m4, T:TA].rearrange("p (b t) -> p b t", t=ND))
                dve.tensor_tensor_scan(osq, hrow[m4, 40:80], hrow[m4, 0:40], 0.0, ADD, ALU.max)
                mp = ln
                dve.memset(mp, 0.0)
                dve.drain()
                cp(MTr[m4, T:TA].rearrange("p (b t) -> p b t", t=ND), osq.rearrange("p (b t) -> p b t", t=5)[:, :, 1:5])
                for t in range(1, NT):
                    dve.tensor_copy(mp[m4, t * P:(t + 1) * P], MTr[m4, t * P - 1:t * P].to_broadcast([4, P]))
                dve.tensor_copy(mp[m4, T:TA].rearrange("p (b t) -> p b t", t=ND), isq[:, :, 0:1].to_broadcast([4, NB, ND]))
                cp(rs, Rr[0:NR, :])
                tt(rs[m4, :], Rr[m4, :], iv[m4, :], SUB)
                tt(Rr[m4, :], Rr[m4, :], MTr[m4, :], SUB)
                tt(Er[0:NR, :], Rr[0:NR, :], mp, ADD)
                for c0, n, l in ((0, NT, P), (T, NB, ND)):
                    v = lambda b: b[0:NR, c0:c0 + n * l].rearrange("p (n l) -> p n l", l=l)
                    dve.tensor_tensor(v(rk), v(Rr)[:, :, l - 1:l].to_broadcast([NR, n, l]), v(rs), SUB)
                done(rest)
                yield
                rest.begin(dve, PRE, "s_rv")
                ts(Vr[R_M:NR, :], Vr[R_M:NR, :], 1e38, None, ALU.min)
                stt(rn, Vr[0:NR, :], -1.0, Er[0:NR, :], MUL, MUL)
                done(rest)
                yield
                for n in range(3):
                    rest.begin(dve, PRE, f"s_rcolc{n}")
                    for t in range(2 * n, min(2 * n + 2, NT + 1)):
                        w = P if t < NT else NS
                        for r0, c0, m in ((R_G, T_G, 4), (R_S, T_S, 8), (R_M, T_M, 4)):
                            dve.tensor_copy(cols[0:w, t, :, c0:c0 + m], ps[0:w, 2 + t % 2, 0:4 * NR].rearrange("p (k r) -> p k r", k=4)[:, :, r0:r0 + m])
                    done(rest)
                    yield
                rest.begin(dve, PRE, "s_tailc")
                tail_copies(CONV_S, 2, s_tail, s_spad)
                done(rest)
                yield
                for n, f in enumerate(CONV_S):
                    rest.begin(dve, PRE, f"s_conv{n}")
                    conv(f, s_acc[:, 544 * (n % 2):544 * (n % 2 + 1)], s_spad.rearrange("p (f b k) -> p f b k", f=4, k=7)[:, n],
                         [vt[:, V_SCW + k * 4 + n:V_SCW + k * 4 + n + 1] for k in range(4)], vt[:, V_SCB + n:V_SCB + n + 1])
                    done(rest)
                    yield

            def hgrn_pre():
                hgrn.begin(dve, PRE, "h_lb0")
                tt(hrow[0:1, 0:256], hrow[0:1, 0:256], hrow[0:1, 0:256], SUB)
                done(hgrn)
                yield
                hgrn.begin(dve, PRE, "h_lb2")
                rest.after(dve, PRE, "s_w_b")
                dve.tensor_copy(hrow2[0:1, 0:256].rearrange("o (h v) -> o h v", v=32), hrow[0:1, 256:264].unsqueeze(2).to_broadcast([1, 8, 32]))
                dve.reciprocal(hrow2[0:1, 256:512], hrow[0:1, 0:256])
                dve.drain()
                tt(hrow[0:1, 0:256], hrow[0:1, 0:256], hrow2[0:1, 256:512], MUL)
                tt(hrow[0:1, 0:256], hrow[0:1, 0:256], hrow[0:1, 0:256], SUB)
                done(hgrn)
                yield
                hgrn.begin(dve, PRE, "h_lb4")
                lbc = hcol[:, :, 0]
                cp(lbc, ps[:, 6, 0:2])
                cp(dcol[:, :], ps[:, 6, 2:4])
                ts(hcol[:, :, 1], lbc, -1.0, 1.0, MUL, ADD)
                ts(hcol[:, :, 2], lbc, 0.0, None, ALU.is_gt)
                ts(hcol[:, :, 3], lbc, 2.0 ** -60, None, ALU.max)
                ts(hcol[:, :, 4], hcol[:, :, 1], 2.0 ** -60, None, ALU.max)
                done(hgrn)
                yield
                hgrn.begin(dve, PRE, "h_lb6")
                tt(hcol[:, :, 3], hcol[:, :, 3], hcol[:, :, 2], MUL)
                ts(hcol[:, :, 5], hcol[:, :, 2], BIG, -BIG, MUL, ADD)
                tt(hcol[:, :, 3], hcol[:, :, 3], hcol[:, :, 5], ADD)
                for f in range(2):
                    dve.tensor_scalar(kg[:, f, :], kg[:, f, :], hcol[:, f, 1:2], None, MUL)
                done(hgrn)
                yield
                a_, b_ = part(C0, TA), part(C0 + 544, TA)
                for f in range(2):
                    fz = pj[:, HF + f, :]
                    hgrn.begin(dve, PRE, f"h_b{f}")
                    stt(a_, fz, 0.0, a_, ALU.min, SUB)
                    ts(a_, a_, hcol[:, f, 4:5], None, ADD)
                    ts(b_, a_, hcol[:, f, 3:4], None, SUB)
                    done(hgrn)
                    yield
                    hgrn.begin(dve, PRE, f"h_g{f}")
                    ts(a_, a_, hcol[:, f, 3:4], None, ALU.max)
                    tt(a_, a_, b_, ADD)
                    dve.tensor_tensor_scan(pj[:, HF + f, :], cst[:, K_RST:K_RST + TA], a_, 0.0, MUL, ADD)
                    done(hgrn)
                    yield

            def col(t, kind, row, n, w, width):
                return cols[0:w, t, kind, row:row + n].unsqueeze(2).to_broadcast([w, n, width])

            def half(q):
                return slice(q * DK, (q + 1) * DK)

            def decays(t, w, D_, bank, row, chain):
                for q in range(2):
                    dve.tensor_tensor(D_[:, 2 * q:2 * q + 2, :], ps[0:w, bank, 2 * q * w:(2 * q + 2) * w].rearrange("m (p l) -> m p l", p=2),
                                      cols[0:w, t, 0, row + q:row + q + 3:2].unsqueeze(2).to_broadcast([w, 2, w]), SUB)
                dve.drain()
                dve.tensor_tensor(D_, D_, neg(t).unsqueeze(1).to_broadcast([w, 4, w]), ADD).then_inc(chain.sem, 1)

            def keep_last(dst, src, t, w, n):
                if t < NT:
                    dve.tensor_copy(dst[:, 0:n, 0:1], src[:, :, w - 1:w])
                else:
                    dve.tensor_copy(dst[:, 0:n, :], src[:, :, ND - 1:w:ND])

            def spread(dst, src, n, v):
                own = cst[0:NS, K_OWN:K_OWN + NB].unsqueeze(2).to_broadcast([NS, NB, v])
                for h in range(n):
                    dve.tensor_tensor(dst[0:NS, h * NB * v:(h + 1) * NB * v].rearrange("m (b v) -> m b v", b=NB),
                                      src(h).unsqueeze(1).to_broadcast([NS, NB, v]), own, MUL)

            def grow(S, e, inc, shape, chain):
                tt(S, S, e, MUL)
                dve.tensor_tensor(S, S, inc, ADD)

            def gdn_dve():
                yield from gdn_pre()
                for t in range(NT + 1):
                    w = P if t < NT else NS
                    c = slice(t * P, t * P + w)
                    v = lambda b: b[0:w, 0:4 * w].rearrange("m (h l) -> m h l", h=4)
                    U_, L_, D_, A_ = v(gU), v(gL), v(gD), v(gAt)
                    f = lambda b: b[:, 0:2 * w].rearrange("k (p l) -> k p l", p=2)
                    tok = lambda b: b[0:w, 0:256].rearrange("m (h v) -> m h v", h=4)
                    m4_ = lambda n: mask(n, w).unsqueeze(1).to_broadcast([w, 4, w])
                    gdn.begin(dve, t, "g_scale")
                    ktok, vtok = (ps[0:w, 4, o:o + 256].rearrange("m (h v) -> m h v", h=4) for o in (0, 256))
                    dve.tensor_tensor(tok(g_vb), vtok, col(t, 2, T_G, 4, w, DK), MUL)
                    dve.tensor_tensor(tok(g_kn), ktok, col(t, 3, T_G, 4, w, DK), MUL)
                    dve.tensor_tensor(tok(g_kd), ktok, col(t, 1, T_G, 4, w, DK), MUL)
                    Eb = ps[:, 5, 0:2 * w].rearrange("k (p l) -> k p l", p=2)
                    Bb = ps[:, 5, 256:256 + 2 * w].rearrange("k (p l) -> k p l", p=2)
                    dve.tensor_tensor(f(g_qs), pj[:, GQ:GQ + 2, c], Eb, MUL)
                    keep_last(eG, Eb, t, w, 2)
                    dve.tensor_tensor(f(g_kb), pj[:, GK:GK + 2, c], Bb, MUL)
                    done(gdn)
                    yield
                    gdn.begin(dve, t, "g_diff")
                    decays(t, w, D_, 4, T_G, gdn)
                    yield
                    gdn.begin(dve, t, "g_lower")
                    tt(gAt[0:w, 0:4 * w].rearrange("m (q x) -> m q x", q=2), ps[0:w, 4:6, 0:2 * w],
                       gD[0:w, 0:4 * w].rearrange("m (q x) -> m q x", q=2), MUL)
                    dve.tensor_tensor(U_, A_, m4_(0), MUL)
                    tt(L_, A_, m4_(1), MUL)
                    tt(U_, ident[0:w, 0:w].unsqueeze(1).to_broadcast([w, 4, w]), U_, SUB)
                    done(gdn)
                    yield
                    lv = levels_of(t)
                    for n in lv[1:]:
                        gdn.begin(dve, t, f"g_upd{n}")
                        dve.tensor_tensor(gU[0:w, 0:4 * w], gU[0:w, 0:4 * w], ps[0:w, 5, 0:4 * w], SUB)
                        if n != lv[-1]:
                            dve.tensor_tensor(gT[0:w, 0:4 * w], gT[0:w, 0:4 * w], ps[0:w, 4, 0:4 * w], SUB)
                            dve.tensor_tensor(L_, A_, m4_(n + 1), MUL)
                        done(gdn)
                        yield
                    gdn.begin(dve, t, "g_aq")
                    D2 = gD[0:w, 0:4 * w].rearrange("m (q x) -> m q x", q=2)
                    dve.tensor_tensor(D2, ps[0:w, 4:6, 0:2 * w], D2, MUL).then_inc(gdn_s, 1)
                    yield
                    gdn.begin(dve, t, "g_uc")
                    if t < NT:
                        ut = g_u[0:w, 0:256].rearrange("m (p q v) -> m q p v", p=2, q=2)
                        for q in range(2):
                            dve.tensor_copy(ut[:, q], ps[0:w, 4 + q, 0:2 * DK].rearrange("m (p v) -> m p v", p=2))
                        done(gdn)
                        yield
                    else:
                        for q in range(2):
                            dve.tensor_copy(g_sk[half(q), 0:2 * w], ps[half(q), 4 + q, 0:2 * w])
                        done(gdn)
                        yield
                        gdn.begin(dve, t, "g_utc")
                        cp(g_u[0:w, 0:256], ps[0:w, 4, 0:256])
                        spread(g_Ue, lambda h: g_u[0:w, h * DK:(h + 1) * DK], 4, DK)
                        done(gdn)
                        yield
                    gdn.begin(dve, t, "g_outc")
                    for q in range(2):
                        dve.tensor_copy(pj[half(q), GV:GV + 2, c], ps[half(q), 4 + q, 0:2 * w].rearrange("k (p l) -> k p l", p=2))
                    if t < NT:
                        grow(S_g[:, :, :], eG[:, :, 0:1].to_broadcast([P, 2, DK]),
                             ps[:, 4, 256:256 + 2 * DK].rearrange("k (p v) -> k p v", p=2), None, gdn)
                        done(gdn)
                        yield
                    else:
                        done(gdn)
                        yield
                        gdn.begin(dve, t, "g_statec")
                        grow(Q_g[:, :, :, :], eG[:, :, :].unsqueeze(3).to_broadcast([P, 2, NB, DK]),
                             ps[:, 4:6, :].rearrange("k p (b v) -> k p b v", b=NB), None, gdn)
                        done(gdn)
                        yield

            def hgrn_dve():
                yield from hgrn_pre()
                for t in range(NT + 1):
                    w = P if t < NT else NS
                    c = slice(t * P, t * P + w)
                    v = lambda b: b[0:w, 0:4 * w].rearrange("m (h l) -> m h l", h=4)
                    f = lambda b: b[:, 0:2 * w].rearrange("k (p l) -> k p l", p=2)
                    D_ = v(hD)
                    g = pj[:, HF:HF + 2, c]

                    def level_diff(n):
                        s = LEVELS[n]
                        for p in range(2):
                            x = g[:, p, :].rearrange("k (b i) -> k b i", i=2 * s)
                            dve.tensor_tensor(f(hEf)[:, p, :].rearrange("k (b i) -> k b i", i=2 * s), x,
                                              x[:, :, s - 1:s].to_broadcast([P, w // (2 * s), 2 * s]), SUB)

                    hgrn.begin(dve, t, "h_diag")
                    for q in range(2):
                        dve.tensor_tensor(D_[:, 2 * q:2 * q + 2, :], ps[0:w, 6 + q, 0:2 * w].rearrange("m (p l) -> m p l", p=2),
                                          ident[0:w, 0:w].unsqueeze(1).to_broadcast([w, 2, w]), MUL)
                    level_diff(0)
                    done(hgrn)
                    yield
                    for n in levels_of(t):
                        hgrn.begin(dve, t, f"h_sc{n}")
                        dve.tensor_tensor(f(hQl), pj[:, HQ:HQ + 2, c], f(hEf), MUL)
                        dve.tensor_tensor(f(hKl), kg[:, :, c], f(hEf), MUL)
                        done(hgrn)
                        yield
                        hgrn.begin(dve, t, f"h_add{n}")
                        X_ = v(hX)
                        for q in range(2):
                            dve.tensor_tensor(X_[:, 2 * q:2 * q + 2, :], ps[0:w, 6 + q, 0:2 * w].rearrange("m (p l) -> m p l", p=2),
                                              mask(n, w).unsqueeze(1).to_broadcast([w, 2, w]), MUL)
                        if n != levels_of(t)[-1]:
                            level_diff(n + 1)
                        else:
                            for p in range(2):
                                if t < NT:
                                    dve.tensor_tensor(f(hEf)[:, p, :], g[:, p, w - 1:w].to_broadcast([P, w]), g[:, p, :], SUB)
                                else:
                                    x = g[:, p, :].rearrange("k (b i) -> k b i", i=ND)
                                    dve.tensor_tensor(f(hEf)[:, p, :].rearrange("k (b i) -> k b i", i=ND),
                                                      x[:, :, ND - 1:ND].to_broadcast([P, NB, ND]), x, SUB)
                        dve.drain()
                        dve.tensor_tensor(D_, D_, X_, ADD)
                        done(hgrn)
                        yield
                    hgrn.begin(dve, t, "h_kd")
                    dve.tensor_tensor(f(hEf), kg[:, :, c], f(hEf), MUL)
                    keep_last(eH, f(hQ), t, w, 2)
                    dve.drain()
                    dve.tensor_tensor(f(hQ), f(hQ), pj[:, HQ:HQ + 2, c], MUL)
                    done(hgrn)
                    yield
                    hgrn.begin(dve, t, "h_tokc")
                    dve.tensor_copy(hKd[0:w, 0:256], ps[0:w, 6, 0:256])
                    dve.tensor_copy(hV[0:w, 0:256], ps[0:w, 6, 256:512])
                    done(hgrn)
                    yield
                    hgrn.begin(dve, t, "h_outc")
                    for q in range(2):
                        dve.tensor_copy(pj[half(q), HI:HI + 2, c], ps[half(q), 6 + q, 0:2 * w].rearrange("k (p l) -> k p l", p=2))
                    if t < NT:
                        grow(S_h[:, :, :], eH[:, :, 0:1].to_broadcast([P, 2, DK]),
                             ps[:, 6, 256:256 + 2 * DK].rearrange("k (p v) -> k p v", p=2), None, hgrn)
                        done(hgrn)
                        yield
                    else:
                        spread(h_Ue, lambda h: hV[0:w, h * DK:(h + 1) * DK], 4, DK)
                        done(hgrn)
                        yield
                        hgrn.begin(dve, t, "h_statec")
                        grow(Q_h[:, :, :, :], eH[:, :, :].unsqueeze(3).to_broadcast([P, 2, NB, DK]),
                             ps[:, 6:8, :].rearrange("k p (b v) -> k p b v", b=NB), None, hgrn)
                        done(hgrn)
                        yield
            def rest_dve():
                yield from rest_pre()
                for t in range(NT + 1):
                    w = P if t < NT else NS
                    c = slice(t * P, t * P + w)
                    rest.begin(dve, t, "s_diff")
                    if t == 0:
                        dve.wait_ge(d_tail_s, 9 * 16)
                    D8 = bD[0:w, 0:8 * w].rearrange("m (h l) -> m h l", h=8)
                    for g_ in range(2):
                        dve.tensor_tensor(D8[:, 4 * g_:4 * g_ + 4, :], ps[0:w, 2 + g_, 0:4 * w].rearrange("m (j l) -> m j l", j=4),
                                          col(t, 0, T_S + 4 * g_, 4, w, w), SUB)
                    dve.drain()
                    dve.tensor_tensor(D8, D8, neg(t).unsqueeze(1).to_broadcast([w, 8, w]), ADD)
                    done(rest)
                    yield
                    rest.begin(dve, t, "s_att")
                    for g_ in range(2):
                        dve.tensor_tensor(D8[:, 4 * g_:4 * g_ + 4, :], D8[:, 4 * g_:4 * g_ + 4, :],
                                          ps[0:w, 2 + g_, 0:w].unsqueeze(1).to_broadcast([w, 4, w]), MUL)
                        dve.tensor_tensor(bKd[0:w, g_ * 256:(g_ + 1) * 256].rearrange("m (j n) -> m j n", j=4),
                                          ps[0:w, 2, 128 + g_ * DK:128 + (g_ + 1) * DK].unsqueeze(1).to_broadcast([w, 4, DK]),
                                          col(t, 1, T_S + 4 * g_, 4, w, DK), MUL)
                    for b in [bV]:
                        dve.tensor_tensor(b[0:w, 0:256].rearrange("m (h v) -> m h v", h=8),
                                          ps[0:w, 2, 256:512].rearrange("m (h v) -> m h v", h=8), col(t, 2, T_S, 8, w, 32), MUL)
                    done(rest)
                    yield
                    rest.begin(dve, t, "s_q")
                    E4 = ps[:, 2, 0:4 * w].rearrange("k (j l) -> k j l", j=4)
                    dve.tensor_tensor(bQ[:, 0:4 * w].rearrange("k (j l) -> k j l", j=4), E4,
                                      pj[:, SC, c].unsqueeze(1).to_broadcast([P, 4, w]), MUL)
                    keep_last(eR, E4, t, w, 4)
                    done(rest)
                    yield
                    rest.begin(dve, t, "s_outc")
                    for g_ in range(2):
                        dve.scalar_tensor_tensor(out=pj[:, SX + g_, c], in0=pj[:, SX + g_, c], scalar=dcol[:, g_:g_ + 1],
                                                 in1=ps[:, 2 + g_, 0:w], op0=MUL, op1=ADD)
                    if t < NT:
                        grow(S_s[:, :, :], eR[:, :, 0:1].to_broadcast([P, 4, 32]),
                             ps[:, 2, 256:384].rearrange("k (j v) -> k j v", j=4), None, rest)
                        done(rest)
                        yield
                    else:
                        spread(b_Ue, lambda h: bV[0:w, h * 32:(h + 1) * 32], 8, 32)
                        done(rest)
                        yield
                        rest.begin(dve, t, "s_statec")
                        for j in range(4):
                            grow(Qs(Q_s)[:, j], eR[:, j, :].unsqueeze(2).to_broadcast([P, NB, 32]),
                                 ps[:, 2 + j // 2, (j % 2) * 256:(j % 2 + 1) * 256].rearrange("k (b v) -> k b v", b=NB), None, rest)
                        done(rest)
                        yield
                for t in range(NT + 1):
                    w = P if t < NT else NS
                    c = slice(t * P, t * P + w)
                    v = lambda b: b[0:w, 0:4 * w].rearrange("m (h l) -> m h l", h=4)
                    f = lambda b: b[:, 0:2 * w].rearrange("k (p l) -> k p l", p=2)
                    tok = lambda b: b[0:w, 0:256].rearrange("m (h v) -> m h v", h=4)
                    D_ = v(bD)
                    rest.begin(dve, t, "m_scale")
                    ktok = ps[0:w, 2, 0:256].rearrange("m (h v) -> m h v", h=4)
                    dve.tensor_tensor(tok(bKd), ktok, col(t, 1, T_M, 4, w, DK), MUL)
                    for b in [bV]:
                        dve.tensor_copy(b[0:w, 0:256], ps[0:w, 2, 256:512])
                    Eb = ps[:, 3, 0:2 * w].rearrange("k (p l) -> k p l", p=2)
                    dve.scalar_tensor_tensor(out=f(bQ), in0=pj[:, MQ:MQ + 2, c], scalar=DK ** -0.5, in1=Eb, op0=MUL, op1=MUL)
                    keep_last(eR, Eb, t, w, 2)
                    if t == NT:
                        dve.wait_ge(d_q["mlstm"], 128)
                        for p in range(2):
                            dve.tensor_copy(Q_n[:, p, :, 1:DK], Q_n[:, p, :, 0:1].to_broadcast([P, NB, DK - 1]))
                    done(rest)
                    yield
                    rest.begin(dve, t, "m_diff")
                    decays(t, w, D_, 2, T_M, rest)
                    yield
                    rest.begin(dve, t, "m_att")
                    for q in range(2):
                        dve.scalar_tensor_tensor(out=bD[0:w, 2 * q * w:(2 * q + 2) * w], in0=ps[0:w, 2 + q, 0:2 * w], scalar=DK ** -0.5,
                                                 in1=bD[0:w, 2 * q * w:(2 * q + 2) * w], op0=MUL, op1=MUL)
                    done(rest)
                    yield
                    rest.begin(dve, t, "m_outc")
                    den = bDen
                    for q in range(2):
                        dve.tensor_copy(pj[half(q), MV:MV + 2, c], ps[half(q), 2 + q, 0:2 * w].rearrange("k (p l) -> k p l", p=2))
                        dve.tensor_copy(den[half(q), 0:2 * w], ps[half(q), 2 + q, 256:256 + 2 * w])
                    done(rest)
                    yield
                    rest.begin(dve, t, "m_denc")
                    stt(den[:, 0:2 * w], den[:, 0:2 * w], -1.0, den[:, 0:2 * w], MUL, ALU.max)
                    tt(den[:, 0:2 * w], den[:, 0:2 * w], ps[:, 2, 0:2 * w], ALU.max)
                    dve.reciprocal(den[:, 0:2 * w], den[:, 0:2 * w])
                    dve.drain()
                    tt(pj[:, MV:MV + 2, c], pj[:, MV:MV + 2, c], f(den), MUL)
                    if t < NT:
                        for S, o in ((S_c, 0), (S_n, 128)):
                            grow(S[:, :, :], eR[:, 0:2, 0:1].to_broadcast([P, 2, DK]),
                                 ps[:, 3, o:o + 2 * DK].rearrange("k (p v) -> k p v", p=2), None, rest)
                        done(rest)
                        yield
                    else:
                        spread(b_Ue, lambda h: bV[0:w, h * DK:(h + 1) * DK], 4, DK)
                        done(rest)
                        yield
                        for name, Q in (("m_statec", Q_c), ("m_normc", Q_n)):
                            rest.begin(dve, t, name)
                            grow(Q[:, :, :, :], eR[:, 0:2, :].unsqueeze(3).to_broadcast([P, 2, NB, DK]),
                                 ps[:, 2:4, :].rearrange("k p (b v) -> k p b v", b=NB), None, rest)
                            if name == "m_statec":
                                spread(b_Ue, lambda h: ones[0:w, 0:DK], 4, DK)
                            done(rest)
                            yield

            gens = {"g": gdn_dve(), "h": hgrn_dve(), "s": rest_dve()}
            for chain, t, name, engine in order:
                if engine == "dve":
                    next(gens[chain])

            mid.begin(dve, 0, "mod2")
            gdn.after(dve, NT, "g_statec")
            hgrn.after(dve, NT, "h_statec")
            rest.after(dve, NT, "m_normc")
            dve.wait_ge(x_read, UNITS)
            tt(mod[:, 16:48, :], mod[:, 16:48, :], ada_bias(16, 48), ADD)
            done(mid)
            for n in range(4):
                gate_t = (GZ, HG, SZ, MO)[n]
                mid.begin(dve, 0, f"o_sq{n}")
                for f in range(2):
                    o = pj[:, BR[2 * n + f], :]
                    if n == 2:
                        tt(o, o, pj[:, gate_t + f, :], MUL)
                    dve.tensor_tensor(rstd2(scr)[:, f, :], o, o, MUL)
                done(mid)
                mid.begin(dve, 0, f"o_n{n}")
                for f in range(2):
                    o = pj[:, BR[2 * n + f], :]
                    wn = (V_GN, V_HN, V_SN + f, V_MN)[n]
                    stt(o, o, vt[:, wn:wn + 1], rstd2(scr)[:, f, :], MUL, MUL)
                    if n != 2:
                        tt(o, o, pj[:, gate_t + f, :], MUL)
                done(mid)

            for k in range(32):
                dve.wait_ge(lin_done, k + 1)
                dve.wait_ge(gate_ready, k + 1)
                lift = ps[:, 2 * (k % 4):2 * (k % 4) + 2, 0:HN]
                out = merged_t(pj, k // 4)
                if k % 4 == 0:
                    dve.tensor_tensor(two(out), two(gbuf(pj)[:, k % 4, :]), lift, MUL).then_inc(lin_read, 1)
                    dve.drain()
                else:
                    dve.tensor_tensor(two(mtmp(scr)), two(gbuf(pj)[:, k % 4, :]), lift, MUL).then_inc(lin_read, 1)
                    dve.drain()
                    tt(out, out, mtmp(scr), ADD)
            mid.begin(dve, 0, "upc")
            done(mid)

            dve.wait_ge(d_xin, 16)

            def residual(tile0, d, c0):
                par = d % 2
                dve.wait_ge(tile_done, tile0 + d + 1)
                gt = mod[:, c0 + d, :]
                n1 = T - HN
                dve.scalar_tensor_tensor(out=xT[:, d, 0:HN], in0=ps[:, 2 * par, 0:HN], scalar=gt[:, 0:1], in1=xT[:, d, 0:HN], op0=MUL, op1=ADD)
                dve.scalar_tensor_tensor(out=xT[:, d, HN:T], in0=ps[:, 2 * par + 1, 0:n1], scalar=gt[:, 0:1], in1=xT[:, d, HN:T], op0=MUL, op1=ADD)
                m = mtmp(scr)[:, 0:NS].rearrange("p (b t) -> p b t", t=ND)
                tt(m, ps[:, 2 * par + 1, n1:HN].rearrange("p (b t) -> p b t", t=ND), gt[:, 1:9].unsqueeze(2).to_broadcast([P, NB, ND]), MUL)
                dve.tensor_tensor(xT[:, d, T:TA], xT[:, d, T:TA], mtmp(scr)[:, 0:NS], ADD)
                dve.drain().then_inc(tile_read, 1)

            for d in range(KD):
                residual(tiles_before["wout"], d, 16)
            mid.begin(dve, 0, "res1")
            done(mid)
            squares(mid, "sq2", xT)
            modulate(mid, "norm2", xT, V_N2, 24)

            def ff_mul(i, e):
                dve.wait_ge(lin_done, i * 2 + (32 + e + 1))
                dve.wait_ge(tile_read, i * 2 + (tiles_before["ffa"] + e + 1))
                dve.tensor_tensor(pj[:, bass.ds(i * 2 + (8 + e), 1), :].rearrange("p o (h n) -> p (o h) n", h=2),
                                  two(fbuf(scr)[:, e, :]), ps[:, 4 + 2 * e:6 + 2 * e, 0:HN], MUL).then_inc(lin_read, 1)
            with dve.Fori(0, 11) as i:
                for e in range(2):
                    ff_mul(i, e)
            mid.begin(dve, 0, "ffac")
            done(mid)
            for d in range(KD):
                residual(tiles_before["ffb"], d, 40)
            mid.begin(dve, 0, "res2")
            done(mid)
            squares(mid, "sq3", xT)
            mid.begin(dve, 0, "norm3")
            for k in range(KD):
                dve.scalar_tensor_tensor(out=hT[:, k, :], in0=xT[:, k, :], scalar=vt[:, V_NF + k:V_NF + k + 1], in1=rstd[:, :], op0=MUL, op1=MUL)
            done(mid)


def xtok(pj):
    return pj[:, :, :].rearrange("p a b -> p (a b)")[:, 0:NT * D].rearrange("p (a d) -> p a d", d=D)


def xstok(pj):
    return pj[:, :, :].rearrange("p a b -> p (a b)")[0:NS, NT * D:NT * D + D]


def ctok(pj):
    return pj[:, :, :].rearrange("p a b -> p (a b)")[:, NT * D + D:NT * D + 2 * D]


def ytok(pj, t):
    return pj[:, :, :].rearrange("p a b -> p (a b)")[0:(P if t < NT else NS), t * D:(t + 1) * D]


def rowbuf(scr, n):
    return scr[0:NR, B0 + 544 * n:B0 + 544 * (n + 1)]


def RS(scr):
    return rowbuf(scr, 1)


def RK(scr):
    return rowbuf(scr, 0)


def RN(scr):
    return rowbuf(scr, 3)


def Qs(Q):
    return Q[:, :, :, :].rearrange("k p b v -> k (p b v)").rearrange("k (j b v) -> k j b v", j=4, b=NB)


def wb(scr):
    return scr[:, 0:8 * D].rearrange("p (n c) -> p n c", c=D)


def rstd2(scr):
    return scr[:, 8192:9280].rearrange("p (f n) -> p f n", f=2)


def mtmp(scr):
    return scr[:, 9280:9280 + TA]


def fbuf(scr):
    return scr[:, 0:2 * TA].rearrange("p (e n) -> p e n", e=2)


GBUF = 14


def gbuf(pj):
    return pj[:, GBUF:GBUF + 4, :]


MERGED = [0, 1, 2, 3, 6, 7, 8, 9]


def merged_t(pj, d):
    return pj[:, MERGED[d], :]


_INS = ['x_prompt', 'x_sample', 'c_prompt', 'c_sample', 'state_gdn', 'state_gdn_conv', 'state_hgrn', 'state_ssd',
        'state_ssd_conv', 'state_mlstm_c', 'state_mlstm_n', 'state_mlstm_m', 'ada_w', 'ada_b', 'norm1_w', 'norm2_w', 'w_in',
        'gdn_conv_w', 'gdn_conv_b', 'gdn_a_log', 'gdn_dt_bias', 'gdn_norm_w', 'hg_lb_logits', 'hg_norm_w', 'ssd_conv_w',
        'ssd_conv_b', 'ssd_a_log', 'ssd_dt_bias', 'ssd_d', 'ssd_norm_w', 'ml_b_i', 'ml_b_f', 'ml_norm_w', 'w_branch',
        'w_out', 'ffn_w_in', 'ffn_w_out', 'final_norm_w']


def _state_shapes(b):
    return [(1, b, 4, 64, 64), (1, b, 3, 768), (1, b, 4, 64, 64), (1, b, 8, 64, 32), (1, b, 3, 512), (1, b, 4, 64, 64),
            (1, b, 4, 64), (1, b, 4)]


_OUTS = [(1, T, D), (NB, ND, D)] + _state_shapes(1) + _state_shapes(NB)


def kernel(**inputs):
    import concourse.bacc as _bacc
    from concourse.bass_utils import run_bass_kernel_spmd as _run

    nc = _bacc.Bacc("TRN2", target_bir_lowering=False, num_devices=1)
    arrays, args = {}, {}
    for name in _INS + ["const"]:
        a = host_constants() if name == "const" else np.ascontiguousarray(inputs[name])
        arrays[f"in_{name}_dram"] = a
        args[name] = nc.dram_tensor(f"in_{name}_dram", a.shape, mybir.dt.from_np(a.dtype), kind="ExternalInput").ap()
    outs = [nc.dram_tensor(f"out_{i}_dram", shape, F32, kind="ExternalOutput").ap() for i, shape in enumerate(_OUTS)]
    trunk(nc, args, outs)
    r = _run(nc, [arrays], core_ids=[0])
    return tuple(r.results[0][f"out_{i}_dram"] for i in range(len(_OUTS)))
```

```python
from contextlib import ExitStack

import numpy as np

import concourse.bass as bass
from concourse import mybir

F32 = mybir.dt.float32
F32R = mybir.dt.float32r
ALU = mybir.AluOpType
ACT = mybir.ActivationFunctionType
AX = mybir.AxisListType

P = 128
D = 1024
KD = D // P
T = 512
B0, C0, SCR = 4864, 8448, 11264
NB, ND = 8, 4
NS = NB * ND
TA = T + NS
HN = TA // 2
NT = T // P
FF = 2816
KF = FF // P
DK = 64
EPS = 1e-6
BIG = 1e30
R = 4
SLOT = 2048

MIX_ORDER = [0, 1, 2, 9, 10, 4, 5, 6, 11, 12, 13, 3, 8, 7, 14]
GROUP_COLS = [0, 256, 512, 768, 1032, 1288, 1544, 1800, 2056, 2312, 2568, 2832, 3088, 3344, 3600]
C_GB, C_GA, C_DT, C_MI, C_MF, C_GATE = 1024, 1028, 2824, 3856, 3860, 3864
GQ, GK, GV, GZ, HQ, HF, HI, HG, SZ, SX, SB, SC, MQ, MK, MV, MO = 0, 2, 4, 6, 8, 10, 12, 14, 16, 18, 20, 21, 22, 24, 26, 28
BR = [GV, GV + 1, HI, HI + 1, SX, SX + 1, MV, MV + 1]
CONV_G, CONV_S = [0, 1, 2, 3, 4, 5], [18, 19, 20, 21]
R_G, R_S, R_M, NR = 0, 32, 64, 96
T_G, T_S, T_M, NCOL = 0, 4, 12, 16
LEVELS = [1, 2, 4, 8, 16, 32, 64]
Y_BANK = [6, 0, 2, 6, 0]
ADA_FROM = 5
MERGED, MERGED_HI = [0, 1, 2, 3, 6, 7, 8, 9], [14, 15, 16, 17, 28, 29, 4, 5]
GBUF = [10, 11, 24, 25, 20, 21]
N_RAW = 6
LAG = 7
PIECE = KF // 2 * P
M_WOUT = 4 * KD
M_FFA = M_WOUT + KD
M_FFB = M_FFA + 2 * KF

K_ID, K_B64, K_ONE, K_MASK, K_NEG, K_NEGS, K_RST, K_OWN, K_SGN, K_N = 0, 128, 256, 384, 1280, 1408, 1440, 1984, 1992, 1993
V_ADAB, V_N1, V_N2, V_NF, V_GCW, V_GCB, V_SCW, V_SCB, V_1 = 0, 48, 56, 64, 72, 96, 102, 118, 122
V_SN, V_GN, V_HN, V_MN, V_2 = 122, 124, 125, 126, 127


def host_constants():
    c = np.zeros((P, K_N), np.float32)
    i = np.arange(P)
    c[:, K_ID:K_ID + P] = np.eye(P)
    c[:, K_B64:K_B64 + P] = i[:, None] // DK == i[None] // DK
    c[:, K_ONE:K_ONE + P] = 1
    m, l = i[:, None], i[None]
    for n, s in enumerate(LEVELS):
        c[:, K_MASK + n * P:K_MASK + (n + 1) * P] = (m // (2 * s) == l // (2 * s)) & (m % (2 * s) < s) & (l % (2 * s) >= s)
    c[:, K_NEG:K_NEG + P] = np.where(m <= l, 0, -BIG)
    m, l = m[:NS], l[:, :NS]
    c[:NS, K_NEGS:K_NEGS + NS] = np.where((m <= l) & (m // ND == l // ND), 0, -BIG)
    reset = np.ones(TA)
    reset[0:T:P] = 0
    reset[T::ND] = 0
    c[:, K_RST:K_RST + TA] = reset
    c[:NS, K_OWN:K_OWN + NB] = i[:NS, None] // ND == np.arange(NB)
    c[:, K_SGN] = np.where(i < R_M, 1, -1)
    return c


class Chain:

    def __init__(self, sem, stages):
        self.sem, self.stages = sem, stages
        self.at = {(t, name): n for n, (t, name, _) in enumerate(stages)}

    def begin(self, eng, t, name):
        n = self.at[(t, name)]
        if n:
            eng.wait_ge(self.sem, n)

    def after(self, eng, t, name):
        eng.wait_ge(self.sem, self.at[(t, name)] + 1)


PRE = -1


def gdn_stages(t):
    if t == PRE:
        s = [("tail", "pe"), ("tailc", "dve")]
        for n in range(6):
            s += [(f"conv{n}", "dve"), (f"silu{n}", "act")]
        s += [("l2sq", "dve")]
        for n in range(4):
            s += [(f"l2_{n}", "pe"), (f"l2r{n}", "act")]
        return [(t, "g_" + n, e) for n, e in s + [("l2m", "dve")]]
    s = [("tokens", "pe"), ("scale", "dve"), ("bcast", "pe"), ("diff", "dve"), ("decay", "act"), ("kk", "pe"),
         ("lower", "dve"), ("first", "pe"), ("t1", "act")]
    for n in levels_of(t)[1:]:
        s += [(f"x{n}", "pe"), (f"xc{n}", "act"), (f"y{n}", "pe"), (f"upd{n}", "dve")]
    s += [("qk", "pe"), ("aq", "dve"), ("sk", "pe"), ("skc", "act"), ("u", "pe"), ("uc", "dve")]
    if t == NT:
        s += [("ut", "pe"), ("utc", "dve")]
    s += [("out", "pe"), ("outc", "dve")]
    if t == NT:
        s += [("state", "pe"), ("statec", "dve")]
    return [(t, "g_" + n, e) for n, e in s]


def hgrn_stages(t):
    if t == PRE:
        s = [("lb0", "dve"), ("lb1", "act"), ("lb2", "dve"), ("lb3", "pe"), ("lb4", "dve"), ("lb5", "act"), ("silu", "act"),
             ("lb6", "dve")]
        for f in range(2):
            s += [(f"ls{f}", "act"), (f"b{f}", "dve"), (f"ln{f}", "act"), (f"g{f}", "dve")]
        return [(t, "h_" + n, e) for n, e in s]
    s = [("qk", "pe"), ("diag", "dve")]
    for n in levels_of(t):
        s += [(f"dec{n}", "act"), (f"sc{n}", "dve"), (f"qk{n}", "pe"), (f"add{n}", "dve")]
    s += [("dec", "act"), ("kd", "dve"), ("tok", "pe"), ("tokc", "dve"), ("out", "pe"), ("outc", "dve")]
    if t == NT:
        s += [("state", "pe"), ("statec", "dve")]
    return [(t, "h_" + n, e) for n, e in s]


def ssd_stages(t):
    if t == PRE:
        s = [("w_a", "pe"), ("rz", "dve"), ("w_b", "pe"), ("rb", "act"), ("ri", "dve"), ("rexp", "act"), ("rv", "dve")]
        for n in range(3):
            s += [(f"rcol{n}", "pe"), (f"rcolc{n}", "dve")]
        s += [("tail", "pe"), ("tailc", "dve")]
        for n in range(4):
            s += [(f"conv{n}", "dve"), (f"silu{n}", "act")]
        return [(t, "s_" + n, e) for n, e in s]
    s = [("bcast", "pe"), ("diff", "dve"), ("decay", "act"), ("cb", "pe"), ("att", "dve"), ("e", "pe"),
         ("q", "dve"), ("out", "pe"), ("outc", "dve")]
    if t == NT:
        s += [("state", "pe"), ("statec", "dve")]
    return [(t, "s_" + n, e) for n, e in s]


def mlstm_stages(t):
    s = [("tok", "pe"), ("scale", "dve"), ("bcast", "pe"), ("diff", "dve"), ("decay", "act"), ("qk", "pe"),
         ("att", "dve"), ("out", "pe"), ("outc", "dve"), ("den", "pe"), ("denc", "dve")]
    if t == NT:
        s += [("state", "pe"), ("statec", "dve"), ("norm", "pe"), ("normc", "dve")]
    return [(t, "m_" + n, e) for n, e in s]


def levels_of(t):
    return range(len(LEVELS)) if t < NT else range(2)


SEQUENCE = []
for _n in range(len(MIX_ORDER)):
    SEQUENCE += [("mix", 4 * _n + _v) for _v in range(4)]
    if _n >= ADA_FROM:
        SEQUENCE[-1:] = [("ada", _n - ADA_FROM), SEQUENCE[-1], ("turn", _n - ADA_FROM)] if _n - ADA_FROM < 8 else SEQUENCE[-1:]
UNITS = len(SEQUENCE)
POS = {u: n for n, u in enumerate(SEQUENCE)}


def units_through(f):
    return POS[("mix", 4 * MIX_ORDER.index(f // 2) + 2 * (f % 2) + 1)] + 1


NEEDS = {
    ("g", PRE, "g_tail"): [("x", units_through(5))],
    ("g", 0, "g_tokens"): [("s", PRE, "s_rcolc2")],
    ("h", PRE, "h_silu"): [("x", units_through(13)), ("s", PRE, "s_w_b")],
    ("h", PRE, "h_lb2"): [("s", PRE, "s_w_b")],
    ("s", PRE, "s_tail"): [("x", units_through(21))],
    ("s", 0, "m_tok"): [("x", units_through(27))],
}
AHEAD = 0.003
COST = {"pe": 1.2, "dve": 1.2, "act": 0.9}
COSTS = {"g_scale": 2.3, "g_diff": 1.4, "g_lower": 2.6, "g_upd": 2.0, "g_aq": 0.7, "g_uc": 0.5, "h_diag": 1.0, "h_sc": 0.9,
         "h_add": 1.8, "s_diff": 2.4, "s_att": 2.6, "s_conv": 3.6, "g_conv": 3.6, "s_ri": 16.0, "g_l2sq": 2.4, "g_l2m": 2.4,
         "h_b": 2.2, "h_g": 3.0, "h_ls": 2.6, "h_ln": 2.6, "h_silu": 3.0, "s_rb": 3.0, "g_y": 1.9, "s_w_a": 7.0, "s_w_b": 7.0,
         "g_tail": 1.8, "g_silu": 0.8, "s_silu": 0.8}


def cost(name, engine):
    for k in range(len(name), 2, -1):
        if name[:k] in COSTS:
            return COSTS[name[:k]]
    return COST[engine]


def shared_order(chains):
    free = {"pe": 0.0, "dve": 0.0, "act": 0.0}
    at = {c: 0 for c in chains}
    when = {}
    ready = {c: 0.0 for c in chains}
    out, unit, part_, evac = [], 0, 0, []
    left = {c: sum(cost(name, eng) + 0.1 for _, name, eng in stages) for c, stages in chains.items()}
    while unit < UNITS or any(at[c] < len(chains[c]) for c in chains):
        best = None
        for c in chains:
            if at[c] >= len(chains[c]):
                continue
            t, name, eng = chains[c][at[c]]
            needs = [when.get(("x", n[1]) if n[0] == "x" else n) for n in NEEDS.get((c, t, name), [])]
            if None in needs:
                continue
            start = max([free[eng], ready[c]] + needs)
            rank = start - AHEAD * left[c]
            if best is None or rank < best_rank - 1e-9:
                best, best_rank = (start, c, t, name, eng), rank
        if evac:
            start = max(free["act"], evac[0][0])
            if best is None or start <= best[0]:
                best = (start, "x", evac[0][1], "read", "act")
        if unit < UNITS:
            kind, v = SEQUENCE[unit]
            needs = [unit - 1] if unit >= 2 else []
            if kind == "turn":
                needs.append(POS[("ada", v)] + 1)
            known = all(("x", n) in when for n in needs)
            start = max([free["pe"]] + [when.get(("x", n), 0.0) for n in needs])
            if known and (best is None or start < best[0]):
                best = (start, "x", unit, f"part{part_}", "pe")
        start, c, t, name, eng = best
        if c == "x" and eng == "act":
            free[eng] = start + 0.5
            when[("x", t + 1)] = free[eng]
            evac.pop(0)
        elif c == "x":
            free[eng] = start + {"mix": 1.85, "ada": 3.4, "turn": 0.3}[SEQUENCE[t][0]]
            if part_ == 1:
                evac.append((free[eng], unit))
                unit, part_ = unit + 1, 0
            else:
                part_ = 1
        else:
            free[eng] = start + cost(name, eng)
            ready[c] = free[eng] + 0.1
            when[(c, t, name)] = ready[c]
            at[c] += 1
            left[c] -= cost(name, eng) + 0.1
        out.append((c, t, name, eng))
    while evac:
        out.append(("x", evac.pop(0)[1], "read", "act"))
    return out


def trunk(nc, A, O):
    ctx = ExitStack()
    with ctx:
        ctx.enter_context(nc.allow_non_contiguous_dma(reason="state vectors, a few KB"))

        def sb(name, shape):
            return ctx.enter_context(nc.sbuf_tensor(name, shape, F32))

        def sem(name):
            return ctx.enter_context(nc.semaphore(name))

        ps = ctx.enter_context(nc.psum_tensor("ps", [P, 8, 512], F32))
        cst = sb("cst", [P, K_N])
        vt = sb("vt", [P, V_2])
        ring = sb("ring", [P, R, SLOT])
        cT = sb("cT", [P, KD, NB + 1])
        mod = sb("mod", [P, 6 * KD, NB + 1])
        coef = sb("coef", [P, KD, NB + 1])
        rstd = sb("rstd", [P, TA])
        colp = sb("colp", [P, 4])
        hcol = sb("hcol", [P, 2, 6])
        dcol = sb("dcol", [P, 2])
        hrow = sb("hrow", [P, 264])
        cols = sb("cols", [P, NT + 1, 4, NCOL])
        Rr = sb("Rr", [P, TA])
        Er = sb("Er", [P, TA])
        Vr = sb("Vr", [P, TA])
        pair_buf = (Er, Vr)
        MTr = sb("MTr", [P, TA])
        kg = sb("kg", [P, 2, TA])
        S_g = sb("S_g", [P, 2, DK])
        S_h = sb("S_h", [P, 2, DK])
        S_s = sb("S_s", [P, 4, 32])
        S_c = sb("S_c", [P, 2, DK])
        S_n = sb("S_n", [P, 2, DK])
        Q = sb("Q", [P, 5, 1024])
        Q_g, Q_h, Q_s, Q_c, Q_n = (Q[:, n, :].rearrange("k (p b v) -> k p b v", p=2, b=NB) for n in range(5))
        eG = sb("eG", [P, 2, NB])
        eH = sb("eH", [P, 2, NB])
        eR = sb("eR", [P, 4, NB])
        twice = [("hT", [P, KD, TA]),
                 ("pj", [P, 30, TA]),
                 ("scr", [P, SCR])]
        guards = [nc.sbuf_tensor(name, shape, F32) for name, shape in twice]
        hT, pj, scr = (g.__enter__() for g in guards)
        for g in reversed(guards):
            g.__exit__(None, None, None)
        hT_parts, pj_parts, scr_parts = (ctx.enter_context(nc.sbuf_tensor(name + "_parts", shape, F32R)) for name, shape in twice)
        x_out = nc.dram_tensor("x_scratch", [P, KD * TA], F32, kind="Internal").ap()

        def part(at, n):
            return scr[:, at:at + n]

        ada_rows = part(5256, 2048)[0:NB + 1, :]

        xT0 = part(0, KD * TA).rearrange("p (k n) -> p k n", n=TA)
        xT = Q[:, :, :].rearrange("p a b -> p (a b)")[:, 0:KD * TA].rearrange("p (k n) -> p k n", n=TA)
        vrow = part(5000, 2 * P).rearrange("p (a c) -> p a c", a=2)
        wsm = part(C0, KD * 2 * NR).rearrange("p (k e r) -> p k e r", k=KD, e=2)

        gT, gU, gX, gL, gD = (part(512 * n, 512) for n in range(5))
        g_vb, g_kn, g_kd, g_u, g_sk, g_qs, g_kb = (part(2560 + 256 * n, 256) for n in range(7))
        gAt = part(4352, 512)
        g_Ue = part(0, 2048)
        g_acc, g_hist, g_spad, g_tail = part(0, 1088), part(1088, 768), part(1856, 336), part(2192, 768)
        bD, bKd, bV, bQ, bDen = part(B0, 1024), part(B0 + 2048, 512), part(B0 + 2560, 256), part(B0 + 2816, 512), part(B0 + 1536, 256)
        b_Ue = part(B0, 2048)
        s_acc, s_spad, s_tail, s_hist = part(B0, 1088), part(B0 + 1088, 224), part(B0 + 1312, 512), part(B0 + 2720, 512)
        hD, hX, hQl, hKl, hEf = part(C0, 512), part(C0 + 512, 512), part(C0 + 1024, 256), part(C0 + 1280, 256), part(C0 + 1536, 256)
        hV, hQ, hKd = part(C0 + 2048, 256), part(C0 + 2304, 256), part(C0 + 2560, 256)
        h_Ue = part(C0, 2048)
        hrow2 = part(C0 + 1600, 512)

        h_hi = scr_parts[:, 0:KD * TA].rearrange("p (k n) -> p k n", n=TA)
        h_lo = hT_parts[:, :, :]
        w_hi, w_lo = ([scr_parts[:, B0 + (2 * e + q) * PIECE:B0 + (2 * e + q + 1) * PIECE] for e in range(2)] for q in range(2))
        m_hi = [pj_parts[:, f, :] for f in MERGED_HI]
        m_lo = [pj_parts[:, f, :] for f in MERGED]
        f_hi = [pj_parts[:, i, :] for i in range(8)] + [h_hi[:, i, :] for i in range(8)] + [h_lo[:, i, :] for i in range(KF - 16)]
        f_lo = [pj_parts[:, 8 + i, :] for i in range(KF)]
        wb_slot = [kg[:, :, :].rearrange("p a n -> p (a n)")[:, 0:KD * P].rearrange("p (n c) -> p n c", c=P),
                   pj[:, 22:24, :].rearrange("p a n -> p (a n)")[:, 0:KD * P].rearrange("p (n c) -> p n c", c=P)]

        rms = [[Er[:, :], Vr[:, :]]] + [[pj[:, f, :], pj[:, f + 1, :]] for f in (0, 2, 8)]

        gates = [pj[:, f, :] for f in GBUF] + [Er[:, :], Vr[:, :]]

        def piece(m):
            if m < M_WOUT:
                n, e = first["gate"] + m // 2, m % 2
                return n, ring[:, n % R, :].rearrange("p (k e c) -> p k e c", k=KD, e=2)[:, :, e, :]
            if m < M_FFA:
                n, e = first["wout"] + (m - M_WOUT) // 2, m % 2
                return n, ring[:, n % R, :].rearrange("p (k c) -> p k c", k=KD)[:, :, e * P:(e + 1) * P]
            if m < M_FFB:
                n, e = first["ffa"] + (m - M_FFA) // 2, m % 2
                return n, ring[:, n % R, :].rearrange("p (k e c) -> p k e c", k=KD, e=2)[:, :, e, :]
            n = first["ffb"] + m - M_FFB
            return n, ring[:, n % R, 0:PIECE].rearrange("p (k c) -> p k c", c=P)

        def parts(m):
            n = KD if m < M_FFB else KF // 2
            return (b[m % 2][:, 0:n * P].rearrange("p (k c) -> p k c", c=P) for b in (w_hi, w_lo))

        ident = cst[:, K_ID:K_ID + P]
        b64 = cst[:, K_B64:K_B64 + P]
        ones = cst[:, K_ONE:K_ONE + P]

        def mask(n, p):
            return cst[0:p, K_MASK + n * P:K_MASK + n * P + p]

        def neg(t):
            return cst[:, K_NEG:K_NEG + P] if t < NT else cst[0:NS, K_NEGS:K_NEGS + NS]

        d_cst, d_vec, d_x, d_c, d_wsm, d_row, d_hist, d_st = (sem(n) for n in
            ("d_cst", "d_vec", "d_x", "d_c", "d_wsm", "d_row", "d_hist", "d_st"))
        d_q = {n: sem(f"d_q_{n}") for n in ("gdn", "hgrn", "ssd", "mlstm")}
        d_wb = [sem("d_wb0"), sem("d_wb1")]
        d_xout, d_xin = sem("d_xout"), sem("d_xin")
        d_tail_g, d_tail_s = sem("d_tail_g"), sem("d_tail_s")
        w_split_hi, w_split = sem("w_split_hi"), sem("w_split")
        w_done = sem("w_done")
        gate_read = sem("gate_read")
        act_hi, act_split = sem("act_hi"), sem("act_split")
        stream_in = sem("stream_in")
        normed = sem("normed")
        high_done = sem("high_done")
        gate_in_hi, gate_in = sem("gate_in_hi"), sem("gate_in")
        rms_ready, branch_ready = sem("rms_ready"), sem("branch_ready")
        merged = sem("merged")
        squared, summed = sem("squared"), sem("summed")
        y_ready, y_done, y_act, y_dve = (sem(n) for n in ("y_ready", "y_done", "y_act", "y_dve"))
        w_in_slot = [sem(f"w_in_slot{n}") for n in range(R)]
        w_used = sem("w_used")
        zeroed = sem("zeroed")
        x_done, x_read = sem("x_done"), sem("x_read")
        tile_read = sem("tile_read")
        lin_done, lin_read = sem("lin_done"), sem("lin_read")
        gate_ready = sem("gate_ready")
        stored = sem("stored")
        pre_s, gdn_s, hgrn_s, rest_s, mid_s = sem("pre"), sem("gdn"), sem("hgrn"), sem("rest"), sem("mid")

        pre = [("silc", "act"), ("ct", "pe"), ("ctc", "dve")]
        for d in range(KD):
            pre += [(f"x{d}", "pe"), (f"xc{d}", "act"), (f"sq{d}", "dve"), (f"ss{d}", "pe")]
        pre += [("rs1", "act"), ("turn1", "pe"), ("mod1", "dve"), ("norm1", "act")]
        pre = Chain(pre_s, [(0, n, e) for n, e in pre])
        tiles = range(NT + 1)
        gdn = Chain(gdn_s, [s for t in (PRE, *tiles) for s in gdn_stages(t)])
        hgrn = Chain(hgrn_s, [s for t in (PRE, *tiles) for s in hgrn_stages(t)])
        rest = Chain(rest_s, [s for t in (PRE, *tiles) for s in ssd_stages(t)] + [s for t in tiles for s in mlstm_stages(t)])
        order = shared_order({"g": gdn.stages, "h": hgrn.stages, "s": rest.stages})
        mid = [("mod2", "dve"), ("silus", "act")]
        for n in range(4):
            mid += [(f"o_sq{n}", "dve"), (f"o_ss{n}", "pe"), (f"o_rs{n}", "act")]
        mid += [("up", "pe"), ("upc", "dve"), ("ss2", "pe"), ("rs2", "act"), ("ffa", "pe"), ("ffac", "dve"), ("ss3", "pe"),
                ("rs3", "act"), ("cols3", "pe"), ("colc3", "dve")]
        mid = Chain(mid_s, [(0, n, e) for n, e in mid])

        phases = [("ada1", 8), ("window", 15 + 16), ("gate", 16), ("wout", 4), ("ffa", 22), ("ffb", 16)]
        first, n = {}, 0
        for kind, count in phases:
            first[kind] = n
            n += count
        counts = dict(phases)
        window, last_unit, load_of = [("ada1", n) for n in range(8)], {}, {}
        for u, (kind, v) in enumerate(SEQUENCE):
            if kind == "mix" and v % 4 == 0:
                load_of[("mixer", v // 4)] = len(window)
                window.append(("mixer", v // 4))
            if kind == "mix":
                last_unit[("mixer", v // 4)] = u
            if kind == "ada":
                for e in range(2):
                    load_of[("ada2", 2 * v + e)] = len(window)
                    window.append(("ada2", 2 * v + e))
                    last_unit[("ada2", 2 * v + e)] = u
        tiles_before = {"wout": 0, "ffa": 8, "ffb": 30}

        def landed(eng, slot, n):
            if isinstance(n, int):
                eng.wait_ge(w_in_slot[slot], 32 * (n // R + 1))
            else:
                eng.wait_ge(w_in_slot[slot], n * (32 // R) + (32 - slot * (32 // R)))

        block = ctx.enter_context(nc.Block())

        @block.sync
        def _(sp):
            sp.dma_start(ctok(pj)[0:1, :], A["c_prompt"]).then_inc(d_c, 16)
            sp.dma_start(ctok(pj)[1:NB + 1, :], A["c_sample"]).then_inc(d_c, 16)
            sp.dma_start(cst[:, :], A["const"]).then_inc(d_cst, 16)
            sp.dma_start(xtok(pj), A["x_prompt"][0].rearrange("(a p) d -> p a d", p=P)).then_inc(d_x, 16)
            sp.dma_start(xstok(pj), A["x_sample"].rearrange("b t d -> (b t) d")).then_inc(d_x, 16)
            def kp(name):
                return A[name][0].rearrange("(k p) c -> p k c", p=P)

            def load(kind, slot, idx):
                full = ring[:, slot, :]
                if kind in ("ada1", "ada2", "mixer", "wout"):
                    src = kp({"ada1": "ada_w", "ada2": "ada_w", "mixer": "w_in", "wout": "w_out"}[kind])
                    if kind == "mixer":
                        c0 = GROUP_COLS[MIX_ORDER[idx]]
                    else:
                        c0 = idx * 256 + (2048 if kind == "ada2" else 0)
                    dst = full.rearrange("p (k c) -> p k c", k=KD)
                    for h in range(2):
                        sp.dma_start(dst[:, 4 * h:4 * h + 4, :], src[:, 4 * h:4 * h + 4, bass.ds(c0, 256)]).then_inc(w_in_slot[slot], 16)
                elif kind == "gate":
                    dst = full.rearrange("p (k e c) -> p k e c", k=KD, e=2)
                    for e in range(2):
                        c0 = C_GATE + (2 * (idx % 2) + e) * D + idx // 2 * P
                        sp.dma_start(dst[:, :, e, :], kp("w_in")[:, :, c0:c0 + P]).then_inc(w_in_slot[slot], 16)
                elif kind == "ffa":
                    dst = full.rearrange("p (k e c) -> p k e c", k=KD, e=2)
                    for e in range(2):
                        sp.dma_start(dst[:, :, e, :], kp("ffn_w_in")[:, :, bass.ds(idx * P + e * FF, P)]).then_inc(w_in_slot[slot], 16)
                else:
                    dst = full[:, 0:11 * P].rearrange("p (k c) -> p k c", c=P)
                    e, d = idx
                    for k0, k1 in ((0, 6), (6, 11)):
                        sp.dma_start(dst[:, k0:k1, :], kp("ffn_w_out")[:, 11 * e + k0:11 * e + k1, bass.ds(d * P, P)]).then_inc(w_in_slot[slot], 16)

            def vectors():
                rows = lambda a, n: A[a].rearrange("o (r c) -> (o r) c", c=P)
                for name, at, n in (("ada_b", V_ADAB, 48), ("norm1_w", V_N1, 8), ("norm2_w", V_N2, 8),
                                    ("gdn_conv_b", V_GCB, 6), ("ssd_conv_b", V_SCB, 4)):
                    sp.dma_start(vrow[at:at + n, 0, :], rows(name, n)).then_inc(d_vec, 16)
                sp.dma_start(vrow[V_NF:V_NF + 8, 0, :], A["final_norm_w"].rearrange("(r c) -> r c", c=P)).then_inc(d_vec, 16)
                sp.dma_start(vrow[V_GCW:V_GCW + 24, 0, :], A["gdn_conv_w"].rearrange("o k (r c) -> (o k r) c", c=P)).then_inc(d_vec, 16)
                sp.dma_start(vrow[V_SCW:V_SCW + 16, 0, :], A["ssd_conv_w"].rearrange("o k (r c) -> (o k r) c", c=P)).then_inc(d_vec, 16)
                sp.dma_start(vrow[0:2, 1, :], rows("ssd_norm_w", 2)).then_inc(d_vec, 16)
                for n, name in enumerate(("gdn_norm_w", "hg_norm_w", "ml_norm_w")):
                    for h in range(2):
                        sp.dma_start(vrow[2 + n:3 + n, 1, h * DK:(h + 1) * DK], A[name]).then_inc(d_vec, 16)
                sp.dma_start(hrow[0:1, 256:264], A["ssd_d"]).then_inc(d_vec, 16)
                sp.dma_start(hrow[0:1, 0:256], A["hg_lb_logits"]).then_inc(d_vec, 16)

            def slot_of(kind, idx):
                return (first[kind] + idx) % R

            for idx in range(counts["ada1"]):
                if idx == R:
                    vectors()
                if idx >= R:
                    sp.wait_ge(w_used, idx - R + 1)
                load("ada1", slot_of("ada1", idx), idx)
            sp.wait_ge(zeroed, 1)
            for e, at, c0, w in ((0, R_G, C_GA, 4), (0, R_S, C_DT, 8), (0, R_M, C_MF, 4), (1, R_G, C_GB, 4), (1, R_M, C_MI, 4)):
                sp.dma_start(wsm[:, :, e, at:at + w], kp("w_in")[:, :, c0:c0 + w]).then_inc(d_wsm, 16)
            for at, name, c in ((R_G, "gdn_dt_bias", 0), (R_S, "ssd_dt_bias", 0), (R_M, "ml_b_f", 0),
                                (R_G, "gdn_a_log", 1), (R_S, "ssd_a_log", 1), (R_M, "ml_b_i", 2)):
                w = A[name].shape[1]
                sp.dma_start(colp[at:at + w, c:c + 1], A[name].rearrange("o h -> h o")).then_inc(d_row, 16)
            sp.dma_start(hrow[64:68, 0:NB * 5:5], A["state_mlstm_m"][0].rearrange("b h -> h b")).then_inc(d_st, 16)
            loads = window + [("gate", n) for n in range(R)]
            for n in range(8, len(loads)):
                kind, idx = loads[n]
                held, hidx = loads[n - R]
                if held == "ada1":
                    sp.wait_ge(w_used, hidx + 1)
                else:
                    sp.wait_ge(x_done, last_unit[(held, hidx)] + 1)
                load(kind, n % R, idx)
                if n == 11:
                    pre.after(sp, 0, "xc7")
                    sp.dma_start(x_out, part(0, KD * TA)).then_inc(d_xout, 16)
                    sp.dma_start(s_hist[0:3 * NB, :], A["state_ssd_conv"][0].rearrange("b k c -> (b k) c")).then_inc(d_hist, 16)
                    pre.after(sp, 0, "norm1")
                    sp.wait_ge(d_xout, 16)
                    sp.dma_start(g_hist[0:3 * NB, :], A["state_gdn_conv"][0].rearrange("b k c -> (b k) c")).then_inc(d_hist, 16)
                if n == 14:
                    for p in range(2):
                        for q in range(2):
                            at, h = slice(q * DK, (q + 1) * DK), 2 * p + q
                            for Qx, name, d in ((Q_g, "state_gdn", "gdn"), (Q_h, "state_hgrn", "hgrn"), (Q_c, "state_mlstm_c", "mlstm")):
                                sp.dma_start(Qx[at, p], A[name][0, :, h].rearrange("b k v -> k b v")).then_inc(d_q[d], 16)
                            sp.dma_start(Q_n[at, p, :, 0], A["state_mlstm_n"][0, :, h].rearrange("b k -> k b")).then_inc(d_q["mlstm"], 16)
                    for g in range(2):
                        for j in range(4):
                            sp.dma_start(Qs(Q_s)[g * DK:(g + 1) * DK, j], A["state_ssd"][0, :, 4 * g + j].rearrange("b n v -> n b v")).then_inc(d_q["ssd"], 16)
            stored_at = [0]

            def store(dst, src):
                sp.dma_start(dst, src).then_inc(stored, 16)
                stored_at[0] += 16

            def heads(dst, S):
                for p in range(2):
                    for q in range(2):
                        store(dst[2 * p + q], S[q * DK:(q + 1) * DK, p])

            def qheads(dst, S):
                for p in range(2):
                    for q in range(2):
                        store(dst[:, 2 * p + q].rearrange("b k v -> k b v"), S[q * DK:(q + 1) * DK, p])

            def lift_weights(d):
                if d >= 2:
                    sp.wait_ge(lin_done, 4 * (d - 1))
                sp.dma_start(wb_slot[d % 2], A["w_branch"][0].rearrange("n (k p) c -> p (n k) c", p=P)[:, :, d * P:(d + 1) * P]).then_inc(d_wb[d % 2], 16)

            hgrn.after(sp, NT, "h_statec")
            lift_weights(0)
            qheads(O[12][0], Q_h)
            heads(O[4][0, 0], S_h)
            gdn.after(sp, NT, "g_statec")
            qheads(O[10][0], Q_g)
            heads(O[2][0, 0], S_g)
            rest.after(sp, NT, "m_normc")
            lift_weights(1)
            for g in range(2):
                for j in range(4):
                    store(O[13][0, :, 4 * g + j].rearrange("b n v -> n b v"), Qs(Q_s)[g * DK:(g + 1) * DK, j])
                    store(O[5][0, 0, 4 * g + j], S_s[g * DK:(g + 1) * DK, j])
            qheads(O[15][0], Q_c)
            heads(O[7][0, 0], S_c)
            for p in range(2):
                for q in range(2):
                    store(O[16][0, :, 2 * p + q].rearrange("b k -> k b"), Q_n[q * DK:(q + 1) * DK, p, :, 0])
                    store(O[8][0, 0, 2 * p + q].unsqueeze(1), S_n[q * DK:(q + 1) * DK, p, 0:1])
            store(O[9][0].rearrange("o h -> h o"), MTr[R_M:R_M + 4, T - 1:T])
            store(O[17][0].rearrange("b h -> h b"), MTr[R_M:R_M + 4, T + ND - 1:TA:ND])
            for idx in range(R, counts["gate"]):
                sp.wait_ge(w_split, 2 * (idx - R) + 2)
                load("gate", slot_of("gate", idx), idx)
                if idx == 7:
                    sp.wait_ge(stored, stored_at[0])
                    sp.dma_start(Q[:, :, :].rearrange("p a b -> p (a b)")[:, 0:KD * TA], x_out).then_inc(d_xin, 16)
                if idx >= 8 and idx % 2 == 0:
                    lift_weights(idx // 2 - 2)
            for idx in range(R):
                sp.wait_ge(w_split, 2 * (counts["gate"] - R + idx) + 2)
                load("wout", slot_of("wout", idx), idx)
                if idx % 2 == 0:
                    lift_weights(6 + idx // 2)
            for idx in range(R):
                sp.wait_ge(w_split, M_WOUT + 2 * idx + 2)
                load("ffa", slot_of("ffa", idx), idx)
            with sp.Fori(0, 4) as i:
                for r in range(R):
                    sp.wait_ge(w_split, i * (2 * R) + (M_FFA + 2 * r + 2))
                    load("ffa", slot_of("ffa", r), i * R + (R + r))
            for idx in range(5 * R, counts["ffa"]):
                sp.wait_ge(w_split, M_FFA + 2 * (idx - R) + 2)
                load("ffa", slot_of("ffa", idx), idx)
            for idx in range(R):
                sp.wait_ge(w_split, M_FFB - 2 * (R - idx) + 2)
                load("ffb", slot_of("ffb", idx), (idx % 2, idx // 2))
            with sp.Fori(0, 3) as i:
                for r in range(R):
                    sp.wait_ge(w_split, i * R + (M_FFB + r + 1))
                    load("ffb", slot_of("ffb", r), (r % 2, i * 2 + (2 + r // 2)))
            for t in range(NT + 1):
                sp.wait_ge(y_act, t + 1)
                sp.wait_ge(y_dve, t + 1)
                yt = ytok(pj, t)
                store(O[0][0, t * P:(t + 1) * P, :] if t < NT else O[1].rearrange("b t d -> (b t) d"), yt)
            sp.wait_ge(stored, stored_at[0])
            sp.wait_ge(d_tail_g, 9 * 16)
            sp.wait_ge(d_tail_s, 9 * 16)

        @block.gpsimd
        def _(pool):
            pool.memset(wsm[:, :, :, :], 0.0)
            pool.memset(colp[:, :], 0.0)
            pool.drain()
            for S in (S_g, S_h, S_s, S_c, S_n):
                pool.memset(S[:, :, :], 0.0)
            pool.drain().then_inc(zeroed, 1)
            for chain, name, tl, po, so, d in ((gdn, "g_tailc", g_tail, O[3], O[11], d_tail_g), (rest, "s_tailc", s_tail, O[6], O[14], d_tail_s)):
                chain.after(pool, PRE, name)
                pool.dma_start(po[0, 0], tl[NS - 3:NS, :]).then_inc(d, 16)
                for b in range(NB):
                    r0 = NS + ND * b + 1
                    pool.dma_start(so[0, b], tl[r0:r0 + 3, :]).then_inc(d, 16)

        @block.tensor
        def _(pe):
            def mm(out, lhsT, rhs, start=True, stop=True):
                return pe.matmul(out, lhsT, rhs, start=start, stop=stop, skip_group_check=True)

            def tr(out, in_):
                n = in_.shape[0]
                return pe.transpose(out, in_, ident[0:n, 0:n])

            pe.wait_ge(d_cst, 16)
            pre.begin(pe, 0, "ct")
            for k in range(KD):
                last = tr(ps[:, 5, (NB + 1) * k:(NB + 1) * (k + 1)], ctok(pj)[0:NB + 1, k * P:(k + 1) * P])
            last.then_inc(pre_s, 1)
            def ada_rows_of(out, slot):
                for k in range(KD):
                    last = mm(out, cT[:, k, :], ring[:, slot, k * 256:(k + 1) * 256], k == 0, k == KD - 1)
                return last

            pe.wait_ge(d_x, 32)
            pre.after(pe, 0, "ctc")
            for d in range(KD):
                pre.begin(pe, 0, f"x{d}")
                for a in range(NT):
                    tr(ps[:, 0, a * P:(a + 1) * P], xtok(pj)[:, a, d * P:(d + 1) * P])
                tr(ps[:, 1, 0:NS], xstok(pj)[:, d * P:(d + 1) * P]).then_inc(pre_s, 1)
                landed(pe, d % R, d)
                ada_rows_of(ps[0:NB + 1, (2, 3, 6, 7)[d // 2], d % 2 * 256:d % 2 * 256 + 256], d % R).then_inc(w_used, 1)
                pre.begin(pe, 0, f"ss{d}")
                for h in range(2):
                    last = mm(ps[:, 4 + h, 0:HN], ones, hT[:, d, h * HN:(h + 1) * HN], d == 0, d == KD - 1)
                last.then_inc(pre_s, 1)
            pre.begin(pe, 0, "turn1")
            pe.wait_ge(d_vec, 16 * 17)
            tr(ps[:, 1, 0:V_1], vrow[0:V_1, 0, :])
            tr(ps[:, 1, V_1:V_2], vrow[0:V_2 - V_1, 1, :])
            for c in range(16):
                last = tr(ps[:, 0, c * 9:(c + 1) * 9], ada_rows[:, c * P:(c + 1) * P])
            last.then_inc(pre_s, 1)

            def sum_squares(d, n):
                pe.wait_ge(squared, n + d + 1)
                for h in range(2):
                    last = mm(ps[:, 4 + h, 0:HN], ones, pair_buf[d % 2][:, h * HN:(h + 1) * HN], d == 0, d == KD - 1)
                last.then_inc(summed, 1)

            def unit_part(u, part_):
                if part_ == 0 and u >= 2:
                    pe.wait_ge(x_read, u - 1)
                kind, v = SEQUENCE[u]
                if kind == "mix":
                    n, c, h = load_of[("mixer", v // 4)], v // 2 % 2, v % 2
                    if part_ == 0:
                        landed(pe, n % R, n)
                    for k in range(4 * part_, 4 * part_ + 4):
                        if u == 0:
                            pe.wait_ge(stream_in, k + 1)
                        at = k * 256 + c * P
                        last = mm(ps[:, u % 2, 0:HN], ring[:, n % R, at:at + P], hT[:, k, h * HN:(h + 1) * HN], k == 0, k == KD - 1)
                elif kind == "ada":
                    n = load_of[("ada2", 2 * v + part_)]
                    landed(pe, n % R, n)
                    last = ada_rows_of(ps[0:NB + 1, u % 2, part_ * 256:(part_ + 1) * 256], n % R)
                elif part_ == 1:
                    pe.wait_ge(x_read, POS[("ada", v)] + 1)
                    for c in range(4):
                        last = tr(ps[:, u % 2, c * 9:(c + 1) * 9], rstd[0:NB + 1, c * P:(c + 1) * P])
                if part_ == 1:
                    last.then_inc(x_done, 1)

            def pick(h, n):
                return ident[0:NR, h:h + 1].to_broadcast([NR, n])

            def bcast2(out, h0, step, rows):
                for q in range(2):
                    last = mm(out[half(q)], pick(h0 + step * q, DK), rows)
                return last

            def half(q):
                return slice(q * DK, (q + 1) * DK)

            def tails(feats, hist, bank):
                for n in range(len(feats)):
                    tr(ps[:, bank + 1, 256 + n * 24:256 + (n + 1) * 24], hist[0:3 * NB, n * P:(n + 1) * P])
                for n, f in enumerate(feats):
                    last = tr(ps[0:2 * NS, bank + n // 4, (n % 4) * P:(n % 4 + 1) * P], pj[:, f, T - NS:TA])
                return last

            def gdn_pe():
                gdn.begin(pe, PRE, "g_tail")
                pe.wait_ge(x_read, units_through(GV + 1))
                pe.wait_ge(d_hist, 32)
                tails(CONV_G, g_hist, 4).then_inc(gdn_s, 1)
                yield
                for n in range(4):
                    gdn.begin(pe, PRE, f"g_l2_{n}")
                    for h in range(2):
                        last = mm(ps[:, 4 + h, 0:HN], b64, part(544 * n, TA)[:, h * HN:(h + 1) * HN])
                    last.then_inc(gdn_s, 1)
                    yield
                for t in range(NT + 1):
                    w = P if t < NT else NS
                    c = slice(t * P, t * P + w)
                    v = lambda b: b[0:w, 0:4 * w].rearrange("m (h l) -> m h l", h=4)
                    T_, U_, X_, L_, D_ = v(gT), v(gU), v(gX), v(gL), v(gD)
                    f = lambda b: b[:, 0:2 * w].rearrange("k (p l) -> k p l", p=2)
                    qs, kb, sk = f(g_qs), f(g_kb), f(g_sk)
                    B0_, B1_ = ps[:, 4, :], ps[:, 5, :]
                    gdn.begin(pe, t, "g_tokens")
                    if t == 0:
                        rest.after(pe, PRE, "s_rcolc2")
                    for p in range(2):
                        tr(B0_[0:w, p * P:(p + 1) * P], pj[:, GK + p, c])
                        tr(B0_[0:w, 256 + p * P:256 + (p + 1) * P], pj[:, GV + p, c])
                    for p in range(2):
                        bcast2(B1_[:, p * w:(p + 1) * w], 2 * p, 1, Er[0:NR, c])
                        last = bcast2(B1_[:, 256 + p * w:256 + (p + 1) * w], 2 * p, 1, Vr[0:NR, c])
                    last.then_inc(gdn_s, 1)
                    yield
                    gdn.begin(pe, t, "g_bcast")
                    for q in range(2):
                        for p in range(2):
                            last = mm(B0_[0:w, (2 * q + p) * w:(2 * q + p + 1) * w], pick(2 * p + q, w), Rr[0:NR, c])
                    last.then_inc(gdn_s, 1)
                    yield
                    gdn.begin(pe, t, "g_kk")
                    for q in range(2):
                        for p in range(2):
                            last = mm(ps[0:w, 4 + q, p * w:(p + 1) * w], pj[half(q), GK + p, c], kb[half(q), p, :])
                    last.then_inc(gdn_s, 1)
                    yield
                    gdn.begin(pe, t, "g_first")
                    for h in range(4):
                        last = tr(B0_[0:w, h * w:(h + 1) * w], U_[:, h, :])
                    last.then_inc(gdn_s, 1)
                    yield
                    for n in levels_of(t)[1:]:
                        gdn.begin(pe, t, f"g_x{n}")
                        for h in range(4):
                            last = mm(B0_[0:w, h * w:(h + 1) * w], L_[:, h, :], T_[:, h, :])
                        last.then_inc(gdn_s, 1)
                        yield
                        gdn.begin(pe, t, f"g_y{n}")
                        for h in range(4):
                            mm(B0_[0:w, h * w:(h + 1) * w], U_[:, h, :], X_[:, h, :])
                        for h in range(4):
                            last = mm(B1_[0:w, h * w:(h + 1) * w], X_[:, h, :], U_[:, h, :])
                        last.then_inc(gdn_s, 1)
                        yield
                    gdn.begin(pe, t, "g_qk")
                    for q in range(2):
                        for p in range(2):
                            last = mm(ps[0:w, 4 + q, p * w:(p + 1) * w], pj[half(q), GK + p, c], pj[half(q), GQ + p, c])
                    last.then_inc(gdn_s, 1)
                    yield
                    gdn.begin(pe, t, "g_sk")
                    for q in range(2):
                        for p in range(2):
                            h = 2 * p + q
                            last = mm(B0_[half(q), p * w:(p + 1) * w], g_kn[0:w, h * DK:(h + 1) * DK], U_[:, 2 * q + p, :])
                    last.then_inc(gdn_s, 1)
                    yield
                    gdn.begin(pe, t, "g_u")
                    for q in range(2):
                        for p in range(2):
                            h, x = 2 * p + q, 2 * q + p
                            if t < NT:
                                o = ps[0:w, 4 + q, p * DK:(p + 1) * DK]
                                mm(o, U_[:, x, :], g_vb[0:w, h * DK:(h + 1) * DK], True, False)
                                last = mm(o, sk[half(q), p, :], S_g[half(q), p, :], False, True)
                            else:
                                if (p, q) == (0, 0):
                                    pe.wait_ge(d_q["gdn"], 64)
                                o = ps[half(q), 4 + q, p * w:(p + 1) * w]
                                mm(o, g_vb[0:w, h * DK:(h + 1) * DK], U_[:, x, :], True, False)
                                for b in range(NB):
                                    last = mm(o[:, ND * b:ND * b + ND], Q_g[half(q), p, b, :], sk[half(q), p, ND * b:ND * b + ND],
                                              False, b == NB - 1)
                    last.then_inc(gdn_s, 1)
                    yield
                    if t == NT:
                        gdn.begin(pe, t, "g_ut")
                        for p in range(2):
                            last = tr(B0_[0:w, p * P:(p + 1) * P], g_sk[:, p * w:(p + 1) * w])
                        last.then_inc(gdn_s, 1)
                        yield
                    gdn.begin(pe, t, "g_out")
                    for q in range(2):
                        for p in range(2):
                            h, x = 2 * p + q, 2 * q + p
                            o = ps[half(q), 4 + q, p * w:(p + 1) * w]
                            mm(o, g_u[0:w, h * DK:(h + 1) * DK], D_[:, x, :], True, False)
                            if t < NT:
                                last = mm(o, S_g[half(q), p, :], qs[half(q), p, :], False, True)
                            else:
                                for b in range(NB):
                                    last = mm(o[:, ND * b:ND * b + ND], Q_g[half(q), p, b, :], qs[half(q), p, ND * b:ND * b + ND],
                                              False, b == NB - 1)
                    if t < NT:
                        for h in range(4):
                            last = mm(B0_[half(h % 2), 256 + (h // 2) * DK:256 + (h // 2 + 1) * DK],
                                      g_kd[0:w, h * DK:(h + 1) * DK], g_u[0:w, h * DK:(h + 1) * DK])
                    last.then_inc(gdn_s, 1)
                    yield
                    if t == NT:
                        gdn.begin(pe, t, "g_state")
                        for h in range(4):
                            last = mm(ps[half(h % 2), 4 + h // 2, :], g_kd[0:w, h * DK:(h + 1) * DK],
                                      g_Ue[0:w, h * 512:(h + 1) * 512])
                        last.then_inc(gdn_s, 1)
                        yield

            def scores(t, bank, keys, queries):
                w = P if t < NT else NS
                for q in range(2):
                    for p in range(2):
                        last = mm(ps[0:w, bank + q, p * w:(p + 1) * w], keys[half(q), p, :], queries[half(q), p, :])
                return last

            def outputs(t, bank, vals, at, St, Qt, qs, col):
                w = P if t < NT else NS
                for q in range(2):
                    for p in range(2):
                        h, x = 2 * p + q, 2 * q + p
                        o = ps[half(q), bank + q, col + p * w:col + (p + 1) * w]
                        mm(o, vals(h), at[:, x, :], True, False)
                        if t < NT:
                            last = mm(o, St[half(q), p, :], qs[half(q), p, :], False, True)
                        else:
                            for b in range(NB):
                                last = mm(o[:, ND * b:ND * b + ND], Qt[half(q), p, b, :],
                                          qs[half(q), p, ND * b:ND * b + ND], False, b == NB - 1)
                return last

            def increments(kd, vals, bank, col):
                for h in range(4):
                    last = mm(ps[half(h % 2), bank, col + (h // 2) * DK:col + (h // 2 + 1) * DK],
                              kd[:, h * DK:(h + 1) * DK], vals(h))
                return last

            def q_increments(kd, Ue, bank):
                for h in range(4):
                    last = mm(ps[half(h % 2), bank + h // 2, :], kd[0:NS, h * DK:(h + 1) * DK], Ue[0:NS, h * 512:(h + 1) * 512])
                return last

            def hgrn_pe():
                hgrn.begin(pe, PRE, "h_lb3")
                for p in range(2):
                    mm(ps[:, 6, p:p + 1], hrow[0:1, p * P:(p + 1) * P], ones[0:1, 0:1])
                    last = mm(ps[:, 6, 2 + p:3 + p], hrow2[0:1, p * P:(p + 1) * P], ones[0:1, 0:1])
                last.then_inc(hgrn_s, 1)
                yield
                for t in range(NT + 1):
                    w = P if t < NT else NS
                    c = slice(t * P, t * P + w)
                    f = lambda b: b[:, 0:2 * w].rearrange("k (p l) -> k p l", p=2)
                    v = lambda b: b[0:w, 0:4 * w].rearrange("m (h l) -> m h l", h=4)
                    hgrn.begin(pe, t, "h_qk")
                    scores(t, 6, kg[:, :, c], pj[:, HQ:HQ + 2, c]).then_inc(hgrn_s, 1)
                    yield
                    for n in levels_of(t):
                        hgrn.begin(pe, t, f"h_qk{n}")
                        scores(t, 6, f(hKl), f(hQl)).then_inc(hgrn_s, 1)
                        yield
                    hgrn.begin(pe, t, "h_tok")
                    for p in range(2):
                        tr(ps[0:w, 6, p * P:(p + 1) * P], f(hEf)[:, p, :])
                        last = tr(ps[0:w, 6, 256 + p * P:256 + (p + 1) * P], pj[:, HI + p, c])
                    last.then_inc(hgrn_s, 1)
                    yield
                    hgrn.begin(pe, t, "h_out")
                    if t == NT:
                        pe.wait_ge(d_q["hgrn"], 64)
                    vals = lambda h: hV[0:w, h * DK:(h + 1) * DK]
                    last = outputs(t, 6, vals, v(hD), S_h, Q_h, f(hQ), 0)
                    if t < NT:
                        last = increments(hKd, vals, 6, 256)
                    last.then_inc(hgrn_s, 1)
                    yield
                    if t == NT:
                        hgrn.begin(pe, t, "h_state")
                        q_increments(hKd, h_Ue, 6).then_inc(hgrn_s, 1)
                        yield

            def rest_pe():
                pre.after(pe, 0, "norm1")
                for e, name in enumerate(("s_w_a", "s_w_b")):
                    rest.begin(pe, PRE, name)
                    pe.wait_ge(d_wsm, 80)
                    for h in range(2):
                        for k in range(KD):
                            last = mm(ps[0:NR, 2 + h, 0:HN], wsm[:, k, e, :], hT[:, k, h * HN:(h + 1) * HN], k == 0, k == KD - 1)
                    last.then_inc(rest_s, 1)
                    yield
                for n in range(3):
                    rest.begin(pe, PRE, f"s_rcol{n}")
                    for t in range(2 * n, min(2 * n + 2, NT + 1)):
                        c0, w = t * P, (P if t < NT else NS)
                        for m, src in enumerate((RS(scr), RK(scr), Vr, RN(scr))):
                            last = tr(ps[0:w, 2 + t % 2, m * NR:(m + 1) * NR], src[0:NR, c0:c0 + w])
                    last.then_inc(rest_s, 1)
                    yield
                rest.begin(pe, PRE, "s_tail")
                pe.wait_ge(x_read, units_through(SC))
                pe.wait_ge(d_hist, 32)
                tails(CONV_S, s_hist, 2).then_inc(rest_s, 1)
                yield
                for t in range(NT + 1):
                    w = P if t < NT else NS
                    c = slice(t * P, t * P + w)
                    rest.begin(pe, t, "s_bcast")
                    for g in range(2):
                        for j in range(4):
                            last = mm(ps[0:w, 2 + g, j * w:(j + 1) * w], pick(R_S + 4 * g + j, w), Rr[0:NR, c])
                    last.then_inc(rest_s, 1)
                    yield
                    rest.begin(pe, t, "s_cb")
                    for g in range(2):
                        mm(ps[0:w, 2 + g, 0:w], pj[half(g), SB, c], pj[half(g), SC, c])
                    tr(ps[0:w, 2, 128:256], pj[:, SB, c])
                    for g in range(2):
                        last = tr(ps[0:w, 2, 256 + g * P:256 + (g + 1) * P], pj[:, SX + g, c])
                    last.then_inc(rest_s, 1)
                    yield
                    rest.begin(pe, t, "s_e")
                    for j in range(4):
                        last = bcast2(ps[:, 2, j * w:(j + 1) * w], R_S + j, 4, Er[0:NR, c])
                    last.then_inc(rest_s, 1)
                    yield
                    rest.begin(pe, t, "s_out")
                    if t == NT:
                        pe.wait_ge(d_q["ssd"], 128)
                    att = bD[0:w, 0:8 * w].rearrange("m (h l) -> m h l", h=8)
                    qs = bQ[:, 0:4 * w].rearrange("k (j l) -> k j l", j=4)
                    for g in range(2):
                        for j in range(4):
                            h = 4 * g + j
                            o = ps[32 * j:32 * j + 32, 2 + g, 0:w]
                            mm(o, bV[0:w, h * 32:(h + 1) * 32], att[:, h, :], True, False)
                            if t < NT:
                                last = mm(o, S_s[half(g), j, :], qs[half(g), j, :], False, True)
                            else:
                                for b in range(NB):
                                    last = mm(o[:, ND * b:ND * b + ND], Qs(Q_s)[half(g), j, b, :],
                                              qs[half(g), j, ND * b:ND * b + ND], False, b == NB - 1)
                    if t < NT:
                        for h in range(8):
                            last = mm(ps[half(h // 4), 2, 256 + (h % 4) * 32:256 + (h % 4 + 1) * 32],
                                      bKd[0:w, h * DK:(h + 1) * DK], bV[0:w, h * 32:(h + 1) * 32])
                    last.then_inc(rest_s, 1)
                    yield
                    if t == NT:
                        rest.begin(pe, t, "s_state")
                        for h in range(8):
                            j = h % 4
                            last = mm(ps[half(h // 4), 2 + j // 2, (j % 2) * 256:(j % 2 + 1) * 256],
                                      bKd[0:w, h * DK:(h + 1) * DK], b_Ue[0:w, h * 256:(h + 1) * 256])
                        last.then_inc(rest_s, 1)
                        yield
                for t in range(NT + 1):
                    w = P if t < NT else NS
                    c = slice(t * P, t * P + w)
                    f = lambda b: b[:, 0:2 * w].rearrange("k (p l) -> k p l", p=2)
                    v = lambda b: b[0:w, 0:4 * w].rearrange("m (h l) -> m h l", h=4)
                    rest.begin(pe, t, "m_tok")
                    if t == 0:
                        pe.wait_ge(x_read, units_through(MV + 1))
                    for p in range(2):
                        tr(ps[0:w, 2, p * P:(p + 1) * P], pj[:, MK + p, c])
                        tr(ps[0:w, 2, 256 + p * P:256 + (p + 1) * P], pj[:, MV + p, c])
                    for p in range(2):
                        last = bcast2(ps[:, 3, p * w:(p + 1) * w], R_M + 2 * p, 1, Er[0:NR, c])
                    last.then_inc(rest_s, 1)
                    yield
                    rest.begin(pe, t, "m_bcast")
                    for q in range(2):
                        for p in range(2):
                            last = mm(ps[0:w, 2, (2 * q + p) * w:(2 * q + p + 1) * w], pick(R_M + 2 * p + q, w), Rr[0:NR, c])
                    last.then_inc(rest_s, 1)
                    yield
                    rest.begin(pe, t, "m_qk")
                    scores(t, 2, pj[:, MK:MK + 2, c], pj[:, MQ:MQ + 2, c]).then_inc(rest_s, 1)
                    yield
                    rest.begin(pe, t, "m_out")
                    if t == NT:
                        pe.wait_ge(d_q["mlstm"], 128)
                    vals = lambda h: bV[0:w, h * DK:(h + 1) * DK]
                    on = lambda h: ones[0:w, 0:DK]
                    outputs(t, 2, vals, v(bD), S_c, Q_c, f(bQ), 0)
                    outputs(t, 2, on, v(bD), S_n, Q_n, f(bQ), 256).then_inc(rest_s, 1)
                    yield
                    rest.begin(pe, t, "m_den")
                    for p in range(2):
                        last = bcast2(ps[:, 2, p * w:(p + 1) * w], R_M + 2 * p, 1, Vr[0:NR, c])
                    if t < NT:
                        increments(bKd, vals, 3, 0)
                        last = increments(bKd, on, 3, 128)
                    last.then_inc(rest_s, 1)
                    yield
                    if t == NT:
                        for name in ("m_state", "m_norm"):
                            rest.begin(pe, t, name)
                            q_increments(bKd, b_Ue, 2).then_inc(rest_s, 1)
                            yield

            gens = {"g": gdn_pe(), "h": hgrn_pe(), "s": rest_pe()}
            for chain, t, name, engine in order:
                if engine == "pe" and chain == "x":
                    unit_part(t, int(name[-1]))
                elif engine == "pe":
                    next(gens[chain])

            def product(m, bank, hi, lo, start=True, stop=True, at=None, tiles_split=None, tiles=act_split):
                pe.wait_ge(w_split, (m if at is None else at) + 1)
                wh, wl = parts(m)
                n = len(hi)
                for k in range(n):
                    if tiles_split is not None:
                        pe.wait_ge(tiles, tiles_split + k + 1)
                    for h in range(2):
                        c = slice(h * HN, (h + 1) * HN)
                        o = ps[:, bank + h, 0:HN]
                        mm(o, wh[:, k, :], hi[k][:, c], start and k == 0, False)
                        mm(o, wl[:, k, :], hi[k][:, c], False, False)
                        last = mm(o, wh[:, k, :], lo[k][:, c], False, stop and k == n - 1)
                last.then_inc(w_done, 1)

            h_parts = [h_hi[:, k, :] for k in range(KD)], [h_lo[:, k, :] for k in range(KD)]
            for k in range(4 * KD + LAG):
                if k < 4 * KD:
                    if k >= 2:
                        pe.wait_ge(gate_read, k - 1)
                    product(k, 2 * (k % 2), *h_parts, tiles_split=0 if k == 0 else None, tiles=gate_in)
                if 1 <= k < 5:
                    n = k - 1
                    mid.begin(pe, 0, f"o_ss{n}")
                    for f in range(2):
                        for h in range(2):
                            last = mm(ps[:, 4 + 2 * f + h, 0:HN], ones if n == 2 else b64, rms[n][f][:, h * HN:(h + 1) * HN])
                    last.then_inc(mid_s, 1)
                if k >= LAG:
                    j = k - LAG
                    d, n = j // 4, j % 4
                    if j < 4:
                        pe.wait_ge(branch_ready, j + 1)
                    if n == 0:
                        pe.wait_ge(d_wb[d % 2], 16 * (d // 2 + 1))
                    if j >= 2:
                        pe.wait_ge(lin_read, j - 1)
                    for h in range(2):
                        for kk in range(2):
                            last = mm(ps[:, 4 + 2 * (j % 2) + h, 0:HN], wb_slot[d % 2][:, 2 * n + kk, :],
                                      pj[:, BR[2 * n + kk], h * HN:(h + 1) * HN], kk == 0, kk == 1)
                    last.then_inc(lin_done, 1)
            pe.drain().then_inc(mid_s, 1)

            mid.begin(pe, 0, "ss2")
            for j in range(KD):
                if j >= 2:
                    pe.wait_ge(tile_read, tiles_before["wout"] + j - 1)
                product(M_WOUT + j, 2 * (j % 2), m_hi, m_lo, tiles_split=0 if j == 0 else None)
                if j:
                    sum_squares(j - 1, 0)
            sum_squares(KD - 1, 0)
            pe.drain().then_inc(mid_s, 1)
            mid.begin(pe, 0, "ffa")
            pe.wait_ge(act_split, KD + 1)

            def ffa(idx, par):
                later = not isinstance(idx, int) or idx >= 2
                if later:
                    pe.wait_ge(tile_read, idx + (tiles_before["ffa"] - 1))
                product(M_FFA, 2 * par, *h_parts, at=idx * 2 + M_FFA,
                        tiles_split=KD + 1 if isinstance(idx, int) and idx == 0 else None)
                if later:
                    pe.wait_ge(lin_read, idx + (4 * KD - 1))
                product(M_FFA + 1, 4 + 2 * par, *h_parts, at=idx * 2 + (M_FFA + 1))
            for idx in range(2):
                ffa(idx, idx)
            with pe.Fori(0, KF // 2 - 1) as i:
                for r in range(2):
                    ffa(i * 2 + (2 + r), r)
            pe.drain().then_inc(mid_s, 1)

            def ffb(d, par, kind):
                if kind == "later":
                    pe.wait_ge(tile_read, d + (tiles_before["ffb"] - 1))
                for e in range(2):
                    c = slice(11 * e, 11 * e + 11)
                    product(M_FFB + e, 2 * par, f_hi[c], f_lo[c], e == 0, e == 1, at=d * 2 + (M_FFB + e),
                            tiles_split=2 * KD + 1 + 11 * e if kind == "first" else None)
            mid.after(pe, 0, "ffac")
            for d in range(2):
                ffb(d, d, "first" if d == 0 else "second")
                if d:
                    sum_squares(d - 1, KD)
            for d in range(2, KD):
                ffb(d, d % 2, "later")
                sum_squares(d - 1, KD)

            def turn(t, bank, k0=0):
                w = P if t < NT else NS
                for k in range(k0, KD):
                    if t == 0:
                        pe.wait_ge(y_ready, k + 1)
                    last = tr(ps[0:w, bank + k // 4, (k % 4) * P:(k % 4 + 1) * P], xT[:, k, t * P:t * P + w])
                last.then_inc(y_done, 1)
            turn(0, Y_BANK[0])
            sum_squares(KD - 1, KD)
            pe.drain().then_inc(mid_s, 1)
            pe.wait_ge(tile_read, tiles_before["ffb"] + KD)
            turn(1, Y_BANK[1])
            turn(2, Y_BANK[2])
            mid.begin(pe, 0, "cols3")
            for t in range(NT + 1):
                w = P if t < NT else NS
                last = mm(ps[0:w, 4, t:t + 1], rstd[0:1, t * P:t * P + w], ones[0:1, 0:1])
            last.then_inc(mid_s, 1)
            for t in (3, 4):
                pe.wait_ge(y_act, t - 2)
                pe.wait_ge(y_dve, t - 2)
                turn(t, Y_BANK[t])

        @block.scalar
        def _(act):
            pre.begin(act, 0, "silc")
            act.wait_ge(d_c, 32)
            act.activation(ctok(pj)[0:NB + 1, :], ctok(pj)[0:NB + 1, :], ACT.Silu).then_inc(pre_s, 1)
            def ada_out(b):
                act.activation(ada_rows[:, b * 512:(b + 1) * 512], ps[0:NB + 1, (2, 3, 6, 7)[b], :], ACT.Copy)

            for d in range(KD):
                if d in (3, 5, 7):
                    act.wait_ge(w_used, d - 1)
                    ada_out((d - 3) // 2)
                pre.begin(act, 0, f"xc{d}")
                act.activation(xT0[:, d, 0:T], ps[:, 0, :], ACT.Copy)
                act.activation(xT0[:, d, T:TA], ps[:, 1, 0:NS], ACT.Copy)
                act.drain().then_inc(pre_s, 1)
            act.wait_ge(w_used, KD)
            ada_out(3)

            def rsqrt(chain, name, dst, src, scale):
                chain.begin(act, 0, name)
                act.wait_ge(zeroed, 2)
                act.activation(dst, src, ACT.Ln, scale=scale, bias=colp[:, 3:4])
                act.drain()
                act.activation(dst, dst, ACT.Exp, scale=-0.5)
                act.drain().then_inc(chain.sem, 1)

            two = lambda b: b.rearrange("p (h n) -> p h n", h=2)
            rsqrt(pre, "rs1", two(rstd[:, :]), ps[:, 4:6, 0:HN], 1.0 / D)
            pre.begin(act, 0, "norm1")
            for k in range(KD):
                act.wait_ge(normed, k + 1)
                act.activation(hT[:, k, 0:T], hT[:, k, 0:T], ACT.Identity, bias=mod[:, k, 0:1]).then_inc(stream_in, 1)
            act.drain().then_inc(pre_s, 1)

            def read_unit(u):
                act.wait_ge(x_done, u + 1)
                kind, v = SEQUENCE[u]
                if kind == "mix":
                    f, h = 2 * MIX_ORDER[v // 4] + v // 2 % 2, v % 2
                    act.activation(pj[:, f, h * HN:(h + 1) * HN], ps[:, u % 2, 0:HN], ACT.Copy).then_inc(x_read, 1)
                elif kind == "ada":
                    act.activation(rstd[0:NB + 1, 0:512], ps[0:NB + 1, u % 2, :], ACT.Copy).then_inc(x_read, 1)
                else:
                    c0 = 16 + 4 * v
                    act.activation(mod[:, c0:c0 + 4, :].rearrange("p c b -> p (c b)"), ps[:, u % 2, 0:36], ACT.Copy).then_inc(x_read, 1)

            def gdn_act():
                for n, f in enumerate(CONV_G):
                    gdn.begin(act, PRE, f"g_silu{n}")
                    act.activation(pj[:, f, :], g_acc[:, 544 * (n % 2):544 * (n % 2 + 1)], ACT.Silu).then_inc(gdn_s, 1)
                    yield
                for n in range(4):
                    gdn.begin(act, PRE, f"g_l2r{n}")
                    x = part(2176 + 544 * n, TA)
                    act.activation(two(x), ps[:, 4:6, 0:HN], ACT.Ln, bias=colp[:, 3:4])
                    act.drain()
                    act.activation(x, x, ACT.Exp, scale=-0.5).then_inc(gdn_s, 1)
                    yield
                for t in range(NT + 1):
                    w = P if t < NT else NS
                    gdn.begin(act, t, "g_decay")
                    act.activation(gD[0:w, 0:4 * w], gD[0:w, 0:4 * w], ACT.Exp).then_inc(gdn_s, 1)
                    yield
                    gdn.begin(act, t, "g_t1")
                    act.activation(gT[0:w, 0:4 * w], ps[0:w, 4, 0:4 * w], ACT.Copy).then_inc(gdn_s, 1)
                    yield
                    for n in levels_of(t)[1:]:
                        gdn.begin(act, t, f"g_xc{n}")
                        act.activation(gX[0:w, 0:4 * w], ps[0:w, 4, 0:4 * w], ACT.Copy).then_inc(gdn_s, 1)
                        yield
                    gdn.begin(act, t, "g_skc")
                    act.activation(g_sk[:, 0:2 * w], ps[:, 4, 0:2 * w], ACT.Copy).then_inc(gdn_s, 1)
                    yield

            def hgrn_act():
                hgrn.begin(act, PRE, "h_lb1")
                act.activation(hrow[0:1, 0:256], hrow[0:1, 0:256], ACT.Exp).then_inc(hgrn_s, 1)
                yield
                hgrn.begin(act, PRE, "h_lb5")
                act.activation(hcol[:, :, 3:5], hcol[:, :, 3:5], ACT.Ln).then_inc(hgrn_s, 1)
                yield
                hgrn.begin(act, PRE, "h_silu")
                act.wait_ge(x_read, units_through(HI + 1))
                rest.after(act, PRE, "s_w_b")
                for m in range(2):
                    act.activation(kg[:, m, :], pj[:, HF + m, :], ACT.Sigmoid, scale=-1.0)
                for m in range(2):
                    act.activation(pj[:, HQ + m, :], pj[:, HQ + m, :], ACT.Silu)
                act.drain().then_inc(hgrn_s, 1)
                yield
                a_, b_ = part(C0, TA), part(C0 + 544, TA)
                for f in range(2):
                    for name, x, src in ((f"h_ls{f}", a_, pj[:, HF + f, :]), (f"h_ln{f}", b_, b_)):
                        hgrn.begin(act, PRE, name)
                        act.activation(x, src, ACT.Abs)
                        act.drain()
                        act.activation(x, x, ACT.Exp, scale=-1.0)
                        act.drain()
                        act.activation(x, x, ACT.Ln, bias=1.0).then_inc(hgrn_s, 1)
                        yield
                for t in range(NT + 1):
                    w = P if t < NT else NS
                    for n in levels_of(t):
                        hgrn.begin(act, t, f"h_dec{n}")
                        act.activation(hEf[:, 0:2 * w], hEf[:, 0:2 * w], ACT.Abs)
                        act.drain()
                        act.activation(hEf[:, 0:2 * w], hEf[:, 0:2 * w], ACT.Exp, scale=-1.0).then_inc(hgrn_s, 1)
                        yield
                    hgrn.begin(act, t, "h_dec")
                    act.activation(hQ[:, 0:2 * w].rearrange("k (p l) -> k p l", p=2), pj[:, HF:HF + 2, t * P:t * P + w], ACT.Exp)
                    act.activation(hEf[:, 0:2 * w], hEf[:, 0:2 * w], ACT.Exp)
                    act.drain().then_inc(hgrn_s, 1)
                    yield

            def rest_act():
                rest.begin(act, PRE, "s_rb")
                act.wait_ge(d_row, 96)
                z, e, ln = (rowbuf(scr, n) for n in range(3))
                act.activation(two(Vr[0:32, :]), ps[0:32, 2:4, 0:HN], ACT.Sigmoid)
                act.activation(e, z, ACT.Abs)
                act.activation(colp[0:NR, 1:2], colp[0:NR, 1:2], ACT.Exp)
                act.drain()
                act.activation(e, e, ACT.Exp, scale=-1.0)
                act.drain()
                act.activation(ln, e, ACT.Ln, bias=1.0)
                act.drain().then_inc(rest_s, 1)
                yield
                rest.begin(act, PRE, "s_rexp")
                act.activation(Er[0:NR, :], Er[0:NR, :], ACT.Exp)
                act.activation(RK(scr), RK(scr), ACT.Exp)
                act.activation(Vr[R_M:NR, :], MTr[R_M:NR, :], ACT.Exp, scale=-1.0)
                act.drain().then_inc(rest_s, 1)
                yield
                for n, f in enumerate(CONV_S):
                    rest.begin(act, PRE, f"s_silu{n}")
                    act.activation(pj[:, f, :], s_acc[:, 544 * (n % 2):544 * (n % 2 + 1)], ACT.Silu).then_inc(rest_s, 1)
                    yield
                for name, n in (("s_decay", 8), ("m_decay", 4)):
                    for t in range(NT + 1):
                        w = P if t < NT else NS
                        rest.begin(act, t, name)
                        act.activation(bD[0:w, 0:n * w], bD[0:w, 0:n * w], ACT.Exp).then_inc(rest_s, 1)
                        yield

            gens = {"g": gdn_act(), "h": hgrn_act(), "s": rest_act()}
            for chain, t, name, engine in order:
                if engine == "act" and chain == "x":
                    read_unit(t)
                elif engine == "act":
                    next(gens[chain])
                elif (chain, t, name) == ("g", NT, "g_statec"):
                    gdn.after(act, NT, "g_statec")
                    for k in range(KD):
                        act.activation(h_hi[:, k, :], hT[:, k, :], ACT.Copy).then_inc(gate_in_hi, 1)

            def high(m, at=None, n_at=None):
                n, src = piece(m)
                landed(act, n % R, n if n_at is None else n_at)
                if m >= 2:
                    act.wait_ge(w_done, (m if at is None else at) + (-1))
                hi, _ = parts(m)
                act.activation(hi, src, ACT.Copy).then_inc(w_split_hi, 1)

            rest.after(act, NT, "m_normc")
            high(0)
            hgrn.after(act, NT, "h_statec")
            high(1)
            mid.begin(act, 0, "silus")
            for m in (GZ, GZ + 1, HG, HG + 1, SZ, SZ + 1):
                act.activation(pj[:, m, :], pj[:, m, :], ACT.Silu)
            for m in (MO, MO + 1):
                act.activation(pj[:, m, :], pj[:, m, :], ACT.Sigmoid)
            act.drain().then_inc(mid_s, 1)

            def gate_out(k, func):
                act.wait_ge(w_done, k + 1)
                if k >= len(gates):
                    act.wait_ge(lin_read, k - len(gates) + 1)
                act.activation(two(gates[k % len(gates)]), ps[:, 2 * (k % 2):2 * (k % 2) + 2, 0:HN], func).then_inc(gate_read, 1)

            def merged_high(d):
                act.wait_ge(merged, d + 1)
                act.activation(m_hi[d], merged_t(pj, d), ACT.Copy).then_inc(act_hi, 1)

            for n in range(4):
                high(n + 2)
                gate_out(n, ACT.Copy)
                mid.begin(act, 0, f"o_rs{n}")
                for f in range(2):
                    act.activation(two(rms[n][f]), ps[:, 4 + 2 * f:6 + 2 * f, 0:HN], ACT.Ln,
                                   scale=1.0 / (P if n == 2 else DK), bias=colp[:, 3:4])
                act.drain().then_inc(mid_s, 1)
            high(6)
            gate_out(4, ACT.Copy)
            for n in range(4):
                for f in range(2):
                    act.activation(rms[n][f], rms[n][f], ACT.Exp, scale=-0.5)
                act.drain().then_inc(rms_ready, 1)
            high(7)
            gate_out(5, ACT.Copy)
            act.drain()
            for k in range(N_RAW):
                act.activation(gates[k], gates[k], ACT.Sigmoid).then_inc(gate_ready, 1)
            act.wait_ge(branch_ready, 1)
            for k in range(N_RAW, 4 * KD):
                high(k + 2)
                gate_out(k, ACT.Sigmoid)
                if k >= 11 and k % 4 == 3:
                    merged_high((k - 11) // 4)
            act.wait_ge(lin_done, 4 * KD - 3)
            merged_high(6)
            merged_high(7)
            for j in range(KD):
                high(M_WOUT + j + 2)
            rsqrt(mid, "rs2", two(rstd[:, :]), ps[:, 4:6, 0:HN], 1.0 / D)
            act.wait_ge(normed, KD + 1)
            act.activation(h_hi[:, :, T:TA], hT[:, :, T:TA], ACT.Copy).then_inc(high_done, 1)
            for k in range(KD):
                act.wait_ge(normed, KD + k + 2)
                act.activation(h_hi[:, k, 0:T], hT[:, k, 0:T], ACT.Identity, bias=mod[:, 24 + k, 0:1]).then_inc(high_done, 1)

            def ff_act(i, r, last=False):
                e = r % 2
                m = M_FFA + 2 * ((r + 1) % R) if not last else M_FFB
                for q in range(2):
                    at = i * 2 + (M_FFA + 2 + q)
                    high(m + q, at=at, n_at=i + (first["ffa"] + 1) if not last else None)
                    if q == 0:
                        act.wait_ge(w_done, i * 2 + (M_FFA + 1))
                        act.wait_ge(lin_read, i + (4 * KD - 1))
                        act.activation(two(pair_buf[e][:, :]), ps[:, 2 * e:2 * e + 2, 0:HN], ACT.Silu).then_inc(tile_read, 1)
            with act.Fori(0, KF // R) as i:
                for r in range(R):
                    ff_act(i * R + r, r)
            ff_act(KF - 2, 0)
            for k in range(8):
                act.activation(f_hi[k], pj[:, 8 + k, :], ACT.Copy).then_inc(act_hi, 1)
            ff_act(KF - 1, 1, last=True)
            mid.after(act, 0, "ffac")
            for k in range(8, KF):
                act.activation(f_hi[k], pj[:, 8 + k, :], ACT.Copy).then_inc(act_hi, 1)
            with act.Fori(0, 3) as i:
                for r in range(R):
                    high(M_FFB + (2 + r) % R, at=i * R + (M_FFB + 2 + r), n_at=i * R + (first["ffb"] + 2 + r))
            for q in range(2):
                high(M_FFB + 14 + q)
            rsqrt(mid, "rs3", two(rstd[:, :]), ps[:, 4:6, 0:HN], 1.0 / D)
            mid.after(act, 0, "colc3")
            for t in range(NT + 1):
                w = P if t < NT else NS
                act.wait_ge(y_done, t + 1)
                act.activation(ytok(pj, t)[:, 0:512], ps[0:w, Y_BANK[t], :], ACT.Identity, scale=coef[0:w, 0, t:t + 1]).then_inc(y_act, 1)

        @block.vector
        def _(dve):
            MUL, ADD, SUB = ALU.mult, ALU.add, ALU.subtract

            def tt(out, a, b, op):
                r = dve.tensor_tensor(out, a, b, op)
                dve.drain()
                return r

            def ts(out, a, s1, s2, op0, op1=None):
                r = dve.tensor_scalar(out, a, s1, s2, op0, *([op1] if op1 is not None else []))
                dve.drain()
                return r

            def stt(out, a, s, b, op0, op1):
                r = dve.scalar_tensor_tensor(out=out, in0=a, scalar=s, in1=b, op0=op0, op1=op1)
                dve.drain()
                return r

            def cp(out, a):
                r = dve.tensor_copy(out, a)
                dve.drain()
                return r

            def done(chain):
                dve.drain().then_inc(chain.sem, 1)

            dve.wait_ge(zeroed, 1)
            dve.memset(colp[:, 3:4], EPS)
            for b in (MTr, Vr):
                dve.memset(b[:, :], 0.0)
            dve.memset(hrow[64:96, :], 0.0)
            dve.drain().then_inc(zeroed, 1)
            pre.begin(dve, 0, "ctc")
            cp(cT[:, :, :].rearrange("p k b -> p (k b)"), ps[:, 5, 0:KD * (NB + 1)])
            done(pre)

            for d in range(KD):
                pre.begin(dve, 0, f"sq{d}")
                dve.tensor_tensor(hT[:, d, :], xT0[:, d, :], xT0[:, d, :], MUL).then_inc(pre_s, 1)

            def ada_bias(c0, c1):
                return vt[:, V_ADAB + c0:V_ADAB + c1].unsqueeze(2).to_broadcast([P, c1 - c0, 9])

            pre.begin(dve, 0, "mod1")
            cp(vt[:, :], ps[:, 1, 0:V_2])
            tt(mod[:, 0:16, :], ps[:, 0, 0:144].rearrange("p (c b) -> p c b", b=9), ada_bias(0, 16), ADD)
            done(pre)


            def coefficients(w0, c0):
                ts(coef[:, :, :], mod[:, c0 + KD:c0 + 2 * KD, :], 1.0, None, ADD)
                tt(coef[:, :, :], coef[:, :, :], vt[:, w0:w0 + KD].unsqueeze(2).to_broadcast([P, KD, 9]), MUL)

            def normalise_samples(x, c0):
                hs = hT[:, :, T:TA]
                h4 = hs.rearrange("p k (b t) -> p k b t", t=ND)
                tt(hs, x[:, :, T:TA], rstd[:, T:TA].unsqueeze(1).to_broadcast([P, KD, NS]), MUL)
                for b in range(NB):
                    c = slice(ND * b, ND * b + ND)
                    dve.tensor_tensor(hs[:, :, c], hs[:, :, c], coef[:, :, 1 + b:2 + b].to_broadcast([P, KD, ND]), MUL)
                dve.drain()
                for b in range(NB):
                    c = slice(ND * b, ND * b + ND)
                    dve.tensor_tensor(hs[:, :, c], hs[:, :, c], mod[:, c0:c0 + KD, 1 + b:2 + b].to_broadcast([P, KD, ND]), ADD)

            def normalise(x, k):
                dve.scalar_tensor_tensor(out=hT[:, k, 0:T], in0=x[:, k, 0:T], scalar=coef[:, k, 0:1], in1=rstd[:, 0:T],
                                         op0=MUL, op1=MUL).then_inc(normed, 1)

            coefficients(V_N1, 0)
            normalise_samples(xT0, 0)
            for k in range(KD):
                normalise(xT0, k)
            def tail_copies(feats, bank, tl, spad):
                n = len(feats)
                for b in range(0, n, 4):
                    wd = P * min(4, n - b)
                    dve.tensor_copy(tl[0:2 * NS, b * P:b * P + wd], ps[0:2 * NS, bank + b // 4, 0:wd])
                sp7 = spad.rearrange("p (f b k) -> p f b k", f=n, k=7)
                dve.tensor_copy(sp7[:, :, :, 0:3], ps[:, bank + 1, 256:256 + 24 * n].rearrange("p (f b k) -> p f b k", f=n, k=3))
                for m, f in enumerate(feats):
                    dve.tensor_copy(sp7[:, m, :, 3:7], pj[:, f, T:TA].rearrange("p (b t) -> p b t", t=ND))

            def conv(f, acc, hist7, w_, b_):
                sa = acc[:, T:TA].rearrange("p (b t) -> p b t", t=ND)
                dve.tensor_scalar(acc[:, 0:T], pj[:, f, 0:T], w_[3], b_, MUL, ADD)
                ts(sa, hist7[:, :, 3:7], w_[3], b_, MUL, ADD)
                for k in (2, 1, 0):
                    d = 3 - k
                    dve.scalar_tensor_tensor(out=acc[:, d:T], in0=pj[:, f, 0:T - d], scalar=w_[k], in1=acc[:, d:T], op0=MUL, op1=ADD)
                    stt(sa, hist7[:, :, k:k + 4], w_[k], sa, MUL, ADD)

            two = lambda b: b.rearrange("p (h n) -> p h n", h=2)

            def gdn_pre():
                gdn.begin(dve, PRE, "g_tailc")
                tail_copies(CONV_G, 4, g_tail, g_spad)
                done(gdn)
                yield
                for n, f in enumerate(CONV_G):
                    gdn.begin(dve, PRE, f"g_conv{n}")
                    conv(f, g_acc[:, 544 * (n % 2):544 * (n % 2 + 1)], g_spad.rearrange("p (f b k) -> p f b k", f=6, k=7)[:, n],
                         [vt[:, V_GCW + k * 6 + n:V_GCW + k * 6 + n + 1] for k in range(4)], vt[:, V_GCB + n:V_GCB + n + 1])
                    done(gdn)
                    yield
                gdn.begin(dve, PRE, "g_l2sq")
                dve.wait_ge(d_tail_g, 9 * 16)
                for n, f in enumerate((GQ, GQ + 1, GK, GK + 1)):
                    dve.tensor_tensor(part(544 * n, TA), pj[:, f, :], pj[:, f, :], MUL)
                done(gdn)
                yield
                gdn.begin(dve, PRE, "g_l2m")
                for n, f in enumerate((GQ, GQ + 1, GK, GK + 1)):
                    dve.scalar_tensor_tensor(out=pj[:, f, :], in0=pj[:, f, :], scalar=DK ** -0.5 if n < 2 else 1.0,
                                             in1=part(2176 + 544 * n, TA), op0=MUL, op1=MUL)
                done(gdn)
                yield

            def rest_pre():
                z, e, ln, t1, t2 = (rowbuf(scr, n) for n in range(5))
                rs, rk, rn = RS(scr), RK(scr), RN(scr)
                rest.begin(dve, PRE, "s_rz")
                dve.wait_ge(d_row, 96)
                ts(two(z), ps[0:NR, 2:4, 0:HN], colp[0:NR, 0:1], cst[0:NR, K_SGN:K_SGN + 1], ADD, MUL)
                done(rest)
                yield
                rest.begin(dve, PRE, "s_ri")
                dve.wait_ge(d_st, 16)
                ts(t1, e, 1.0, 1.0, ADD, SUB)
                tt(t1, e, t1, SUB)
                tt(ln, ln, t1, ADD)
                stt(z, z, 0.0, ln, ALU.max, ADD)
                cp(Vr[32:64, :], z[32:64, :])
                ts(colp[0:NR, 1:2], colp[0:NR, 1:2], -1.0, None, MUL)
                ts(t1, z, colp[0:NR, 1:2], None, MUL)
                dve.tensor_tensor_scan(Rr[0:NR, :], cst[0:NR, K_RST:K_RST + TA], t1, 0.0, MUL, ADD)
                m4 = slice(R_M, R_M + 4)
                iv = t2
                ts(two(iv[R_M:NR, :]), ps[R_M:NR, 2:4, 0:HN], colp[R_M:NR, 2:3], None, ADD)
                dve.tensor_tensor_scan(MTr[m4, 0:T], t1[m4, 0:T], iv[m4, 0:T], 0.0, ADD, ALU.max)
                isq = hrow[m4, 0:40].rearrange("p (b t) -> p b t", t=5)
                fsq = hrow[m4, 40:80].rearrange("p (b t) -> p b t", t=5)
                osq = hrow[m4, 80:120]
                cp(isq[:, :, 1:5], iv[m4, T:TA].rearrange("p (b t) -> p b t", t=ND))
                dve.memset(fsq, -BIG)
                dve.drain()
                cp(fsq[:, :, 1:5], t1[m4, T:TA].rearrange("p (b t) -> p b t", t=ND))
                dve.tensor_tensor_scan(osq, hrow[m4, 40:80], hrow[m4, 0:40], 0.0, ADD, ALU.max)
                mp = ln
                dve.memset(mp, 0.0)
                dve.drain()
                cp(MTr[m4, T:TA].rearrange("p (b t) -> p b t", t=ND), osq.rearrange("p (b t) -> p b t", t=5)[:, :, 1:5])
                for t in range(1, NT):
                    dve.tensor_copy(mp[m4, t * P:(t + 1) * P], MTr[m4, t * P - 1:t * P].to_broadcast([4, P]))
                dve.tensor_copy(mp[m4, T:TA].rearrange("p (b t) -> p b t", t=ND), isq[:, :, 0:1].to_broadcast([4, NB, ND]))
                cp(rs, Rr[0:NR, :])
                tt(rs[m4, :], Rr[m4, :], iv[m4, :], SUB)
                tt(Rr[m4, :], Rr[m4, :], MTr[m4, :], SUB)
                tt(Er[0:NR, :], Rr[0:NR, :], mp, ADD)
                for c0, n, l in ((0, NT, P), (T, NB, ND)):
                    v = lambda b: b[0:NR, c0:c0 + n * l].rearrange("p (n l) -> p n l", l=l)
                    dve.tensor_tensor(v(rk), v(Rr)[:, :, l - 1:l].to_broadcast([NR, n, l]), v(rs), SUB)
                done(rest)
                yield
                rest.begin(dve, PRE, "s_rv")
                ts(Vr[R_M:NR, :], Vr[R_M:NR, :], 1e38, None, ALU.min)
                stt(rn, Vr[0:NR, :], -1.0, Er[0:NR, :], MUL, MUL)
                done(rest)
                yield
                for n in range(3):
                    rest.begin(dve, PRE, f"s_rcolc{n}")
                    for t in range(2 * n, min(2 * n + 2, NT + 1)):
                        w = P if t < NT else NS
                        for r0, c0, m in ((R_G, T_G, 4), (R_S, T_S, 8), (R_M, T_M, 4)):
                            dve.tensor_copy(cols[0:w, t, :, c0:c0 + m], ps[0:w, 2 + t % 2, 0:4 * NR].rearrange("p (k r) -> p k r", k=4)[:, :, r0:r0 + m])
                    done(rest)
                    yield
                rest.begin(dve, PRE, "s_tailc")
                tail_copies(CONV_S, 2, s_tail, s_spad)
                done(rest)
                yield
                for n, f in enumerate(CONV_S):
                    rest.begin(dve, PRE, f"s_conv{n}")
                    conv(f, s_acc[:, 544 * (n % 2):544 * (n % 2 + 1)], s_spad.rearrange("p (f b k) -> p f b k", f=4, k=7)[:, n],
                         [vt[:, V_SCW + k * 4 + n:V_SCW + k * 4 + n + 1] for k in range(4)], vt[:, V_SCB + n:V_SCB + n + 1])
                    done(rest)
                    yield

            def hgrn_pre():
                hgrn.begin(dve, PRE, "h_lb0")
                tt(hrow[0:1, 0:256], hrow[0:1, 0:256], hrow[0:1, 0:256], SUB)
                done(hgrn)
                yield
                hgrn.begin(dve, PRE, "h_lb2")
                rest.after(dve, PRE, "s_w_b")
                dve.tensor_copy(hrow2[0:1, 0:256].rearrange("o (h v) -> o h v", v=32), hrow[0:1, 256:264].unsqueeze(2).to_broadcast([1, 8, 32]))
                dve.reciprocal(hrow2[0:1, 256:512], hrow[0:1, 0:256])
                dve.drain()
                tt(hrow[0:1, 0:256], hrow[0:1, 0:256], hrow2[0:1, 256:512], MUL)
                tt(hrow[0:1, 0:256], hrow[0:1, 0:256], hrow[0:1, 0:256], SUB)
                done(hgrn)
                yield
                hgrn.begin(dve, PRE, "h_lb4")
                lbc = hcol[:, :, 0]
                cp(lbc, ps[:, 6, 0:2])
                cp(dcol[:, :], ps[:, 6, 2:4])
                ts(hcol[:, :, 1], lbc, -1.0, 1.0, MUL, ADD)
                ts(hcol[:, :, 2], lbc, 0.0, None, ALU.is_gt)
                ts(hcol[:, :, 3], lbc, 2.0 ** -60, None, ALU.max)
                ts(hcol[:, :, 4], hcol[:, :, 1], 2.0 ** -60, None, ALU.max)
                done(hgrn)
                yield
                hgrn.begin(dve, PRE, "h_lb6")
                tt(hcol[:, :, 3], hcol[:, :, 3], hcol[:, :, 2], MUL)
                ts(hcol[:, :, 5], hcol[:, :, 2], BIG, -BIG, MUL, ADD)
                tt(hcol[:, :, 3], hcol[:, :, 3], hcol[:, :, 5], ADD)
                for f in range(2):
                    dve.tensor_scalar(kg[:, f, :], kg[:, f, :], hcol[:, f, 1:2], None, MUL)
                done(hgrn)
                yield
                a_, b_ = part(C0, TA), part(C0 + 544, TA)
                for f in range(2):
                    fz = pj[:, HF + f, :]
                    hgrn.begin(dve, PRE, f"h_b{f}")
                    stt(a_, fz, 0.0, a_, ALU.min, SUB)
                    ts(a_, a_, hcol[:, f, 4:5], None, ADD)
                    ts(b_, a_, hcol[:, f, 3:4], None, SUB)
                    done(hgrn)
                    yield
                    hgrn.begin(dve, PRE, f"h_g{f}")
                    ts(a_, a_, hcol[:, f, 3:4], None, ALU.max)
                    tt(a_, a_, b_, ADD)
                    dve.tensor_tensor_scan(pj[:, HF + f, :], cst[:, K_RST:K_RST + TA], a_, 0.0, MUL, ADD)
                    done(hgrn)
                    yield

            def col(t, kind, row, n, w, width):
                return cols[0:w, t, kind, row:row + n].unsqueeze(2).to_broadcast([w, n, width])

            def half(q):
                return slice(q * DK, (q + 1) * DK)

            def decays(t, w, D_, bank, row, chain):
                for q in range(2):
                    dve.tensor_tensor(D_[:, 2 * q:2 * q + 2, :], ps[0:w, bank, 2 * q * w:(2 * q + 2) * w].rearrange("m (p l) -> m p l", p=2),
                                      cols[0:w, t, 0, row + q:row + q + 3:2].unsqueeze(2).to_broadcast([w, 2, w]), SUB)
                dve.drain()
                dve.tensor_tensor(D_, D_, neg(t).unsqueeze(1).to_broadcast([w, 4, w]), ADD).then_inc(chain.sem, 1)

            def keep_last(dst, src, t, w, n):
                if t < NT:
                    dve.tensor_copy(dst[:, 0:n, 0:1], src[:, :, w - 1:w])
                else:
                    dve.tensor_copy(dst[:, 0:n, :], src[:, :, ND - 1:w:ND])

            def spread(dst, src, n, v):
                own = cst[0:NS, K_OWN:K_OWN + NB].unsqueeze(2).to_broadcast([NS, NB, v])
                for h in range(n):
                    dve.tensor_tensor(dst[0:NS, h * NB * v:(h + 1) * NB * v].rearrange("m (b v) -> m b v", b=NB),
                                      src(h).unsqueeze(1).to_broadcast([NS, NB, v]), own, MUL)

            def grow(S, e, inc, shape, chain):
                tt(S, S, e, MUL)
                dve.tensor_tensor(S, S, inc, ADD)

            def gdn_dve():
                yield from gdn_pre()
                for t in range(NT + 1):
                    w = P if t < NT else NS
                    c = slice(t * P, t * P + w)
                    v = lambda b: b[0:w, 0:4 * w].rearrange("m (h l) -> m h l", h=4)
                    U_, L_, D_, A_ = v(gU), v(gL), v(gD), v(gAt)
                    f = lambda b: b[:, 0:2 * w].rearrange("k (p l) -> k p l", p=2)
                    tok = lambda b: b[0:w, 0:256].rearrange("m (h v) -> m h v", h=4)
                    m4_ = lambda n: mask(n, w).unsqueeze(1).to_broadcast([w, 4, w])
                    gdn.begin(dve, t, "g_scale")
                    ktok, vtok = (ps[0:w, 4, o:o + 256].rearrange("m (h v) -> m h v", h=4) for o in (0, 256))
                    dve.tensor_tensor(tok(g_vb), vtok, col(t, 2, T_G, 4, w, DK), MUL)
                    dve.tensor_tensor(tok(g_kn), ktok, col(t, 3, T_G, 4, w, DK), MUL)
                    dve.tensor_tensor(tok(g_kd), ktok, col(t, 1, T_G, 4, w, DK), MUL)
                    Eb = ps[:, 5, 0:2 * w].rearrange("k (p l) -> k p l", p=2)
                    Bb = ps[:, 5, 256:256 + 2 * w].rearrange("k (p l) -> k p l", p=2)
                    dve.tensor_tensor(f(g_qs), pj[:, GQ:GQ + 2, c], Eb, MUL)
                    keep_last(eG, Eb, t, w, 2)
                    dve.tensor_tensor(f(g_kb), pj[:, GK:GK + 2, c], Bb, MUL)
                    done(gdn)
                    yield
                    gdn.begin(dve, t, "g_diff")
                    decays(t, w, D_, 4, T_G, gdn)
                    yield
                    gdn.begin(dve, t, "g_lower")
                    tt(gAt[0:w, 0:4 * w].rearrange("m (q x) -> m q x", q=2), ps[0:w, 4:6, 0:2 * w],
                       gD[0:w, 0:4 * w].rearrange("m (q x) -> m q x", q=2), MUL)
                    dve.tensor_tensor(U_, A_, m4_(0), MUL)
                    tt(L_, A_, m4_(1), MUL)
                    tt(U_, ident[0:w, 0:w].unsqueeze(1).to_broadcast([w, 4, w]), U_, SUB)
                    done(gdn)
                    yield
                    lv = levels_of(t)
                    for n in lv[1:]:
                        gdn.begin(dve, t, f"g_upd{n}")
                        dve.tensor_tensor(gU[0:w, 0:4 * w], gU[0:w, 0:4 * w], ps[0:w, 5, 0:4 * w], SUB)
                        if n != lv[-1]:
                            dve.tensor_tensor(gT[0:w, 0:4 * w], gT[0:w, 0:4 * w], ps[0:w, 4, 0:4 * w], SUB)
                            dve.tensor_tensor(L_, A_, m4_(n + 1), MUL)
                        done(gdn)
                        yield
                    gdn.begin(dve, t, "g_aq")
                    D2 = gD[0:w, 0:4 * w].rearrange("m (q x) -> m q x", q=2)
                    dve.tensor_tensor(D2, ps[0:w, 4:6, 0:2 * w], D2, MUL).then_inc(gdn_s, 1)
                    yield
                    gdn.begin(dve, t, "g_uc")
                    if t < NT:
                        ut = g_u[0:w, 0:256].rearrange("m (p q v) -> m q p v", p=2, q=2)
                        for q in range(2):
                            dve.tensor_copy(ut[:, q], ps[0:w, 4 + q, 0:2 * DK].rearrange("m (p v) -> m p v", p=2))
                        done(gdn)
                        yield
                    else:
                        for q in range(2):
                            dve.tensor_copy(g_sk[half(q), 0:2 * w], ps[half(q), 4 + q, 0:2 * w])
                        done(gdn)
                        yield
                        gdn.begin(dve, t, "g_utc")
                        cp(g_u[0:w, 0:256], ps[0:w, 4, 0:256])
                        spread(g_Ue, lambda h: g_u[0:w, h * DK:(h + 1) * DK], 4, DK)
                        done(gdn)
                        yield
                    gdn.begin(dve, t, "g_outc")
                    for q in range(2):
                        dve.tensor_copy(pj[half(q), GV:GV + 2, c], ps[half(q), 4 + q, 0:2 * w].rearrange("k (p l) -> k p l", p=2))
                    if t < NT:
                        grow(S_g[:, :, :], eG[:, :, 0:1].to_broadcast([P, 2, DK]),
                             ps[:, 4, 256:256 + 2 * DK].rearrange("k (p v) -> k p v", p=2), None, gdn)
                        done(gdn)
                        yield
                    else:
                        done(gdn)
                        yield
                        gdn.begin(dve, t, "g_statec")
                        grow(Q_g[:, :, :, :], eG[:, :, :].unsqueeze(3).to_broadcast([P, 2, NB, DK]),
                             ps[:, 4:6, :].rearrange("k p (b v) -> k p b v", b=NB), None, gdn)
                        done(gdn)
                        yield

            def hgrn_dve():
                yield from hgrn_pre()
                for t in range(NT + 1):
                    w = P if t < NT else NS
                    c = slice(t * P, t * P + w)
                    v = lambda b: b[0:w, 0:4 * w].rearrange("m (h l) -> m h l", h=4)
                    f = lambda b: b[:, 0:2 * w].rearrange("k (p l) -> k p l", p=2)
                    D_ = v(hD)
                    g = pj[:, HF:HF + 2, c]

                    def level_diff(n):
                        s = LEVELS[n]
                        for p in range(2):
                            x = g[:, p, :].rearrange("k (b i) -> k b i", i=2 * s)
                            dve.tensor_tensor(f(hEf)[:, p, :].rearrange("k (b i) -> k b i", i=2 * s), x,
                                              x[:, :, s - 1:s].to_broadcast([P, w // (2 * s), 2 * s]), SUB)

                    hgrn.begin(dve, t, "h_diag")
                    for q in range(2):
                        dve.tensor_tensor(D_[:, 2 * q:2 * q + 2, :], ps[0:w, 6 + q, 0:2 * w].rearrange("m (p l) -> m p l", p=2),
                                          ident[0:w, 0:w].unsqueeze(1).to_broadcast([w, 2, w]), MUL)
                    level_diff(0)
                    done(hgrn)
                    yield
                    for n in levels_of(t):
                        hgrn.begin(dve, t, f"h_sc{n}")
                        dve.tensor_tensor(f(hQl), pj[:, HQ:HQ + 2, c], f(hEf), MUL)
                        dve.tensor_tensor(f(hKl), kg[:, :, c], f(hEf), MUL)
                        done(hgrn)
                        yield
                        hgrn.begin(dve, t, f"h_add{n}")
                        X_ = v(hX)
                        for q in range(2):
                            dve.tensor_tensor(X_[:, 2 * q:2 * q + 2, :], ps[0:w, 6 + q, 0:2 * w].rearrange("m (p l) -> m p l", p=2),
                                              mask(n, w).unsqueeze(1).to_broadcast([w, 2, w]), MUL)
                        if n != levels_of(t)[-1]:
                            level_diff(n + 1)
                        else:
                            for p in range(2):
                                if t < NT:
                                    dve.tensor_tensor(f(hEf)[:, p, :], g[:, p, w - 1:w].to_broadcast([P, w]), g[:, p, :], SUB)
                                else:
                                    x = g[:, p, :].rearrange("k (b i) -> k b i", i=ND)
                                    dve.tensor_tensor(f(hEf)[:, p, :].rearrange("k (b i) -> k b i", i=ND),
                                                      x[:, :, ND - 1:ND].to_broadcast([P, NB, ND]), x, SUB)
                        dve.drain()
                        dve.tensor_tensor(D_, D_, X_, ADD)
                        done(hgrn)
                        yield
                    hgrn.begin(dve, t, "h_kd")
                    dve.tensor_tensor(f(hEf), kg[:, :, c], f(hEf), MUL)
                    keep_last(eH, f(hQ), t, w, 2)
                    dve.drain()
                    dve.tensor_tensor(f(hQ), f(hQ), pj[:, HQ:HQ + 2, c], MUL)
                    done(hgrn)
                    yield
                    hgrn.begin(dve, t, "h_tokc")
                    dve.tensor_copy(hKd[0:w, 0:256], ps[0:w, 6, 0:256])
                    dve.tensor_copy(hV[0:w, 0:256], ps[0:w, 6, 256:512])
                    done(hgrn)
                    yield
                    hgrn.begin(dve, t, "h_outc")
                    for q in range(2):
                        dve.tensor_copy(pj[half(q), HI:HI + 2, c], ps[half(q), 6 + q, 0:2 * w].rearrange("k (p l) -> k p l", p=2))
                    if t < NT:
                        grow(S_h[:, :, :], eH[:, :, 0:1].to_broadcast([P, 2, DK]),
                             ps[:, 6, 256:256 + 2 * DK].rearrange("k (p v) -> k p v", p=2), None, hgrn)
                        done(hgrn)
                        yield
                    else:
                        spread(h_Ue, lambda h: hV[0:w, h * DK:(h + 1) * DK], 4, DK)
                        done(hgrn)
                        yield
                        hgrn.begin(dve, t, "h_statec")
                        grow(Q_h[:, :, :, :], eH[:, :, :].unsqueeze(3).to_broadcast([P, 2, NB, DK]),
                             ps[:, 6:8, :].rearrange("k p (b v) -> k p b v", b=NB), None, hgrn)
                        done(hgrn)
                        yield
            def rest_dve():
                yield from rest_pre()
                for t in range(NT + 1):
                    w = P if t < NT else NS
                    c = slice(t * P, t * P + w)
                    rest.begin(dve, t, "s_diff")
                    if t == 0:
                        dve.wait_ge(d_tail_s, 9 * 16)
                    D8 = bD[0:w, 0:8 * w].rearrange("m (h l) -> m h l", h=8)
                    for g_ in range(2):
                        dve.tensor_tensor(D8[:, 4 * g_:4 * g_ + 4, :], ps[0:w, 2 + g_, 0:4 * w].rearrange("m (j l) -> m j l", j=4),
                                          col(t, 0, T_S + 4 * g_, 4, w, w), SUB)
                    dve.drain()
                    dve.tensor_tensor(D8, D8, neg(t).unsqueeze(1).to_broadcast([w, 8, w]), ADD)
                    done(rest)
                    yield
                    rest.begin(dve, t, "s_att")
                    for g_ in range(2):
                        dve.tensor_tensor(D8[:, 4 * g_:4 * g_ + 4, :], D8[:, 4 * g_:4 * g_ + 4, :],
                                          ps[0:w, 2 + g_, 0:w].unsqueeze(1).to_broadcast([w, 4, w]), MUL)
                        dve.tensor_tensor(bKd[0:w, g_ * 256:(g_ + 1) * 256].rearrange("m (j n) -> m j n", j=4),
                                          ps[0:w, 2, 128 + g_ * DK:128 + (g_ + 1) * DK].unsqueeze(1).to_broadcast([w, 4, DK]),
                                          col(t, 1, T_S + 4 * g_, 4, w, DK), MUL)
                    for b in [bV]:
                        dve.tensor_tensor(b[0:w, 0:256].rearrange("m (h v) -> m h v", h=8),
                                          ps[0:w, 2, 256:512].rearrange("m (h v) -> m h v", h=8), col(t, 2, T_S, 8, w, 32), MUL)
                    done(rest)
                    yield
                    rest.begin(dve, t, "s_q")
                    E4 = ps[:, 2, 0:4 * w].rearrange("k (j l) -> k j l", j=4)
                    dve.tensor_tensor(bQ[:, 0:4 * w].rearrange("k (j l) -> k j l", j=4), E4,
                                      pj[:, SC, c].unsqueeze(1).to_broadcast([P, 4, w]), MUL)
                    keep_last(eR, E4, t, w, 4)
                    done(rest)
                    yield
                    rest.begin(dve, t, "s_outc")
                    for g_ in range(2):
                        dve.scalar_tensor_tensor(out=pj[:, SX + g_, c], in0=pj[:, SX + g_, c], scalar=dcol[:, g_:g_ + 1],
                                                 in1=ps[:, 2 + g_, 0:w], op0=MUL, op1=ADD)
                    if t < NT:
                        grow(S_s[:, :, :], eR[:, :, 0:1].to_broadcast([P, 4, 32]),
                             ps[:, 2, 256:384].rearrange("k (j v) -> k j v", j=4), None, rest)
                        done(rest)
                        yield
                    else:
                        spread(b_Ue, lambda h: bV[0:w, h * 32:(h + 1) * 32], 8, 32)
                        done(rest)
                        yield
                        rest.begin(dve, t, "s_statec")
                        for j in range(4):
                            grow(Qs(Q_s)[:, j], eR[:, j, :].unsqueeze(2).to_broadcast([P, NB, 32]),
                                 ps[:, 2 + j // 2, (j % 2) * 256:(j % 2 + 1) * 256].rearrange("k (b v) -> k b v", b=NB), None, rest)
                        done(rest)
                        yield
                for t in range(NT + 1):
                    w = P if t < NT else NS
                    c = slice(t * P, t * P + w)
                    v = lambda b: b[0:w, 0:4 * w].rearrange("m (h l) -> m h l", h=4)
                    f = lambda b: b[:, 0:2 * w].rearrange("k (p l) -> k p l", p=2)
                    tok = lambda b: b[0:w, 0:256].rearrange("m (h v) -> m h v", h=4)
                    D_ = v(bD)
                    rest.begin(dve, t, "m_scale")
                    ktok = ps[0:w, 2, 0:256].rearrange("m (h v) -> m h v", h=4)
                    dve.tensor_tensor(tok(bKd), ktok, col(t, 1, T_M, 4, w, DK), MUL)
                    for b in [bV]:
                        dve.tensor_copy(b[0:w, 0:256], ps[0:w, 2, 256:512])
                    Eb = ps[:, 3, 0:2 * w].rearrange("k (p l) -> k p l", p=2)
                    dve.scalar_tensor_tensor(out=f(bQ), in0=pj[:, MQ:MQ + 2, c], scalar=DK ** -0.5, in1=Eb, op0=MUL, op1=MUL)
                    keep_last(eR, Eb, t, w, 2)
                    if t == NT:
                        dve.wait_ge(d_q["mlstm"], 128)
                        for p in range(2):
                            dve.tensor_copy(Q_n[:, p, :, 1:DK], Q_n[:, p, :, 0:1].to_broadcast([P, NB, DK - 1]))
                    done(rest)
                    yield
                    rest.begin(dve, t, "m_diff")
                    decays(t, w, D_, 2, T_M, rest)
                    yield
                    rest.begin(dve, t, "m_att")
                    for q in range(2):
                        dve.scalar_tensor_tensor(out=bD[0:w, 2 * q * w:(2 * q + 2) * w], in0=ps[0:w, 2 + q, 0:2 * w], scalar=DK ** -0.5,
                                                 in1=bD[0:w, 2 * q * w:(2 * q + 2) * w], op0=MUL, op1=MUL)
                    done(rest)
                    yield
                    rest.begin(dve, t, "m_outc")
                    den = bDen
                    for q in range(2):
                        dve.tensor_copy(pj[half(q), MV:MV + 2, c], ps[half(q), 2 + q, 0:2 * w].rearrange("k (p l) -> k p l", p=2))
                        dve.tensor_copy(den[half(q), 0:2 * w], ps[half(q), 2 + q, 256:256 + 2 * w])
                    done(rest)
                    yield
                    rest.begin(dve, t, "m_denc")
                    stt(den[:, 0:2 * w], den[:, 0:2 * w], -1.0, den[:, 0:2 * w], MUL, ALU.max)
                    tt(den[:, 0:2 * w], den[:, 0:2 * w], ps[:, 2, 0:2 * w], ALU.max)
                    dve.reciprocal(den[:, 0:2 * w], den[:, 0:2 * w])
                    dve.drain()
                    tt(pj[:, MV:MV + 2, c], pj[:, MV:MV + 2, c], f(den), MUL)
                    if t < NT:
                        for S, o in ((S_c, 0), (S_n, 128)):
                            grow(S[:, :, :], eR[:, 0:2, 0:1].to_broadcast([P, 2, DK]),
                                 ps[:, 3, o:o + 2 * DK].rearrange("k (p v) -> k p v", p=2), None, rest)
                        done(rest)
                        yield
                    else:
                        spread(b_Ue, lambda h: bV[0:w, h * DK:(h + 1) * DK], 4, DK)
                        done(rest)
                        yield
                        for name, Q in (("m_statec", Q_c), ("m_normc", Q_n)):
                            rest.begin(dve, t, name)
                            grow(Q[:, :, :, :], eR[:, 0:2, :].unsqueeze(3).to_broadcast([P, 2, NB, DK]),
                                 ps[:, 2:4, :].rearrange("k p (b v) -> k p b v", b=NB), None, rest)
                            if name == "m_statec":
                                spread(b_Ue, lambda h: ones[0:w, 0:DK], 4, DK)
                            done(rest)
                            yield

            gens = {"g": gdn_dve(), "h": hgrn_dve(), "s": rest_dve()}
            for chain, t, name, engine in order:
                if engine == "dve":
                    next(gens[chain])

            mid.begin(dve, 0, "mod2")
            gdn.after(dve, NT, "g_statec")
            hgrn.after(dve, NT, "h_statec")
            rest.after(dve, NT, "m_normc")
            dve.wait_ge(x_read, UNITS)
            tt(mod[:, 16:48, :], mod[:, 16:48, :], ada_bias(16, 48), ADD)
            done(mid)

            def low(m, at=None):
                _, src = piece(m)
                hi, lo = parts(m)
                dve.wait_ge(w_split_hi, (m if at is None else at) + 1)
                dve.tensor_tensor(lo, src, hi.bitcast(F32), SUB).then_inc(w_split, 1)

            low(0)
            for k in range(KD):
                dve.wait_ge(gate_in_hi, k + 1)
                dve.tensor_tensor(h_lo[:, k, :], hT[:, k, :], h_hi[:, k, :].bitcast(F32), SUB).then_inc(gate_in, 1)
            low(1)
            for n in range(4):
                gate_t = (GZ, HG, SZ, MO)[n]
                mid.begin(dve, 0, f"o_sq{n}")
                for f in range(2):
                    o = pj[:, BR[2 * n + f], :]
                    if n == 2:
                        tt(o, o, pj[:, gate_t + f, :], MUL)
                    dve.tensor_tensor(rms[n][f], o, o, MUL)
                done(mid)
                low(n + 2)
            for n in range(4):
                gate_t = (GZ, HG, SZ, MO)[n]
                dve.wait_ge(rms_ready, n + 1)
                for f in range(2):
                    o = pj[:, BR[2 * n + f], :]
                    wn = (V_GN, V_HN, V_SN + f, V_MN)[n]
                    stt(o, o, vt[:, wn:wn + 1], rms[n][f], MUL, MUL)
                    if n != 2:
                        tt(o, o, pj[:, gate_t + f, :], MUL)
                dve.drain().then_inc(branch_ready, 1)
                if n < 2:
                    low(n + 6)

            def merged_low(d):
                dve.wait_ge(act_hi, d + 1)
                dve.tensor_tensor(m_lo[d], merged_t(pj, d), m_hi[d].bitcast(F32), SUB).then_inc(act_split, 1)

            for k in range(4 * KD):
                if k + 8 < M_WOUT + 2:
                    low(k + 8)
                dve.wait_ge(lin_done, k + 1)
                dve.wait_ge(gate_ready if k < N_RAW else gate_read, k + 1)
                lift = ps[:, 4 + 2 * (k % 2):6 + 2 * (k % 2), 0:HN]
                gate_t = two(gates[k % len(gates)])
                out = merged_t(pj, k // 4)
                if k % 4 == 0:
                    dve.tensor_tensor(two(out), gate_t, lift, MUL).then_inc(lin_read, 1)
                    dve.drain()
                else:
                    dve.tensor_tensor(two(Rr[:, :]), gate_t, lift, MUL).then_inc(lin_read, 1)
                    dve.drain()
                    dve.tensor_tensor(out, out, Rr[:, :], ADD)
                    dve.drain()
                    if k % 4 == 3:
                        dve.drain().then_inc(merged, 1)
                if k % 4 == 0 and k >= 8:
                    merged_low(k // 4 - 2)
            mid.begin(dve, 0, "upc")
            done(mid)

            merged_low(6)
            merged_low(7)
            dve.wait_ge(d_xin, 16)

            def residual(pieces, d, c0):
                par = d % 2
                dve.wait_ge(w_done, pieces)
                gt = mod[:, c0 + d, :]
                n1 = T - HN
                dve.scalar_tensor_tensor(out=xT[:, d, 0:HN], in0=ps[:, 2 * par, 0:HN], scalar=gt[:, 0:1], in1=xT[:, d, 0:HN], op0=MUL, op1=ADD)
                dve.scalar_tensor_tensor(out=xT[:, d, HN:T], in0=ps[:, 2 * par + 1, 0:n1], scalar=gt[:, 0:1], in1=xT[:, d, HN:T], op0=MUL, op1=ADD)
                m = Rr[:, 0:NS].rearrange("p (b t) -> p b t", t=ND)
                tt(m, ps[:, 2 * par + 1, n1:HN].rearrange("p (b t) -> p b t", t=ND), gt[:, 1:9].unsqueeze(2).to_broadcast([P, NB, ND]), MUL)
                dve.tensor_tensor(xT[:, d, T:TA], xT[:, d, T:TA], Rr[:, 0:NS], ADD)
                dve.drain().then_inc(tile_read, 1)

            def square(d, n):
                if n + d >= 2:
                    dve.wait_ge(summed, n + d - 1)
                dve.tensor_tensor(pair_buf[d % 2][:, :], xT[:, d, :], xT[:, d, :], MUL).then_inc(squared, 1)

            for d in range(KD):
                low(M_WOUT + d + 2)
                residual(M_WOUT + d + 1, d, 16)
                square(d, 0)
            coefficients(V_N2, 24)
            mid.after(dve, 0, "rs2")
            normalise_samples(xT, 24)
            dve.drain().then_inc(normed, 1)
            normalise(xT, 0)
            dve.wait_ge(high_done, 1)
            dve.tensor_tensor(h_lo[:, :, T:TA], hT[:, :, T:TA], h_hi[:, :, T:TA].bitcast(F32), SUB).then_inc(act_split, 1)
            for k in range(KD):
                if k + 1 < KD:
                    normalise(xT, k + 1)
                dve.wait_ge(high_done, k + 2)
                dve.scalar_tensor_tensor(out=h_lo[:, k, 0:T], in0=hT[:, k, 0:T], scalar=mod[:, 24 + k, 0:1],
                                         in1=h_hi[:, k, 0:T].bitcast(F32), op0=ADD, op1=SUB).then_inc(act_split, 1)

            def ff_dve(i, r, last=False):
                e = r % 2
                m = M_FFA + 2 * ((r + 1) % R) if not last else M_FFB
                low(m, at=i * 2 + (M_FFA + 2))
                low(m + 1, at=i * 2 + (M_FFA + 3))
                dve.wait_ge(tile_read, i + (tiles_before["ffa"] + 1))
                dve.wait_ge(w_done, i * 2 + (M_FFA + 2))
                out = pj[:, 8 + i, :] if isinstance(i, int) else pj[:, bass.ds(i + 8, 1), :].rearrange("p o n -> p (o n)")
                dve.tensor_tensor(two(out), two(pair_buf[e][:, :]), ps[:, 4 + 2 * e:6 + 2 * e, 0:HN], MUL).then_inc(lin_read, 1)
            with dve.Fori(0, KF // R) as i:
                for r in range(R):
                    ff_dve(i * R + r, r)
            def ff_low(k):
                dve.wait_ge(act_hi, KD + k + 1)
                dve.tensor_tensor(f_lo[k], pj[:, 8 + k, :], f_hi[k].bitcast(F32), SUB).then_inc(act_split, 1)

            ff_dve(KF - 2, 0)
            for k in range(8):
                ff_low(k)
            ff_dve(KF - 1, 1, last=True)
            mid.begin(dve, 0, "ffac")
            done(mid)
            for k in range(8, KF):
                ff_low(k)
            for d in range(KD):
                if d < KD - 1:
                    low(M_FFB + 2 * d + 2)
                    low(M_FFB + 2 * d + 3)
                residual(M_FFB + 2 * d + 2, d, 40)
                square(d, KD)
                dve.drain()
                dve.tensor_scalar(xT[:, d, :], xT[:, d, :], vt[:, V_NF + d:V_NF + d + 1], None, MUL).then_inc(y_ready, 1)
            mid.begin(dve, 0, "colc3")
            for t in range(NT + 1):
                w = P if t < NT else NS
                dve.tensor_copy(coef[0:w, 0, t:t + 1], ps[0:w, 4, t:t + 1])
            done(mid)
            for t in range(NT + 1):
                w = P if t < NT else NS
                dve.wait_ge(y_done, t + 1)
                dve.tensor_scalar(ytok(pj, t)[:, 512:1024], ps[0:w, Y_BANK[t] + 1, :], coef[0:w, 0, t:t + 1], None, MUL).then_inc(y_dve, 1)


def xtok(pj):
    return pj[:, :, :].rearrange("p a b -> p (a b)")[:, 0:NT * D].rearrange("p (a d) -> p a d", d=D)


def xstok(pj):
    return pj[:, :, :].rearrange("p a b -> p (a b)")[0:NS, NT * D:NT * D + D]


def ctok(pj):
    return pj[:, :, :].rearrange("p a b -> p (a b)")[:, NT * D + D:NT * D + 2 * D]


def ytok(pj, t):
    return pj[:, :, :].rearrange("p a b -> p (a b)")[0:(P if t < NT else NS), t * D:(t + 1) * D]


def rowbuf(scr, n):
    return scr[0:NR, B0 + 544 * n:B0 + 544 * (n + 1)]


def RS(scr):
    return rowbuf(scr, 1)


def RK(scr):
    return rowbuf(scr, 0)


def RN(scr):
    return rowbuf(scr, 3)


def Qs(Q):
    return Q[:, :, :, :].rearrange("k p b v -> k (p b v)").rearrange("k (j b v) -> k j b v", j=4, b=NB)


def merged_t(pj, d):
    return pj[:, MERGED[d], :]


_INS = ['x_prompt', 'x_sample', 'c_prompt', 'c_sample', 'state_gdn', 'state_gdn_conv', 'state_hgrn', 'state_ssd',
        'state_ssd_conv', 'state_mlstm_c', 'state_mlstm_n', 'state_mlstm_m', 'ada_w', 'ada_b', 'norm1_w', 'norm2_w', 'w_in',
        'gdn_conv_w', 'gdn_conv_b', 'gdn_a_log', 'gdn_dt_bias', 'gdn_norm_w', 'hg_lb_logits', 'hg_norm_w', 'ssd_conv_w',
        'ssd_conv_b', 'ssd_a_log', 'ssd_dt_bias', 'ssd_d', 'ssd_norm_w', 'ml_b_i', 'ml_b_f', 'ml_norm_w', 'w_branch',
        'w_out', 'ffn_w_in', 'ffn_w_out', 'final_norm_w']


def _state_shapes(b):
    return [(1, b, 4, 64, 64), (1, b, 3, 768), (1, b, 4, 64, 64), (1, b, 8, 64, 32), (1, b, 3, 512), (1, b, 4, 64, 64),
            (1, b, 4, 64), (1, b, 4)]


_OUTS = [(1, T, D), (NB, ND, D)] + _state_shapes(1) + _state_shapes(NB)


def kernel(**inputs):
    import concourse.bacc as _bacc
    from concourse.bass_utils import run_bass_kernel_spmd as _run

    nc = _bacc.Bacc("TRN2", target_bir_lowering=False, num_devices=1)
    arrays, args = {}, {}
    for name in _INS + ["const"]:
        a = host_constants() if name == "const" else np.ascontiguousarray(inputs[name])
        arrays[f"in_{name}_dram"] = a
        args[name] = nc.dram_tensor(f"in_{name}_dram", a.shape, mybir.dt.from_np(a.dtype), kind="ExternalInput").ap()
    outs = [nc.dram_tensor(f"out_{i}_dram", shape, F32, kind="ExternalOutput").ap() for i, shape in enumerate(_OUTS)]
    trunk(nc, args, outs)
    r = _run(nc, [arrays], core_ids=[0])
    return tuple(r.results[0][f"out_{i}_dram"] for i in range(len(_OUTS)))
```
